# Optimizing a Trainium2 kernel written in Bass

```python
import jax, jax.numpy as jnp
from jax import lax
import numpy as np

D_MODEL = 1024
BATCH = 1
SEQ = 512
DEPTH = 1

CHUNK = 64
LEFT_CHUNKS = 8
BAND = (LEFT_CHUNKS + 1) * CHUNK
N_HEADS = 8
HEAD_DIM = 64
D_ATTN = N_HEADS * HEAD_DIM
D_CONV = 512
CONV_K = 31
MAX_REL = 128
D_FF = 2816
FFN_CONV_K = 3
EPS = 1e-6
NEG_INF = -1e30
IN_WIDTHS = (D_ATTN, D_ATTN, D_ATTN, D_CONV, D_CONV, D_MODEL, D_MODEL)
D_IN = D_ATTN * 3 + D_CONV * 2 + D_MODEL * 2


def rms_norm(x, g):
    xf = x.astype(jnp.float32)
    y = xf * lax.rsqrt(jnp.mean(xf * xf, axis=-1, keepdims=True) + EPS)
    return (y * g.astype(jnp.float32)).astype(x.dtype)

def layer_norm(x, g, b):
    xf = x.astype(jnp.float32)
    mu = jnp.mean(xf, axis=-1, keepdims=True)
    var = jnp.mean(jnp.square(xf - mu), axis=-1, keepdims=True)
    y = (xf - mu) * lax.rsqrt(var + EPS)
    return (y * g.astype(jnp.float32) + b.astype(jnp.float32)).astype(x.dtype)

def causal_dwconv(x, w, b):
    k = w.shape[0]
    y = lax.conv_general_dilated(
        x, w[:, None, :].astype(x.dtype), window_strides=(1,), padding=[(k - 1, 0)],
        dimension_numbers=('NWC', 'WIO', 'NWC'), feature_group_count=x.shape[-1])
    return y + b

def chunk_band(t):
    b, s, h, dh = t.shape
    nc = s // CHUNK
    tc = t.reshape(b, nc, CHUNK, h, dh)
    tp = jnp.pad(tc, ((0, 0), (LEFT_CHUNKS, 0), (0, 0), (0, 0), (0, 0)))
    band = jnp.stack([tp[:, j:j + nc] for j in range(LEFT_CHUNKS + 1)], axis=2)
    return band.reshape(b, nc, BAND, h, dh)

def chunked_rel_attention(q, k, v, rel_bias):
    b, s, _ = q.shape
    nc = s // CHUNK
    qc = q.reshape(b, nc, CHUNK, N_HEADS, HEAD_DIM)
    kb = chunk_band(k.reshape(b, s, N_HEADS, HEAD_DIM))
    vb = chunk_band(v.reshape(b, s, N_HEADS, HEAD_DIM))
    scores = jnp.einsum('bcqhd,bckhd->bhcqk', qc, kb).astype(jnp.float32) * (HEAD_DIM ** -0.5)
    qi = jnp.arange(CHUNK)
    kj = jnp.arange(BAND)
    rel = LEFT_CHUNKS * CHUNK + qi[:, None] - kj[None, :]
    idx = jnp.clip(rel, -MAX_REL, MAX_REL) + MAX_REL
    bias = rel_bias[:, idx].astype(jnp.float32)
    scores = scores + bias[None, :, None, :, :]
    key_chunk = jnp.arange(nc)[:, None] - LEFT_CHUNKS + (kj // CHUNK)[None, :]
    valid = key_chunk >= 0
    scores = jnp.where(valid[None, None, :, None, :], scores, NEG_INF)
    probs = jax.nn.softmax(scores, axis=-1).astype(v.dtype)
    out = jnp.einsum('bhcqk,bckhd->bcqhd', probs, vb)
    return out.reshape(b, s, D_ATTN)

def token_mixer(h, w_in, b_in, rel_bias, w_attn_o, w_dw, b_dw, g_ln, b_ln,
                w_conv_o, b_conv_o, w_mix_o):
    z = h @ w_in + b_in
    splits = list(np.cumsum(IN_WIDTHS)[:-1])
    q, k, v, glu_a, glu_b, gate_a, gate_b = jnp.split(z, splits, axis=-1)
    a = chunked_rel_attention(q, k, v, rel_bias) @ w_attn_o
    u = glu_a * jax.nn.sigmoid(glu_b)
    u = causal_dwconv(u, w_dw, b_dw)
    u = jax.nn.silu(layer_norm(u, g_ln, b_ln))
    cb = u @ w_conv_o + b_conv_o
    y = jax.nn.sigmoid(gate_a) * a + jax.nn.sigmoid(gate_b) * cb
    return y @ w_mix_o

def conv_ffn(h, w_up, w_dw, b_dw, w_down):
    u = causal_dwconv(h @ w_up, w_dw, b_dw)
    val, gt = jnp.split(u, 2, axis=-1)
    return (jax.nn.gelu(gt) * val) @ w_down

def first_inputs(seed: int = 0) -> dict:
    key = jax.random.key(seed)
    ks = jax.random.split(key, 26)
    L = DEPTH

    def nrm(k, shape, scale):
        return jax.random.normal(k, shape, jnp.float32) * scale

    def gain(k, shape):
        return 1.0 + 0.1 * jax.random.normal(k, shape, jnp.float32)

    return {
        "x": nrm(ks[0], (BATCH, SEQ, D_MODEL), 1.0),
        "c": nrm(ks[1], (BATCH, D_MODEL), 1.0),
        "w_ada": nrm(ks[2], (L, D_MODEL, 6 * D_MODEL), 0.5 * D_MODEL ** -0.5),
        "b_ada": nrm(ks[3], (L, 6 * D_MODEL), 0.01),
        "g_pre_mix": gain(ks[4], (L, D_MODEL)),
        "g_post_mix": gain(ks[5], (L, D_MODEL)),
        "w_in": nrm(ks[6], (L, D_MODEL, D_IN), D_MODEL ** -0.5),
        "b_in": nrm(ks[7], (L, D_IN), 0.01),
        "rel_bias": nrm(ks[8], (L, N_HEADS, 2 * MAX_REL + 1), 0.5),
        "w_attn_o": nrm(ks[9], (L, D_ATTN, D_MODEL), D_ATTN ** -0.5),
        "w_dw_conv": nrm(ks[10], (L, CONV_K, D_CONV), CONV_K ** -0.5),
        "b_dw_conv": nrm(ks[11], (L, D_CONV), 0.01),
        "g_conv_ln": gain(ks[12], (L, D_CONV)),
        "b_conv_ln": nrm(ks[13], (L, D_CONV), 0.01),
        "w_conv_o": nrm(ks[14], (L, D_CONV, D_MODEL), D_CONV ** -0.5),
        "b_conv_o": nrm(ks[15], (L, D_MODEL), 0.01),
        "w_mix_o": nrm(ks[16], (L, D_MODEL, D_MODEL), D_MODEL ** -0.5),
        "g_pre_ffn": gain(ks[17], (L, D_MODEL)),
        "g_post_ffn": gain(ks[18], (L, D_MODEL)),
        "w_up": nrm(ks[19], (L, D_MODEL, 2 * D_FF), D_MODEL ** -0.5),
        "w_dw_ffn": nrm(ks[20], (L, FFN_CONV_K, 2 * D_FF), FFN_CONV_K ** -0.5),
        "b_dw_ffn": nrm(ks[21], (L, 2 * D_FF), 0.01),
        "w_down": nrm(ks[22], (L, D_FF, D_MODEL), D_FF ** -0.5),
    }

def first_block(x, c, w_ada, b_ada, g_pre_mix, g_post_mix, w_in, b_in, rel_bias,
              w_attn_o, w_dw_conv, b_dw_conv, g_conv_ln, b_conv_ln, w_conv_o,
              b_conv_o, w_mix_o, g_pre_ffn, g_post_ffn, w_up, w_dw_ffn, b_dw_ffn,
              w_down):
    c_act = jax.nn.silu(c)
    for l in range(DEPTH):
        mod = c_act @ w_ada[l] + b_ada[l]
        sh_m, sc_m, gt_m, sh_f, sc_f, gt_f = [m[:, None, :] for m in jnp.split(mod, 6, axis=-1)]
        h = rms_norm(x, g_pre_mix[l]) * (1.0 + sc_m) + sh_m
        y = token_mixer(h, w_in[l], b_in[l], rel_bias[l], w_attn_o[l], w_dw_conv[l],
                        b_dw_conv[l], g_conv_ln[l], b_conv_ln[l], w_conv_o[l],
                        b_conv_o[l], w_mix_o[l])
        x = x + gt_m * rms_norm(y, g_post_mix[l])
        h = rms_norm(x, g_pre_ffn[l]) * (1.0 + sc_f) + sh_f
        y = conv_ffn(h, w_up[l], w_dw_ffn[l], b_dw_ffn[l], w_down[l])
        x = x + gt_f * rms_norm(y, g_post_ffn[l])
    return x


DEPTH_2 = 2

N_MIXERS = 2
PLE_DIM = 256
NEG_BIG = -1e30

A_HEADS = 16
A_KV_HEADS = 4
A_GROUP = A_HEADS // A_KV_HEADS
A_HEAD_DIM = D_MODEL // A_HEADS
A_WIDTH = A_HEADS * A_HEAD_DIM
A_KV_WIDTH = A_KV_HEADS * A_HEAD_DIM
A_IN = A_WIDTH + 2 * A_KV_WIDTH + A_WIDTH
WINDOW = 128
BLOCK = 128

B_HEADS = 16
B_NOPE = 64
B_ROPE = 32
B_VDIM = 64
B_WIDTH = B_HEADS * B_VDIM
Q_LORA = 384
KV_LORA = 256
B_IN = Q_LORA + KV_LORA + B_ROPE + B_WIDTH
ROPE_THETA = 10000.0
Q_BLOCK = 128

N_A = (DEPTH_2 + 1) // 2
N_B = DEPTH_2 // 2


def rms_norm_2(x, g):
    xf = x.astype(jnp.float32)
    y = xf * lax.rsqrt(jnp.mean(xf * xf, axis=-1, keepdims=True) + EPS)
    return (y * g.astype(jnp.float32)).astype(x.dtype)

def alibi_slopes(n):
    return 2.0 ** (-8.0 * jnp.arange(1, n + 1, dtype=jnp.float32) / n)

def rotate(x, cos, sin):
    half = x.shape[-1] // 2
    x1, x2 = x[..., :half], x[..., half:]
    return jnp.concatenate([x1 * cos - x2 * sin, x1 * sin + x2 * cos], axis=-1)

def windowed_gqa(u, w_in, sink, w_out):
    B_, S, _ = u.shape
    nb = S // BLOCK
    proj = u @ w_in
    q, k, v, z = jnp.split(proj, [A_WIDTH, A_WIDTH + A_KV_WIDTH, A_WIDTH + 2 * A_KV_WIDTH], axis=-1)
    q = q.reshape(B_, nb, BLOCK, A_KV_HEADS, A_GROUP, A_HEAD_DIM).swapaxes(0, 1)
    k = k.reshape(B_, S, A_KV_HEADS, A_HEAD_DIM)
    v = v.reshape(B_, S, A_KV_HEADS, A_HEAD_DIM)
    pad = ((0, 0), (BLOCK, BLOCK), (0, 0), (0, 0))
    kp = jnp.pad(k, pad)
    vp = jnp.pad(v, pad)
    scale = A_HEAD_DIM ** -0.5
    slopes = alibi_slopes(A_HEADS).reshape(A_KV_HEADS, A_GROUP)
    sink_l = sink.astype(jnp.float32).reshape(A_KV_HEADS, A_GROUP)
    qi = jnp.arange(BLOCK)
    kj = jnp.arange(3 * BLOCK)
    rel = (kj[None, :] - BLOCK) - qi[:, None]
    dist = jnp.abs(rel).astype(jnp.float32)
    in_window = jnp.abs(rel) <= WINDOW

    def block_fn(args):
        q_blk, b = args
        start = b * BLOCK
        k_blk = lax.dynamic_slice_in_dim(kp, start, 3 * BLOCK, axis=1)
        v_blk = lax.dynamic_slice_in_dim(vp, start, 3 * BLOCK, axis=1)
        s_pos = start - BLOCK + kj
        valid = in_window & ((s_pos >= 0) & (s_pos < S))[None, :]
        logits = jnp.einsum('bqkgd,bskd->bkgqs', q_blk, k_blk).astype(jnp.float32) * scale
        logits = logits - slopes[:, :, None, None] * dist
        logits = jnp.where(valid, logits, NEG_BIG)
        sink_col = jnp.broadcast_to(sink_l[None, :, :, None, None], logits.shape[:-1] + (1,))
        probs = jax.nn.softmax(jnp.concatenate([logits, sink_col], axis=-1), axis=-1)[..., :-1]
        return jnp.einsum('bkgqs,bskd->bqkgd', probs.astype(v_blk.dtype), v_blk)

    o = lax.map(block_fn, (q, jnp.arange(nb)))
    o = o.swapaxes(0, 1).reshape(B_, S, A_WIDTH)
    return (o * jax.nn.silu(z)) @ w_out

def mla(u, w_in, q_norm, w_qb, kv_norm, w_kvb, w_out):
    B_, S, _ = u.shape
    nb = S // Q_BLOCK
    proj = u @ w_in
    cq, ckv, k_rope, z = jnp.split(proj, [Q_LORA, Q_LORA + KV_LORA, Q_LORA + KV_LORA + B_ROPE], axis=-1)
    q = (rms_norm_2(cq, q_norm) @ w_qb).reshape(B_, S, B_HEADS, B_NOPE + B_ROPE)
    q_nope, q_rope = q[..., :B_NOPE], q[..., B_NOPE:]
    kv = (rms_norm_2(ckv, kv_norm) @ w_kvb).reshape(B_, S, B_HEADS, B_NOPE + B_VDIM)
    k_nope, v = kv[..., :B_NOPE], kv[..., B_NOPE:]
    half = B_ROPE // 2
    inv_freq = ROPE_THETA ** (-jnp.arange(half, dtype=jnp.float32) / half)
    ang = jnp.arange(S, dtype=jnp.float32)[:, None] * inv_freq[None, :]
    cos, sin = jnp.cos(ang).astype(u.dtype), jnp.sin(ang).astype(u.dtype)
    q_rope = rotate(q_rope, cos[:, None, :], sin[:, None, :])
    k_rope = rotate(k_rope, cos, sin)
    scale = (B_NOPE + B_ROPE) ** -0.5
    qn = q_nope.reshape(B_, nb, Q_BLOCK, B_HEADS, B_NOPE).swapaxes(0, 1)
    qr = q_rope.reshape(B_, nb, Q_BLOCK, B_HEADS, B_ROPE).swapaxes(0, 1)

    def block_fn(args):
        qn_b, qr_b = args
        logits = (jnp.einsum('bqhd,bshd->bhqs', qn_b, k_nope)
                  + jnp.einsum('bqhr,bsr->bhqs', qr_b, k_rope)).astype(jnp.float32) * scale
        probs = jax.nn.softmax(logits, axis=-1)
        return jnp.einsum('bhqs,bshd->bqhd', probs.astype(v.dtype), v)

    o = lax.map(block_fn, (qn, qr)).swapaxes(0, 1).reshape(B_, S, B_WIDTH)
    return (o * jax.nn.silu(z)) @ w_out

def second_inputs(seed: int = 0) -> dict:
    key = jax.random.key(seed)
    ks = jax.random.split(key, 18)
    f32 = jnp.float32
    nrm = lambda k, shape, s: jax.random.normal(k, shape, f32) * s
    gain = lambda k, shape: 1.0 + 0.05 * jax.random.normal(k, shape, f32)
    return {
        "x": jax.random.normal(ks[0], (BATCH, SEQ, D_MODEL), f32),
        "p": jax.random.normal(ks[1], (DEPTH_2, BATCH, SEQ, PLE_DIM), f32),
        "norm_g": gain(ks[2], (DEPTH_2, D_MODEL)),
        "a_w_in": nrm(ks[3], (N_A, D_MODEL, A_IN), D_MODEL ** -0.5),
        "a_sink": nrm(ks[4], (N_A, A_HEADS), 1.0),
        "a_w_out": nrm(ks[5], (N_A, A_WIDTH, D_MODEL), A_WIDTH ** -0.5),
        "b_w_in": nrm(ks[6], (N_B, D_MODEL, B_IN), D_MODEL ** -0.5),
        "b_q_norm": gain(ks[7], (N_B, Q_LORA)),
        "b_w_qb": nrm(ks[8], (N_B, Q_LORA, B_HEADS * (B_NOPE + B_ROPE)), Q_LORA ** -0.5),
        "b_kv_norm": gain(ks[9], (N_B, KV_LORA)),
        "b_w_kvb": nrm(ks[10], (N_B, KV_LORA, B_HEADS * (B_NOPE + B_VDIM)), KV_LORA ** -0.5),
        "b_w_out": nrm(ks[11], (N_B, B_WIDTH, D_MODEL), B_WIDTH ** -0.5),
        "ple_w": nrm(ks[12], (DEPTH_2, PLE_DIM, D_MODEL), PLE_DIM ** -0.5),
        "ple_norm_g": gain(ks[13], (DEPTH_2, D_MODEL)),
        "ple_w_gate": nrm(ks[14], (DEPTH_2, D_MODEL, D_MODEL), D_MODEL ** -0.5),
        "final_norm_g": gain(ks[15], (D_MODEL,)),
    }

def second_block(x, p, norm_g, a_w_in, a_sink, a_w_out, b_w_in, b_q_norm, b_w_qb,
              b_kv_norm, b_w_kvb, b_w_out, ple_w, ple_norm_g, ple_w_gate, final_norm_g):
    h = x
    for i in range(DEPTH_2):
        u = rms_norm_2(h, norm_g[i])
        j = i // N_MIXERS
        if i % N_MIXERS == 0:
            y = windowed_gqa(u, a_w_in[j], a_sink[j], a_w_out[j])
        else:
            y = mla(u, b_w_in[j], b_q_norm[j], b_w_qb[j], b_kv_norm[j], b_w_kvb[j], b_w_out[j])
        h = h + y
        gate = jax.nn.sigmoid(rms_norm_2(h, ple_norm_g[i]) @ ple_w_gate[i])
        h = h + (p[i] @ ple_w[i]) * gate
    return rms_norm_2(h, final_norm_g)


def setup_inputs(seed=0):
    out = dict(first_inputs(seed))
    for name, value in second_inputs(seed + 1).items():
        if name != "x":
            out[name + "_2"] = value
    return out


def reference(
    x, c, w_ada, b_ada, g_pre_mix, g_post_mix, w_in, b_in, rel_bias, w_attn_o, w_dw_conv,
    b_dw_conv, g_conv_ln, b_conv_ln, w_conv_o, b_conv_o, w_mix_o, g_pre_ffn, g_post_ffn, w_up,
    w_dw_ffn, b_dw_ffn, w_down, p_2, norm_g_2, a_w_in_2, a_sink_2, a_w_out_2, b_w_in_2,
    b_q_norm_2, b_w_qb_2, b_kv_norm_2, b_w_kvb_2, b_w_out_2, ple_w_2, ple_norm_g_2,
    ple_w_gate_2, final_norm_g_2,
):
    x = first_block(
        x, c, w_ada, b_ada, g_pre_mix, g_post_mix, w_in, b_in, rel_bias, w_attn_o, w_dw_conv,
        b_dw_conv, g_conv_ln, b_conv_ln, w_conv_o, b_conv_o, w_mix_o, g_pre_ffn, g_post_ffn,
        w_up, w_dw_ffn, b_dw_ffn, w_down,
    )
    return second_block(
        x, p_2, norm_g_2, a_w_in_2, a_sink_2, a_w_out_2, b_w_in_2, b_q_norm_2, b_w_qb_2,
        b_kv_norm_2, b_w_kvb_2, b_w_out_2, ple_w_2, ple_norm_g_2, ple_w_gate_2, final_norm_g_2,
    )


_drawn_inputs = setup_inputs


def setup_inputs(seed=0):
    import zlib

    import numpy as np

    out = dict(_drawn_inputs(seed))
    spreads = {}
    factors = {'b_ada': 3.992,
     'b_in': 8.0,
     'b_dw_conv': 8.0,
     'b_conv_ln': 8.0,
     'b_conv_o': 8.0,
     'b_dw_ffn': 8.0,
     'norm_g_2': 4.574,
     'a_sink_2': 64.0,
     'b_q_norm_2': 8.0,
     'b_kv_norm_2': 8.0,
     'ple_norm_g_2': 13.875}
    for name, (base, spread) in spreads.items():
        noise = np.random.default_rng([zlib.crc32(name.encode()), seed]).standard_normal(out[name].shape)
        drawn = base * np.exp(spread * noise) if base else spread * noise
        out[name] = __import__('jax').numpy.asarray(drawn.astype(out[name].dtype))
    for name, factor in factors.items():
        out[name] = (out[name] * factor).astype(out[name].dtype)
    return out
```

```python
from contextlib import ExitStack

import numpy as np

import concourse.bass as bass
from concourse import mybir

F32 = mybir.dt.float32
F32R = mybir.dt.float32r
ALU = mybir.AluOpType
ACT = mybir.ActivationFunctionType
AX = mybir.AxisListType

P = 128
TOK = 512
D = 1024
KT = D // P
NT = TOK // P
EPS = 1e-6

H1 = 8
HD = 64
D_ATTN = H1 * HD
D_CONV = 512
CONV_K = 31
PAD = CONV_K - 1
CT = D_CONV // P
CHUNK = 64
MAX_REL = 128
D_FF = 2816
FT = D_FF // P
FFN_K = 3
A_HEADS, A_KV, A_GROUP = 16, 4, 4
WINDOW = 128
B_HEADS, B_NOPE, B_ROPE, B_V = 16, 64, 32, 64
Q_LORA, KV_LORA = 384, 256
QT, KVT = Q_LORA // P, KV_LORA // P
PLE = 256
PT_K = PLE // P
MASKED = -1e30
LOWEST = -3e38

CHW = KT * P
RAW = 2
SLOTS = 4
WEIGHT_LEAD = 3
LIN = 4
S_BANK, T_BANK = 4, 6
MOD_BANK, STAT_BANK = 6, 7

STAGES = [("glu", 8), ("qk", 8), ("v", 4), ("gates", 3 * KT), ("mix", KT), ("up", 2 * FT), ("down", FT),
          ("a_q", KT), ("a_k", 2), ("a_z", KT), ("a_v", 2), ("a_out", KT), ("a_ple", 2), ("a_gate", KT),
          ("b_c", 6), ("b_z", KT), ("b_v0", 1), ("b_h0", 4), ("b_v1", 1), ("b_h1", 4), ("b_out", KT),
          ("b_ple", 2), ("b_gate", KT)]
CH = {}
N_CHUNKS = 0
for _name, _n in STAGES:
    CH[_name] = N_CHUNKS
    N_CHUNKS += _n

VECS = [("c", KT), ("b_ada", 6 * KT), ("g_pre_mix", KT), ("g_post_mix", KT), ("b_in", 36), ("w_dw", CONV_K * CT),
        ("b_dw", CT), ("g_ln", CT), ("b_ln", CT), ("b_conv_o", KT), ("g_pre_ffn", KT), ("g_post_ffn", KT),
        ("w_dwf", FFN_K * 2 * FT), ("b_dwf", 2 * FT), ("norm_a", KT), ("norm_b", KT), ("q_norm", QT),
        ("kv_norm", KVT), ("ple_g0", KT), ("ple_g1", KT), ("final_g", KT)]
VO = {}
N_VECS = 0
for _name, _n in VECS:
    VO[_name] = N_VECS
    N_VECS += _n
BI_Q, BI_K, BI_V, BI_GA, BI_GB, BI_A, BI_B = 0, 4, 8, 12, 16, 20, 28

ADA_LATE = [2, 4, 3, 5]


def head_order():
    order = []
    for pair in range(A_KV // 2):
        for j in range(A_GROUP):
            order += [2 * pair * A_GROUP + j, (2 * pair + 1) * A_GROUP + j]
    return order


def mla_tiles():
    order = [("k", 0), ("q", 0), ("q", 1)]
    for h in range(8):
        if h:
            order.append(("o", h - 1))
        if h + 2 < 8:
            if h % 2 == 0:
                order.append(("k", h + 2))
            order.append(("q", h + 2))
    return order + [("o", 7)]


def build(nc, t_x, t_w, t_ada, t_vecs, t_ident, t_rope, t_rel, t_alibi, t_sink, t_p, out):
    with ExitStack() as ctx:
        base0 = [None]

        def sb(name, shape, dt=F32):
            return ctx.enter_context(nc.sbuf_tensor(name, shape, dt))

        def sem(name):
            return ctx.enter_context(nc.semaphore(name))

        x = sb("x_resid", [P, KT, TOK])
        a_hi, a_lo = sb("a_hi", [P, KT, TOK], F32R), sb("a_lo", [P, KT, TOK], F32R)
        w_raw = sb("w_raw", [P, RAW, CHW])
        w_hi, w_lo = sb("w_hi", [P, SLOTS, CHW], F32R), sb("w_lo", [P, SLOTS, CHW], F32R)
        vecs = sb("vecs", [P, N_VECS])
        ident = sb("ident", [P, P])
        ones = sb("ones", [P, P])
        rope = sb("rope", [P, TOK])
        sink = sb("sink", [P, A_HEADS])
        mod = sb("mod", [P, 6 * KT])
        gvec = sb("gvec", [P, 4 * KT])
        c_act = sb("c_act", [P, 2 * KT])
        rs = sb("rs", [P, 3, TOK])
        sq = sb("sq", [P, 2, TOK])
        tmp = sb("tmp", [P, 2, TOK])
        col = sb("col", [P, 6, 4])
        rcol = sb("rcol", [P, NT])
        arena_kib = 100
        slab_at = -(-nc.sbuf_base // 64) * 64
        sb("arena", [P, arena_kib * 256 + 16])

        def at(name, kib, shape, dt=F32):
            size = 4 * int(np.prod(shape[1:]))
            assert kib * 1024 + size <= arena_kib * 1024, name
            return nc.alloc_sbuf_tensor_at(name, shape, dt, offset=slab_at + int(kib * 1024))

        qk_hi, qk_lo = at("qk_hi", 0, [P, 8, TOK], F32R), at("qk_lo", 16, [P, 8, TOK], F32R)
        v_hi, v_lo = at("v_hi", 32, [P, NT, D_ATTN], F32R), at("v_lo", 40, [P, NT, D_ATTN], F32R)
        c_acc = at("c_acc", 48, [P, CT, TOK])
        u_pad = at("u_pad", 56, [P, CT, PAD + TOK])
        rel = at("rel", 65, [P, 2, TOK])
        p1 = at("p1", 69, [P, 4, TOK])
        pt1_hi, pt1_lo = at("pt1_hi", 77, [P, NT, TOK], F32R), at("pt1_lo", 85, [P, NT, TOK], F32R)
        ada_a = at("ada_a", 69, [P, 6, D])
        ada_b = at("ada_b", 92, [P, 2, D])
        acc_a = at("acc_a", 48, [P, 2, D])
        acc_b = at("acc_b", 56, [P, D])
        sig = at("sig", 93, [P, TOK])
        cv_hi, cv_lo = at("cv_hi", 32, [P, CT, TOK], F32R), at("cv_lo", 40, [P, CT, TOK], F32R)
        gsig = at("gsig", 8, [P, 2, TOK])
        gprod = at("gprod", 24, [P, 2, TOK])
        y_hi, y_lo = at("y_hi", 60, [P, KT, TOK], F32R), at("y_lo", 76, [P, KT, TOK], F32R)
        y_f = at("y_f", 0, [P, KT, TOK])
        g_hi, g_lo = at("g_hi", 0, [P, FT, TOK], F32R), at("g_lo", 44, [P, FT, TOK], F32R)
        U0 = FFN_K - 1
        u_ff = at("u_ff", 88, [P, 4, U0 + TOK])
        c_gate = at("c_gate", 97, [P, TOK])
        c_val, gel = sq[:, 1, :], sq[:, 0, :]
        y_d = at("y_d", 0, [P, KT, TOK])
        b_hi, b_lo = at("b_hi", 0, [P, KT, TOK], F32R), at("b_lo", 16, [P, KT, TOK], F32R)
        ka_hi, ka_lo = at("ka_hi", 32, [P, 2, TOK], F32R), at("ka_lo", 36, [P, 2, TOK], F32R)
        va_hi, va_lo = at("va_hi", 40, [P, NT, 256], F32R), at("va_lo", 44, [P, NT, 256], F32R)
        z2 = at("z2", 48, [P, KT, TOK])
        p2 = at("p2", 64, [P, 4, 384])
        pt2_hi, pt2_lo = at("pt2_hi", 72, [P, NT, TOK], F32R), at("pt2_lo", 80, [P, NT, TOK], F32R)
        alibi = at("alibi", 88, [P, 2, 384])
        zs = at("zs", 92, [P, TOK])
        pl = at("pl", 32, [P, KT, TOK])
        p_raw = at("p_raw", 88, [P, PT_K, TOK])
        p_hi, p_lo = at("p_hi", 92, [P, PT_K, TOK], F32R), at("p_lo", 96, [P, PT_K, TOK], F32R)
        gs2 = at("gs2", 72, [P, 2, TOK])
        vb_hi, vb_lo = at("vb_hi", 0, [P, NT, TOK], F32R), at("vb_lo", 8, [P, NT, TOK], F32R)
        z3 = at("z3", 32, [P, KT, TOK])
        cq_hi, cq_lo = at("cq_hi", 48, [P, QT, TOK], F32R), at("cq_lo", 54, [P, QT, TOK], F32R)
        ck_hi, ck_lo = at("ck_hi", 60, [P, KVT, TOK], F32R), at("ck_lo", 64, [P, KVT, TOK], F32R)
        cq_f = at("cq_f", 76, [P, QT + KVT, TOK])
        kr_f = at("kr_f", 86, [P, TOK])
        p3 = at("p3", 68, [P, 4, TOK])
        pt3_hi, pt3_lo = at("pt3_hi", 76, [P, NT, TOK], F32R), at("pt3_lo", 84, [P, NT, TOK], F32R)
        q3_hi, q3_lo = at("q3_hi", 16, [P, 2, TOK], F32R), at("q3_lo", 20, [P, 2, TOK], F32R)
        k3_hi, k3_lo = at("k3_hi", 92, [P, 2, TOK], F32R), at("k3_lo", 96, [P, 2, TOK], F32R)
        q3_f = at("q3_f", 24, [P, TOK])
        q3_r = at("q3_r", 26, [P, TOK])
        zs3 = at("zs3", 68, [P, TOK])
        kr_r = at("kr_r", 88, [P, TOK])

        ps = ctx.enter_context(nc.psum_tensor("ps", [P, 8, TOK], F32))

        consts_in, x_in, rel_in, sink_in = sem("consts_in"), sem("x_in"), [sem(f"rel_in{i}") for i in range(2)], sem("sink_in")
        alibi_in, p_in, out_done = [sem(f"alibi_in{i}") for i in range(2)], sem("p_in"), sem("out_done")
        w_land = [sem(f"w_land{i}") for i in range(RAW)]
        w_hi_done, w_lo_done, down_step = sem("w_hi_done"), sem("w_lo_done"), sem("down_step")
        ada_land = [sem(f"ada_land{i}") for i in range(8)]
        ada_used = sem("ada_used")
        sig_c, c_ready, mod_sum, mod_ready, gains = sem("sig_c"), sem("c_ready"), sem("mod_sum"), sem("mod_ready"), sem("gains")
        ones_set, margins = sem("ones_set"), sem("margins")
        sq_ready, sq_used, stat_free, rs_ready = sem("sq_ready"), sem("sq_used"), sem("stat_free"), sem("rs_ready")
        tmp_w, hi_done = sem("tmp_w"), sem("hi_done")
        lin_done = sem("lin_done")
        dve_step, act_step, conv_step = sem("dve_step"), sem("act_step"), sem("conv_step")
        s_done, s_free, m_ready, e_done = sem("s_done"), sem("s_free"), sem("m_ready"), sem("e_done")
        r_ready, p_ready, t_done, pt_hi_done, pt_ready = sem("r_ready"), sem("p_ready"), sem("t_done"), sem("pt_hi_done"), sem("pt_ready")
        rel_ready = sem("rel_ready")
        h_ready = {n: sem("ready_" + n) for n in (
            "h1", "glu_sig", "glu", "conv", "qk", "v", "o1_half", "o1", "ln_mean", "cv", "gate_sig", "gate_a", "y", "y_f", "x_mix", "h2",
            "u_val", "u_gate", "cf_val", "cf_gate", "gel", "g", "down", "y_d", "x_ffn",
            "in_a", "q_a", "k_a", "z_t", "z_sig", "z_a", "rcol", "v_a", "o2_half", "o2", "x_attn", "in_g", "p", "pl", "gt", "gsig", "x_ple",
            "in_b", "cq", "kr", "kr_sum", "cqn", "ln_sum", "cn", "cn_sig", "rcol_t", "z_tb", "z_sigb", "z_b", "v_b", "q_t", "q_r", "q_b", "k_b", "o3_half", "o3", "fin")}
        R = h_ready
        v_step = sem("v_step")

        def v(name, i=0, n=1):
            return vecs[:, VO[name] + i:VO[name] + i + n]

        evicted = []

        def plan(n, s, start=0, per=1):
            first = len(evicted)
            evicted.extend((s, start + per * (j + 1)) for j in range(n))
            return first

        LT = {}
        first = len(evicted)
        for f in range(CT):
            evicted.append((R["glu"], f + 1))
            evicted.append((R["glu_sig"], f + 1))
        LT["glu"] = first
        LT["qk"] = plan(8, R["qk"])
        LT["v"] = plan(NT, R["v"])
        LT["o1"] = len(evicted)
        for i in range(H1 // 2):
            evicted += [(R["o1_half"], i + 1), (R["o1"], i + 1)]
        LT["gates"] = len(evicted)
        for f in range(KT):
            evicted += [(R["gate_sig"], 2 * f + 1), (R["gate_sig"], 2 * f + 2), (R["gate_a"], 2 * f + 1), (R["y"], f + 1)]
        LT["mix"] = plan(KT, R["y_f"])
        up_free = 2
        LT["up"] = len(evicted)
        for i in range(FT):
            evicted += [(R["u_val"], up_free + i + 1), (R["u_gate"], up_free + i + 1)]
        n_up = len(evicted)
        LT["a_q"] = plan(KT, R["q_a"])
        LT["a_k"] = plan(2, R["k_a"])
        LT["a_z"] = plan(KT, R["z_t"])
        LT["a_v"] = plan(NT, R["v_a"])
        LT["o2"] = len(evicted)
        for i in range(A_HEADS // 2):
            evicted += [(R["o2_half"], i + 1), (R["o2"], i + 1)]
        for l, s in (("a", 0), ("b", KT)):
            if l == "b":
                LT["b_c"] = len(evicted)
                evicted += [(R["cq"], j + 1) for j in range(QT + KVT)] + [(R["kr"], 1)]
                LT["b_z"] = plan(KT, R["z_tb"])
                for half in range(2):
                    LT[f"b_v{half}"] = plan(NT, R["v_b"], NT * half)
                    for kind, h in mla_tiles():
                        g = 8 * half + h
                        if h == 0 and kind == "k":
                            LT[f"b_h{half}"] = len(evicted)
                        evicted.append({"k": (R["k_b"], g + 2), "q": (R["q_t"], g + 1),
                                        "o": (R["o3_half"], g // 2 + 1) if h % 2 == 0 else (R["o3"], g // 2 + 1)}[kind])
            LT[l + "_out"] = plan(KT, R["x_attn"], s)
            LT[l + "_ple"] = plan(KT, R["pl"], s)
            LT[l + "_gate"] = plan(KT, R["gt"], s)

        class Attn:
            def __init__(self, heads, n0, rows, q, k, vv, pbuf, pt, spans, lin, over_keys):
                self.heads, self.n0, self.rows, self.q, self.k, self.v = heads, n0, rows, q, k, vv
                self.p, self.pt, self.spans, self.lin, self.over_keys = pbuf, pt, spans, lin, over_keys

        def half(h):
            return slice(64 * (h % 2), 64 * (h % 2) + 64)

        causal = [(0, t + 1) for t in range(NT)]
        band = [(max(t - 1, 0), min(t + 2, NT)) for t in range(NT)]
        full = [(0, NT)] * NT
        n1 = NT * H1
        n2 = n1 + NT * A_HEADS
        attn1 = Attn(H1, 0, half, lambda h: (qk_hi[half(h), h // 2, :], qk_lo[half(h), h // 2, :]),
                     lambda h: (qk_hi[half(h), 4 + h // 2, :], qk_lo[half(h), 4 + h // 2, :]),
                     lambda h, s: (v_hi[:, s, P * (h // 2):P * (h // 2) + P], v_lo[:, s, P * (h // 2):P * (h // 2) + P]),
                     p1, (pt1_hi, pt1_lo), causal, lambda h: LT["o1"] + h, [(0, 0, 4), (1, 1, 4), (2, 2, 4), (3, 3, 4)])
        attn2 = Attn(A_HEADS, n1, half, lambda h: (b_hi[half(h), h // 2, :], b_lo[half(h), h // 2, :]),
                     lambda h: (ka_hi[half(h), h // 8, :], ka_lo[half(h), h // 8, :]),
                     lambda h, s: (va_hi[:, s, P * (h // 8):P * (h // 8) + P], va_lo[:, s, P * (h // 8):P * (h // 8) + P]),
                     p2, (pt2_hi, pt2_lo), band, lambda h: LT["o2"] + h, [(0, 0, 2), (1, 0, 3), (2, 1, 4), (3, 2, 4)])

        def mla(hf):
            order = mla_tiles()
            place = {kh: i for i, kh in enumerate(order)}
            a = Attn(8, n2 + 8 * NT * hf, half, lambda h: (q3_hi[0:96, h % 2, :], q3_lo[0:96, h % 2, :]),
                     lambda h: (k3_hi[0:96, h % 2, :], k3_lo[0:96, h % 2, :]),
                     lambda h, s: (vb_hi[:, s, P * (h // 2):P * (h // 2) + P], vb_lo[:, s, P * (h // 2):P * (h // 2) + P]),
                     p3, (pt3_hi, pt3_lo), full, lambda h: LT[f"b_h{hf}"] + place[("o", h)], [(s, 0, 4) for s in range(4)])
            a.q_lin = lambda h: LT[f"b_h{hf}"] + place[("q", h)]
            a.k_lin = lambda h: LT[f"b_h{hf}"] + place[("k", h)]
            a.hf = hf
            return a

        attn3 = [mla(0), mla(1)]

        used_at = {}

        def chunks_of(name, tiles, per=1, first=None):
            t0 = LT[name] if first is None else first
            for j in range(dict(STAGES)[name]):
                used_at[CH[name] + j] = (lin_done, t0 + tiles * (j + 1) // per)

        for name in ("glu", "qk", "mix", "up", "a_q", "a_k", "a_z", "a_out", "a_gate", "b_c", "b_z", "b_out", "b_gate"):
            chunks_of(name, 1)
        for j in range(3):
            used_at[CH["v"] + j] = (v_step, j + 1)
        used_at[CH["v"] + 3] = (lin_done, LT["v"] + NT)
        for f in range(KT):
            for j, tiles in enumerate((1, 2, 4)):
                used_at[CH["gates"] + 3 * f + j] = (lin_done, LT["gates"] + 4 * f + tiles)
        for j in range(FT):
            used_at[CH["down"] + j] = (down_step, j + 1)
        used_at[CH["a_v"]] = (v_step, 4)
        used_at[CH["a_v"] + 1] = (lin_done, LT["a_v"] + NT)
        for l in "ab":
            chunks_of(l + "_ple", KT // 2)
        for hf in range(2):
            used_at[CH[f"b_v{hf}"]] = (lin_done, LT[f"b_v{hf}"] + NT)
            for pair in range(4):
                used_at[CH[f"b_h{hf}"] + pair] = (lin_done, attn3[hf].q_lin(2 * pair + 1) + 1)

        block = ctx.enter_context(nc.Block())

        @block.sync
        def _(sp):
            for n in range(RAW):
                sp.dma_start(w_raw[:, n, :], t_w[n]).then_inc(w_land[n], 16)
            turns = (N_CHUNKS - RAW) // RAW
            with sp.Fori(0, turns) as i:
                for j in range(RAW):
                    sp.wait_ge(w_lo_done, i * RAW + (j + 1))
                    sp.dma_start(w_raw[:, j, :], t_w[bass.ds(i * RAW + (RAW + j), 1)].rearrange("o p n -> (o p) n")
                                 ).then_inc(w_land[j], 16)
            for n in range(RAW + turns * RAW, N_CHUNKS):
                sp.wait_ge(w_lo_done, n - RAW + 1)
                sp.dma_start(w_raw[:, n % RAW, :], t_w[n]).then_inc(w_land[n % RAW], 16)
            for k in range(KT):
                sp.wait_ge(R["fin"], k + 1)
                sp.dma_start(out[:, k, :], x[:, k, :]).then_inc(out_done, 16)
            sp.wait_ge(out_done, 16 * KT)

        @block.gpsimd
        def _(pool):
            pool.dma_start(vecs[:, :], t_vecs).then_inc(consts_in, 16)
            pool.dma_start(x[:, :, :], t_x).then_inc(x_in, 16)
            pool.dma_start(ident[:, :], t_ident).then_inc(consts_in, 16)
            pool.dma_start(rope[:, :], t_rope).then_inc(consts_in, 16)
            pool.memset(ones[:, :], 1.0).then_inc(ones_set, 1)
            for u in range(16):
                if u >= 6:
                    pool.wait_ge(ada_used, u - 5)
                pool.dma_start(ada_a[:, u % 6, :], t_ada[(1, 0)[u // 8], u % 8]).then_inc(ada_land[u % 6], 16)
            pool.dma_start(sink[:, :], t_sink.to_broadcast([P, A_HEADS])).then_inc(sink_in, 16)

            pool.wait_ge(mod_ready, 2)
            pool.memset(u_pad[:, :, 0:PAD], 0.0).then_inc(margins, 1)
            for h in range(H1):
                if h >= 2:
                    pool.wait_ge(s_free, NT * (h - 1))
                else:
                    pool.wait_ge(ada_used, 16)
                pool.dma_start(rel[:, h % 2, :], t_rel[h]).then_inc(rel_in[h % 2], 16)
                pool.wait_ge(rel_in[h % 2], 16 * (h // 2 + 1))
                pool.memset(rel[0:CHUNK, h % 2, TOK - CHUNK:TOK], MASKED).then_inc(rel_ready, 1)
            for u in range(32):
                if u < 2:
                    pool.wait_ge(lin_done, LT["o1"] + H1)
                else:
                    pool.wait_ge(ada_used, 16 + u - 1)
                pool.dma_start(ada_b[:, u % 2, :], t_ada[ADA_LATE[u // 8], u % 8]).then_inc(ada_land[6 + u % 2], 16)
            pool.wait_ge(ada_used, 48)
            pool.wait_ge(R["y_f"], KT)
            pool.memset(u_ff[:, :, 0:U0], 0.0).then_inc(margins, 1)
            for layer in range(2):
                if layer == 0:
                    for h in range(A_HEADS):
                        if h < 2:
                            pool.wait_ge(R["x_ffn"], KT)
                        else:
                            pool.wait_ge(s_free, attn2.n0 + NT * (h - 1))
                        pool.dma_start(alibi[:, h % 2, :], t_alibi[h]).then_inc(alibi_in[h % 2], 16)
                else:
                    for g in range(16):
                        pool.wait_ge(R["q_t"], g + 1)
                        pool.tensor_tensor(q3_f[64:96, :], q3_f[64:96, :], q3_r[64:96, :], ALU.add).then_inc(R["q_r"], 1)
                pool.wait_ge((R["o2"], R["o3"])[layer], 8)
                pool.dma_start(p_raw[:, :, :], t_p[layer]).then_inc(p_in, 16)

        @block.tensor
        def _(pe):
            events, squares = [0], [0]

            def mm3(o, w, r, start, stop, skip=False):
                pe.matmul(o, w[0], r[0], start=start, stop=False, skip_group_check=skip)
                pe.matmul(o, w[0], r[1], start=False, stop=False, skip_group_check=skip)
                return pe.matmul(o, w[1], r[0], start=False, stop=stop, skip_group_check=skip)

            def weights(n):
                pe.wait_ge(w_lo_done, n + 1)
                return w_hi[:, n % SLOTS, :], w_lo[:, n % SLOTS, :]

            def free_bank(tile):
                if tile >= LIN:
                    s, val = (R["y_d"], KT) if n_up <= tile < n_up + LIN else evicted[tile - LIN]
                    pe.wait_ge(s, val)
                return ps[:, tile % LIN, :]

            def cols(w, at, width=P):
                return tuple(part[:, at:at + width] for part in w)

            def tiles(name, n, src, ready=None, base=0, kt=KT, per=1, between=None):
                for f in range(n):
                    o = free_bank(LT[name] + f)
                    w = weights(CH[name] + f // per)
                    for k in range(kt):
                        if ready is not None:
                            pe.wait_ge(ready, base + k + 1)
                        m = mm3(o, cols(w, P * (f % per * kt + k)), (src[0][:, k, :], src[1][:, k, :]), k == 0, k == kt - 1)
                    m.then_inc(lin_done, 1)
                    if between is not None:
                        between(f)

            def token_tiles(tile, chunk, n_chunks, src, width, kt, base_step, skip=False):
                banks = [free_bank(tile + t) for t in range(NT)]
                per = kt // n_chunks
                for j in range(n_chunks):
                    w = weights(chunk + j)
                    for kk in range(per):
                        k = j * per + kk
                        for t in range(NT):
                            m = mm3(banks[t][:, 0:width], (src[0][:, k, P * t:P * t + P], src[1][:, k, P * t:P * t + P]),
                                    cols(w, kk * width, width), k == 0, k == kt - 1)
                            if k == kt - 1:
                                m.then_inc(lin_done, 1)
                            elif kk == per - 1 and t == NT - 1:
                                m.then_inc(v_step, 1)

            def begin_event():
                if events[0]:
                    pe.wait_ge(stat_free, events[0])
                events[0] += 1

            def square_sum(k, n):
                if k == 0:
                    begin_event()
                q = squares[0]
                pe.wait_ge(sq_ready, q + 1)
                pe.matmul(ps[:, STAT_BANK, :], ones[:, :], sq[:, q % 2, :], start=(k == 0), stop=(k == n - 1)).then_inc(sq_used, 1)
                squares[0] += 1

            def behind(f):
                if f:
                    square_sum(f - 1, KT)

            def mod_group(g, acc):
                pe.wait_ge(ada_used, 8 * (g + 1))
                if g:
                    pe.wait_ge(mod_ready, g)
                for j in range(KT):
                    m = pe.matmul(ps[:, MOD_BANK, j:j + 1], acc[:, P * j:P * j + P], ones[:, 0:1], start=True, stop=True)
                m.then_inc(mod_sum, 1)

            def scores(a, h, t):
                n = a.n0 + NT * h + t
                if n >= 2:
                    pe.wait_ge(s_free, n - 1)
                b, e = a.spans[t]
                q, k = a.q(h), a.k(h)
                mm3(ps[:, S_BANK + n % 2, 0:P * (e - b)], cols(q, P * t), cols(k, P * b, P * (e - b)), True, True).then_inc(s_done, 1)

            def turn(a, h, t):
                n = a.n0 + NT * h + t
                pe.wait_ge(p_ready, n + 1)
                if n >= 2:
                    pe.wait_ge(pt_ready, n - 1)
                b, e = a.spans[t]
                for s in range(b, e):
                    m = pe.transpose(ps[:, T_BANK + n % 2, P * s:P * s + P], a.p[:, n % 4, P * (s - b):P * (s - b) + P], ident[:, :])
                m.then_inc(t_done, 1)

            def values(a, h):
                pe.wait_ge(pt_ready, a.n0 + NT * (h + 1))
                o = free_bank(a.lin(h))
                for i, (s, t0, t1) in enumerate(a.over_keys):
                    r = tuple(part[:, s, P * t0:P * t1] for part in a.pt)
                    m = mm3(o[:, P * t0:P * t1], a.v(h, s), r, i == 0, i == len(a.over_keys) - 1, skip=True)
                m.then_inc(lin_done, 1)

            def attention(a, before=None, between=None):
                pe.wait_ge(stat_free, events[0])
                for h in range(-1, a.heads + 1):
                    for t in range(NT):
                        if h + 1 < a.heads:
                            if t == 0 and before is not None:
                                before(h + 1)
                            scores(a, h + 1, t)
                        if t == 0 and h >= 1:
                            values(a, h - 1)
                        if 0 <= h < a.heads:
                            turn(a, h, t)
                        if t == 1 and 0 <= h and between is not None:
                            between(h)

            A, B = (a_hi, a_lo), (b_hi, b_lo)

            pe.wait_ge(ones_set, 1)
            mod_group(0, acc_a[:, 0, :])
            mod_group(1, acc_a[:, 1, :])
            for k in range(KT):
                square_sum(k, KT)
            tiles("glu", 8, A, R["h1"])
            tiles("qk", 8, A)
            token_tiles(LT["v"], CH["v"], 4, A, D_ATTN, KT, 0)
            pe.wait_ge(R["qk"], 8)
            pe.wait_ge(R["v"], NT)
            attention(attn1)
            pe.wait_ge(conv_step, CONV_K * CT)
            pe.wait_ge(pt_ready, n1)
            pe.wait_ge(stat_free, events[0])
            for k in range(CT):
                m = pe.matmul(ps[:, STAT_BANK, :], ones[:, :], c_acc[:, k, :], start=(k == 0), stop=(k == CT - 1))
            m.then_inc(R["ln_sum"], 1)
            pe.wait_ge(R["ln_mean"], CT)
            for k in range(CT):
                square_sum(k, CT)
            O1, CV = (qk_hi, qk_lo), (cv_hi, cv_lo)
            pe.wait_ge(R["o1"], H1 // 2)
            for f in range(KT):
                t0, c0 = LT["gates"] + 4 * f, CH["gates"] + 3 * f
                for j in range(2):
                    o, w = free_bank(t0 + j), weights(c0 + j)
                    for k in range(KT):
                        m = mm3(o, cols(w, P * k), (a_hi[:, k, :], a_lo[:, k, :]), k == 0, k == KT - 1)
                    m.then_inc(lin_done, 1)
                w = weights(c0 + 2)
                for j, src in enumerate((O1, CV)):
                    o = free_bank(t0 + 2 + j)
                    for k in range(CT):
                        if src is CV:
                            pe.wait_ge(R["cv"], k + 1)
                        m = mm3(o, cols(w, P * (CT * j + k)), (src[0][:, k, :], src[1][:, k, :]), k == 0, k == CT - 1)
                    m.then_inc(lin_done, 1)
                if f % 2 == 1:
                    mod_group(2 + f // 2, acc_b)
            tiles("mix", KT, (y_hi, y_lo), R["y"], between=behind)
            square_sum(KT - 1, KT)
            for k in range(KT):
                square_sum(k, KT)
            pe.wait_ge(R["h2"], KT)
            with pe.Fori(0, FT // 2) as i:
                for j in range(4):
                    tile, n = LT["up"] + j, CH["up"] + j
                    pe.wait_ge(w_lo_done, i * 4 + (n + 1))
                    pe.wait_ge((R["u_val"], R["u_gate"])[j % 2], i * 2 + (up_free + j // 2 - 1))
                    w = w_hi[:, n % SLOTS, :], w_lo[:, n % SLOTS, :]
                    for k in range(KT):
                        m = mm3(ps[:, tile % LIN, :], cols(w, P * k), (a_hi[:, k, :], a_lo[:, k, :]), k == 0, k == KT - 1)
                    m.then_inc(lin_done, 1)
            pe.wait_ge(R["u_val"], up_free + FT)
            pe.wait_ge(R["u_gate"], up_free + FT)

            def down(k, n, slot, start, stop, ready):
                pe.wait_ge(w_lo_done, n)
                pe.wait_ge(R["g"], ready)
                w = w_hi[:, slot, :], w_lo[:, slot, :]
                r = (g_hi[:, k, :], g_lo[:, k, :]) if isinstance(k, int) else tuple(
                    g.rearrange("p k n -> p (k n)")[:, bass.ds(k, TOK)] for g in (g_hi, g_lo))
                for f in range(KT):
                    m = mm3(ps[:, f, :], cols(w, P * f), r, start, stop)
                m.then_inc(down_step, 1)

            for k in range(2):
                down(k, CH["down"] + k + 1, (CH["down"] + k) % SLOTS, k == 0, False, k + 1)
            turns = (FT - 2) // 4
            with pe.Fori(0, turns - 1) as i:
                for j in range(4):
                    n = CH["down"] + 2 + j
                    down(i * (4 * TOK) + (2 + j) * TOK, i * 4 + (n + 1), n % SLOTS, False, False, i * 4 + (3 + j))
            for k in range(FT - 4, FT):
                down(k, CH["down"] + k + 1, (CH["down"] + k) % SLOTS, False, k == FT - 1, k + 1)
            for k in range(KT):
                if k == 0:
                    pe.wait_ge(R["y_d"], 1)
                square_sum(k, KT)
            pe.wait_ge(R["y_d"], KT)
            for k in range(KT):
                square_sum(k, KT)

            tiles("a_q", KT, A, R["in_a"])
            tiles("a_k", 2, A)
            tiles("a_z", KT, A)
            pe.wait_ge(rs_ready, 6)
            begin_event()
            for t in range(NT):
                m = pe.transpose(ps[:, STAT_BANK, P * t:P * t + P], rs[:, 5 % 3, P * t:P * t + P], ident[:, :])
            m.then_inc(R["rcol_t"], 1)
            token_tiles(LT["a_v"], CH["a_v"], 2, A, 256, KT, 3)
            pe.wait_ge(R["q_a"], KT)
            pe.wait_ge(R["k_a"], 2)
            pe.wait_ge(R["v_a"], NT)
            attention(attn2)

            def rest(l, src, after, o_ready):
                pe.wait_ge(pt_ready, n2 if l == "a" else n2 + 16 * NT)
                pe.wait_ge(o_ready, 8)
                tiles(l + "_out", KT, src, between=behind)
                square_sum(KT - 1, KT)
                base = 0 if l == "a" else PT_K
                tiles(l + "_ple", KT, (p_hi, p_lo), R["p"], base, kt=PT_K, per=4)
                tiles(l + "_gate", KT, after, R["in_g"], 0 if l == "a" else KT, between=behind)
                square_sum(KT - 1, KT)

            rest("a", B, A, R["o2"])

            tiles("b_c", 6, B, R["in_b"])
            for k in range(QT):
                square_sum(k, QT)
            for k in range(KVT):
                square_sum(k, KVT)
            tiles("b_z", KT, B)
            pe.wait_ge(R["cqn"], QT + KVT)
            pe.wait_ge(R["kr"], 3)
            for hf in range(2):
                a = attn3[hf]
                token_tiles(LT[f"b_v{hf}"], CH[f"b_v{hf}"], 1, (ck_hi, ck_lo), TOK, KVT, 0)

                def queries(h):
                    w = weights(CH[f"b_h{hf}"] + h // 2)
                    o = free_bank(a.q_lin(h))
                    for k in range(QT):
                        m = mm3(o, cols(w, P * (h % 2 * QT + k)), (cq_hi[:, k, :], cq_lo[:, k, :]), k == 0, k == QT - 1)
                    m.then_inc(lin_done, 1)

                def keys(h):
                    w = weights(CH[f"b_h{hf}"] + h // 2)
                    o = free_bank(a.k_lin(h))
                    for k in range(KVT):
                        m = mm3(o, cols(w, P * (2 * QT + k)), (ck_hi[:, k, :], ck_lo[:, k, :]), k == 0, k == KVT - 1)
                    m.then_inc(lin_done, 1)

                def before(h):
                    pe.wait_ge(R["q_b"], 8 * hf + h + 1)
                    pe.wait_ge(R["k_b"], 8 * hf + h + 1)
                    if h == 0:
                        pe.wait_ge(R["v_b"], NT * (hf + 1))

                def between(h):
                    if h + 2 < a.heads:
                        if h % 2 == 0:
                            keys(h + 2)
                        queries(h + 2)

                keys(0)
                queries(0)
                queries(1)
                attention(a, before, between)
            rest("b", A, B, R["o3"])

        @block.scalar
        def _(act):
            tmps, his, sqs, rss, steps, evs = [0], [0], [0], [0], [0], [0]

            def split(n):
                if n >= N_CHUNKS:
                    return
                act.wait_ge(w_land[n % RAW], 16 * (n // RAW + 1))
                if n >= SLOTS:
                    act.wait_ge(*used_at[n - SLOTS])
                act.activation(w_hi[:, n % SLOTS, :], w_raw[:, n % RAW, :], ACT.Copy).then_inc(w_hi_done, 1)

            def hi_of_tmp(dst, n=None):
                act.wait_ge(tmp_w, tmps[0] + 1)
                act.activation(dst, tmp[:, tmps[0] % 2, :] if n is None else tmp[:, tmps[0] % 2, 0:n], ACT.Copy).then_inc(hi_done, 1)
                tmps[0] += 1

            def square(src, s, val):
                if s is not None:
                    act.wait_ge(s, val)
                q = sqs[0]
                if q >= 2:
                    act.wait_ge(sq_used, q - 1)
                act.activation(sq[:, q % 2, :], src, ACT.Square).then_inc(sq_ready, 1)
                sqs[0] += 1

            def rsqrt(n):
                act.wait_ge(sq_used, sqs[0])
                act.activation(rs[:, rss[0] % 3, :], ps[:, STAT_BANK, :], ACT.Ln, bias=EPS, scale=1.0 / n).then_inc(stat_free, 1)
                evs[0] += 1
                act.wait_ge(stat_free, evs[0])
                act.activation(rs[:, rss[0] % 3, :], rs[:, rss[0] % 3, :], ACT.Exp, scale=-0.5).then_inc(rs_ready, 1)
                rss[0] += 1

            def exps(a, h, t):
                n = a.n0 + NT * h + t
                b, e = a.spans[t]
                w, c = P * (e - b), n % 4
                act.wait_ge(m_ready, n + 1)
                if a is attn2:
                    g = head_order()[h]
                    act.activation(col[:, 3, c:c + 1], sink[:, g:g + 1], ACT.Exp, bias=col[:, 1, c:c + 1])
                if a in attn3:
                    if n >= 4:
                        act.wait_ge(t_done, n - 3)
                    act.activation(a.p[:, c, 0:w], ps[:, S_BANK + n % 2, 0:w], ACT.Exp, bias=col[:, 1, c:c + 1],
                                   scale=float((B_NOPE + B_ROPE) ** -0.5), accum_out=col[:, 2, c:c + 1]).then_inc(s_free, 1)
                else:
                    act.activation(a.p[:, c, 0:w], a.p[:, c, 0:w], ACT.Exp, bias=col[:, 1, c:c + 1],
                                   accum_out=col[:, 2, c:c + 1]).then_inc(e_done, 1)

            def scale_p(a, h, t):
                n = a.n0 + NT * h + t
                act.wait_ge(r_ready, n - n2 + 1)
                act.activation(a.p[:, n % 4, :], a.p[:, n % 4, :], ACT.Copy, scale=col[:, 4, n % 4:n % 4 + 1]).then_inc(p_ready, 1)

            def turn_hi(a, h, t):
                n = a.n0 + NT * h + t
                b, e = a.spans[t]
                act.wait_ge(t_done, n + 1)
                if t == 0 and h:
                    act.wait_ge(lin_done, a.lin(h - 1) + 1)
                act.activation(a.pt[0][:, b:e, P * t:P * t + P],
                               ps[:, T_BANK + n % 2, P * b:P * e].rearrange("p (s q) -> p s q", q=P), ACT.Copy).then_inc(pt_hi_done, 1)

            def attention(a, outs, steps_=None):
                for h in range(-1, a.heads + 1):
                    for t in range(NT):
                        if h + 1 < a.heads:
                            exps(a, h + 1, t)
                        if t == 0 and h >= 2 and h % 2 == 0:
                            outs(h // 2 - 1)
                        if 0 <= h < a.heads:
                            turn_hi(a, h, t)
                        if a in attn3 and h + 1 < a.heads:
                            scale_p(a, h + 1, t)
                        if steps_ is not None:
                            steps_(h, t)

            def outs_of(bufs):
                return lambda i: hi_of_tmp(bufs[:, i, :])

            for n in range(WEIGHT_LEAD):
                split(n)
            act.wait_ge(consts_in, 48)
            act.activation(c_act[:, KT:2 * KT], v("c", 0, KT), ACT.Sigmoid).then_inc(sig_c, 1)
            for k in range(KT):
                square(x[:, k, :], x_in, 16)
            rsqrt(D)
            for k in range(KT):
                act.wait_ge(tmp_w, tmps[0] + 1)
                act.activation(a_hi[:, k, :], tmp[:, tmps[0] % 2, :], ACT.Identity, bias=mod[:, k:k + 1]).then_inc(hi_done, 1)
                tmps[0] += 1
            for f in range(CT):
                for j in range(2):
                    split(CH["glu"] + 2 * f + j + WEIGHT_LEAD)
                act.wait_ge(lin_done, LT["glu"] + 2 * f + 2)
                if f:
                    act.wait_ge(R["glu"], f)
                act.activation(sig[:, :], ps[:, (LT["glu"] + 2 * f + 1) % LIN, :], ACT.Sigmoid,
                               bias=v("b_in", BI_GB + f)).then_inc(R["glu_sig"], 1)
            for f in range(8):
                split(CH["qk"] + f + WEIGHT_LEAD)
                hi_of_tmp(qk_hi[:, f, :])
            for j in range(4):
                split(CH["v"] + j + WEIGHT_LEAD)
            for t in range(NT):
                act.wait_ge(lin_done, LT["v"] + t + 1)
                act.activation(v_hi[:, t, :], ps[:, (LT["v"] + t) % LIN, :], ACT.Copy).then_inc(hi_done, 1)
            attention(attn1, outs_of(qk_hi))
            for k in range(CT):
                square(c_acc[:, k, :], R["ln_mean"], k + 1)
            rsqrt(D_CONV)
            for k in range(CT):
                act.wait_ge(R["cn"], 2 * k + 1)
                act.activation(gsig[:, k % 2, :], c_acc[:, k, :], ACT.Sigmoid, bias=v("b_ln", k), scale=v("g_ln", k)).then_inc(R["cn_sig"], 1)
                hi_of_tmp(cv_hi[:, k, :])
            for f in range(KT):
                t0, c0 = LT["gates"] + 4 * f, CH["gates"] + 3 * f
                for j, b_at in enumerate((BI_A, BI_B)):
                    split(c0 + j + WEIGHT_LEAD)
                    act.wait_ge(lin_done, t0 + j + 1)
                    if f:
                        act.wait_ge(R["gate_a"], 2 * f - 1 + j)
                    act.activation(gsig[:, j, :], ps[:, (t0 + j) % LIN, :], ACT.Sigmoid, bias=v("b_in", b_at + f)).then_inc(R["gate_sig"], 1)
                split(c0 + 2 + WEIGHT_LEAD)
                hi_of_tmp(y_hi[:, f, :])
            for k in range(KT):
                split(CH["mix"] + k + WEIGHT_LEAD)
                square(y_f[:, k, :], R["y_f"], k + 1)
            rsqrt(D)
            for k in range(KT):
                square(x[:, k, :], R["x_mix"], k + 1)
            rsqrt(D)
            act.wait_ge(gains, 4)
            for k in range(KT):
                act.wait_ge(tmp_w, tmps[0] + 1)
                act.activation(a_hi[:, k, :], tmp[:, tmps[0] % 2, :], ACT.Identity,
                               bias=mod[:, 3 * KT + k:3 * KT + k + 1]).then_inc(hi_done, 1)
                tmps[0] += 1
            act.wait_ge(margins, 2)
            act.sem_inc(R["u_val"], up_free)
            act.sem_inc(R["u_gate"], up_free)
            t0 = tmps[0]
            with act.Fori(0, FT // 2) as i:
                for pair in range(2):
                    for j in range(2):
                        k = 2 * pair + j
                        n = CH["up"] + k + WEIGHT_LEAD
                        act.wait_ge(w_land[n % RAW], i * 32 + 16 * (n // RAW + 1))
                        act.wait_ge(lin_done, i * 4 + (LT["up"] + k))
                        act.activation(w_hi[:, n % SLOTS, :], w_raw[:, n % RAW, :], ACT.Copy).then_inc(w_hi_done, 1)
                    act.wait_ge(tmp_w, i * 2 + (t0 + pair))
                    for j, (c, s, b_at, w_at) in enumerate(((c_val, R["u_val"], 0, 0), (c_gate[:, :], R["u_gate"], FT, FT))):
                        bank = (LT["up"] + 2 * pair + j) % LIN
                        act.wait_ge(lin_done, i * 4 + (LT["up"] + 2 * pair + j + 1))
                        act.activation(c, ps[:, bank, :], ACT.Identity,
                                       bias=vecs[:, bass.ds(i * 2 + (VO["b_dwf"] + b_at + pair), 1)],
                                       scale=vecs[:, bass.ds(i * 2 + (VO["w_dwf"] + 2 * 2 * FT + w_at + pair), 1)])
                        act.activation(u_ff[:, 2 * pair + j, U0:U0 + TOK], ps[:, bank, :], ACT.Copy).then_inc(s, 1)
                    act.wait_ge(R["cf_gate"], i * 4 + (2 * pair + 2))
                    act.activation(gel, c_gate[:, :], ACT.Gelu_apprx_tanh).then_inc(R["gel"], 1)
                    act.wait_ge(tmp_w, i * 2 + (t0 + pair + 1))
                    act.activation(g_hi.rearrange("p k n -> p (k n)")[:, bass.ds(i * (2 * TOK) + pair * TOK, TOK)],
                                   tmp[:, (t0 + pair) % 2, :], ACT.Copy).then_inc(hi_done, 1)
            tmps[0] += FT
            for k in range(3):
                split(CH["down"] + k + WEIGHT_LEAD)
            with act.Fori(0, (FT - 6) // 4) as i:
                for j in range(4):
                    n = CH["down"] + 3 + j + WEIGHT_LEAD
                    act.wait_ge(w_land[n % RAW], i * 32 + 16 * (n // RAW + 1))
                    act.wait_ge(down_step, i * 4 + (3 + j))
                    act.activation(w_hi[:, n % SLOTS, :], w_raw[:, n % RAW, :], ACT.Copy).then_inc(w_hi_done, 1)
            for k in range(3 + (FT - 6) // 4 * 4, FT):
                split(CH["down"] + k + WEIGHT_LEAD)
            for k in range(KT):
                square(y_d[:, KT - 1 - k, :], R["y_d"], k + 1)
            rsqrt(D)

            def scaled_input(hi, gain, k, s, val):
                square(x[:, k, :], s, val)
                act.activation(hi[:, k, :], x[:, k, :], ACT.Identity, scale=v(gain, k)).then_inc(hi_done, 1)

            for k in range(KT):
                scaled_input(a_hi, "norm_a", k, R["x_ffn"], k + 1)
            rsqrt(D)
            for f in range(KT):
                split(CH["a_q"] + f + WEIGHT_LEAD)
                hi_of_tmp(b_hi[:, f, :])
            for f in range(2):
                split(CH["a_k"] + f + WEIGHT_LEAD)
                hi_of_tmp(ka_hi[:, f, :])
            for f in range(KT):
                split(CH["a_z"] + f + WEIGHT_LEAD)
                act.wait_ge(R["z_t"], f + 1)
                if f:
                    act.wait_ge(R["z_a"], f)
                act.activation(zs[:, :], z2[:, f, :], ACT.Sigmoid).then_inc(R["z_sig"], 1)
            for f in range(2):
                split(CH["a_v"] + f + WEIGHT_LEAD)
            evs[0] += 1
            for t in range(NT):
                hi_of_tmp(va_hi[:, t, :], 256)
            act.wait_ge(sink_in, 16)
            attention(attn2, outs_of(b_hi))

            def rest(l, after, nxt):
                i = 0 if l == "a" else 1
                for k in range(KT):
                    split(CH[l + "_out"] + k + WEIGHT_LEAD)
                    scaled_input(after, f"ple_g{i}", k, R["x_attn"], KT * i + k + 1)
                rsqrt(D)
                act.wait_ge(p_in, 16 * (i + 1))
                for k in range(PT_K):
                    act.activation(p_hi[:, k, :], p_raw[:, k, :], ACT.Copy).then_inc(hi_done, 1)
                for k in range(2):
                    split(CH[l + "_ple"] + k + WEIGHT_LEAD)
                for k in range(KT):
                    split(CH[l + "_gate"] + k + WEIGHT_LEAD)
                    act.wait_ge(R["gt"], KT * i + k + 1)
                    act.activation(gs2[:, k % 2, :], gs2[:, k % 2, :], ACT.Sigmoid).then_inc(R["gsig"], 1)
                    if nxt is not None:
                        scaled_input(nxt, "norm_b", k, R["x_ple"], KT * i + k + 1)
                    else:
                        square(x[:, k, :], R["x_ple"], KT * i + k + 1)
                rsqrt(D)

            rest("a", a_hi, b_hi)
            for f in range(QT + KVT):
                split(CH["b_c"] + f + WEIGHT_LEAD)
                square(cq_f[:, f, :], R["cq"], f + 1)
                if f == QT - 1:
                    rsqrt(Q_LORA)
            rsqrt(KV_LORA)
            split(CH["b_c"] + 5 + WEIGHT_LEAD)
            act.wait_ge(R["kr_sum"], 1)
            for b in range(2):
                act.activation(k3_hi[64:96, b, :], kr_f[64:96, :], ACT.Copy).then_inc(hi_done, 1)
            for k in range(QT + KVT):
                hi_of_tmp(cq_hi[:, k, :] if k < QT else ck_hi[:, k - QT, :])
            for f in range(KT):
                split(CH["b_z"] + f + WEIGHT_LEAD)
                act.wait_ge(R["z_tb"], f + 1)
                if f:
                    act.wait_ge(R["z_b"], f)
                act.activation(zs3[:, :], z3[:, f, :], ACT.Sigmoid).then_inc(R["z_sigb"], 1)
            for hf in range(2):
                a = attn3[hf]
                split(CH[f"b_v{hf}"] + WEIGHT_LEAD)
                for t in range(NT):
                    act.wait_ge(lin_done, LT[f"b_v{hf}"] + t + 1)
                    act.activation(vb_hi[:, t, :], ps[:, (LT[f"b_v{hf}"] + t) % LIN, :], ACT.Copy).then_inc(hi_done, 1)

                def key_hi(h):
                    src = ps[64 * (h % 2):64 * (h % 2) + 64, a.k_lin(h - h % 2) % LIN, :]
                    act.wait_ge(lin_done, a.k_lin(h - h % 2) + 1)
                    if h >= 2:
                        act.wait_ge(s_done, a.n0 + NT * (h - 1))
                    if h % 2:
                        act.wait_ge(R["k_b"], 8 * hf + h)
                    act.activation(k3_hi[0:64, h % 2, :], src, ACT.Copy).then_inc(hi_done, 1)

                def query_hi(h):
                    act.wait_ge(R["q_r"], 8 * hf + h + 1)
                    act.activation(q3_hi[0:96, h % 2, :], q3_f[0:96, :], ACT.Copy).then_inc(hi_done, 1)
                    if h % 2:
                        split(CH[f"b_h{hf}"] + h // 2 + WEIGHT_LEAD)

                def steps_of(h, t):
                    if h < 0 or h + 2 >= 8:
                        return
                    if t == 2:
                        if h % 2 == 0:
                            key_hi(h + 2)
                        query_hi(h + 2)
                    if t == 3 and h % 2 == 0:
                        key_hi(h + 3)

                key_hi(0)
                key_hi(1)
                query_hi(0)
                query_hi(1)
                attention(a, lambda i, hf=hf: hi_of_tmp(a_hi[:, 4 * hf + i, :]), steps_of)
            rest("b", b_hi, None)

        @block.vector
        def _(dve):
            tmps, his, lin, steps, taps, units, rss, evs = [0], [0], [0], [0], [0], [0], [0], [0]

            def split(n):
                if n >= N_CHUNKS:
                    return
                dve.wait_ge(w_hi_done, n + 1)
                dve.tensor_tensor(w_lo[:, n % SLOTS, :], w_raw[:, n % RAW, :], w_hi[:, n % SLOTS, :].bitcast(F32),
                                  ALU.subtract).then_inc(w_lo_done, 1)

            def step(ins):
                steps[0] += 1
                ins.then_inc(dve_step, 1)
                dve.wait_ge(dve_step, steps[0])

            def lo(dst, src, hi, ready):
                his[0] += 1
                dve.wait_ge(hi_done, his[0])
                return dve.tensor_tensor(dst, src, hi.bitcast(F32), ALU.subtract).then_inc(ready, 1)

            def tmp_slot():
                tmps[0] += 1
                return tmp[:, (tmps[0] - 1) % 2, :]

            def lo_of_tmp(dst, hi, ready, n=TOK):
                lo(dst, tmp[:, (tmps[0] - 1) % 2, 0:n], hi, ready)

            def bank(tile):
                dve.wait_ge(lin_done, tile + 1)
                return ps[:, tile % LIN, :]

            def wait_rs():
                rss[0] += 1
                dve.wait_ge(rs_ready, rss[0])
                return rs[:, (rss[0] - 1) % 3, :]

            def mod_unit():
                u = units[0]
                units[0] += 1
                slot, turn = (u % 6, u // 6) if u < 16 else (6 + u % 2, (u - 16) // 2)
                src = ada_a[:, u % 6, :] if u < 16 else ada_b[:, u % 2, :]
                acc = acc_a[:, u // 8, :] if u < 16 else acc_b[:, :]
                dve.wait_ge(ada_land[slot], 16 * (turn + 1))
                k = u % 8
                if k == 0:
                    if u >= 24:
                        dve.wait_ge(mod_sum, u // 8)
                    dve.tensor_scalar(acc, src, c_act[:, 0:1], None, ALU.mult).then_inc(ada_used, 1)
                else:
                    dve.wait_ge(ada_used, u)
                    dve.scalar_tensor_tensor(acc, src, c_act[:, k:k + 1], acc, ALU.mult, ALU.add).then_inc(ada_used, 1)

            def mod_group(g):
                grp = (1, 0, *ADA_LATE)[g]
                dve.wait_ge(mod_sum, g + 1)
                dve.tensor_tensor(mod[:, KT * grp:KT * grp + KT], ps[:, MOD_BANK, 0:KT], v("b_ada", KT * grp, KT),
                                  ALU.add).then_inc(mod_ready, 1)

            def gain(i, name, grp, add):
                dve.scalar_tensor_tensor(gvec[:, KT * i:KT * i + KT], mod[:, KT * grp:KT * grp + KT], add, v(name, 0, KT),
                                         ALU.add, ALU.mult).then_inc(gains, 1)

            def conv_taps(n):
                for _ in range(n):
                    i = taps[0]
                    if i == CONV_K * CT:
                        return
                    taps[0] += 1
                    k, f = divmod(i, CT)
                    src, w = u_pad[:, f, k:k + TOK], v("w_dw", k * CT + f)
                    if k == 0:
                        dve.tensor_scalar(c_acc[:, f, :], src, w, v("b_dw", f), ALU.mult, ALU.add).then_inc(conv_step, 1)
                    else:
                        dve.wait_ge(conv_step, i - CT + 1)
                        dve.scalar_tensor_tensor(c_acc[:, f, :], src, w, c_acc[:, f, :], ALU.mult, ALU.add).then_inc(conv_step, 1)

            def maxima(a, h, t):
                n = a.n0 + NT * h + t
                b, e = a.spans[t]
                w, c = P * (e - b), n % 4
                s = ps[:, S_BANK + n % 2, 0:w]
                dve.wait_ge(s_done, n + 1)
                if a in attn3:
                    dve.tensor_reduce(col[:, 0, c:c + 1], s, AX.X, ALU.max, negate=True).then_inc(e_done, 1)
                    dve.wait_ge(e_done, n + 1)
                    dve.tensor_scalar(col[:, 1, c:c + 1], col[:, 0, c:c + 1], float((B_NOPE + B_ROPE) ** -0.5), None,
                                      ALU.mult).then_inc(m_ready, 1)
                    return
                if n >= 4:
                    dve.wait_ge(t_done, n - 3)
                if a is attn1:
                    if t == 0:
                        dve.wait_ge(rel_ready, h + 1)
                    bias, least = rel[:, h % 2, TOK - w:TOK], LOWEST
                else:
                    g = head_order()[h]
                    if t == 0:
                        dve.wait_ge(alibi_in[h % 2], 16 * (h // 2 + 1))
                    off = P * (b - t + 1)
                    bias, least = alibi[:, h % 2, off:off + w], sink[:, g:g + 1]
                dve.tensor_tensor_reduce(a.p[:, c, 0:w], s, bias, 1.0, least, ALU.add, ALU.max, col[:, 0, c:c + 1]).then_inc(s_free, 1)
                dve.wait_ge(s_free, n + 1)
                dve.tensor_scalar(col[:, 1, c:c + 1], col[:, 0, c:c + 1], -1.0, None, ALU.mult).then_inc(m_ready, 1)

            def norms(a, h, t):
                n = a.n0 + NT * h + t
                b, e = a.spans[t]
                w, c = P * (e - b), n % 4
                if a in attn3:
                    dve.wait_ge(s_free, n + 1)
                    dve.reciprocal(col[:, 4, c:c + 1], col[:, 2, c:c + 1]).then_inc(r_ready, 1)
                    return
                dve.wait_ge(e_done, n + 1)
                total = col[:, 2, c:c + 1]
                if a is attn2:
                    step(dve.tensor_tensor(col[:, 5, c:c + 1], total, col[:, 3, c:c + 1], ALU.add))
                    total = col[:, 5, c:c + 1]
                step(dve.reciprocal(col[:, 4, c:c + 1], total))
                dve.tensor_scalar(a.p[:, c, 0:w], a.p[:, c, 0:w], col[:, 4, c:c + 1], None, ALU.mult).then_inc(p_ready, 1)

            def turn_lo(a, h, t):
                n = a.n0 + NT * h + t
                b, e = a.spans[t]
                dve.wait_ge(pt_hi_done, n + 1)
                dve.tensor_tensor(a.pt[1][:, b:e, P * t:P * t + P],
                                  ps[:, T_BANK + n % 2, P * b:P * e].rearrange("p (s q) -> p s q", q=P),
                                  a.pt[0][:, b:e, P * t:P * t + P].bitcast(F32), ALU.subtract).then_inc(pt_ready, 1)

            def attention(a, outs, steps_=None, aside=None):
                for h in range(-1, a.heads + 1):
                    for t in range(NT):
                        if h + 1 < a.heads:
                            maxima(a, h + 1, t)
                        if t == 0 and h >= 1:
                            outs(h - 1)
                        if 0 <= h < a.heads:
                            turn_lo(a, h, t)
                        if h + 1 < a.heads:
                            norms(a, h + 1, t)
                        if steps_ is not None:
                            steps_(h, t)

            def outs_of(a, op, hi, lo_, half_sem, ready, base=0):
                def outs(h):
                    rows = half(h)
                    src = bank(a.lin(h))[rows, :]
                    dst = tmp[rows, tmps[0] % 2, :]
                    m = op(h, rows, dst, src)
                    if h % 2 == 0:
                        m.then_inc(half_sem, 1)
                    else:
                        m.then_inc(tmp_w, 1)
                        tmps[0] += 1
                        lo_of_tmp(lo_[:, base + h // 2, :], hi[:, base + h // 2, :], ready)
                return outs

            for n in range(WEIGHT_LEAD):
                split(n)
            dve.wait_ge(consts_in, 48)
            dve.wait_ge(sig_c, 1)
            step(dve.tensor_tensor(c_act[:, 0:KT], v("c", 0, KT), c_act[:, KT:2 * KT], ALU.mult))
            for u in range(16):
                mod_unit()
            mod_group(0)
            dve.wait_ge(mod_ready, 1)
            gain(0, "g_pre_mix", 1, 1.0)
            mod_group(1)
            r = wait_rs()
            dve.wait_ge(gains, 1)
            dve.wait_ge(mod_ready, 2)

            def modulated(k, r, i, grp, ready):
                slot = tmp_slot()
                dve.scalar_tensor_tensor(slot, x[:, k, :], gvec[:, KT * i + k:KT * i + k + 1], r, ALU.mult, ALU.mult).then_inc(tmp_w, 1)
                his[0] += 1
                dve.wait_ge(hi_done, his[0])
                dve.scalar_tensor_tensor(a_lo[:, k, :], slot, mod[:, KT * grp + k:KT * grp + k + 1], a_hi[:, k, :].bitcast(F32),
                                         ALU.add, ALU.subtract).then_inc(ready, 1)

            for k in range(KT):
                modulated(k, r, 0, 0, R["h1"])
            dve.wait_ge(margins, 1)
            for f in range(CT):
                for j in range(2):
                    split(CH["glu"] + 2 * f + j + WEIGHT_LEAD)
                src = bank(LT["glu"] + 2 * f)
                dve.wait_ge(R["glu_sig"], f + 1)
                dve.scalar_tensor_tensor(u_pad[:, f, PAD:PAD + TOK], src, v("b_in", BI_GA + f), sig[:, :], ALU.add,
                                         ALU.mult).then_inc(R["glu"], 1)
            dve.wait_ge(R["glu"], CT)
            for f in range(8):
                split(CH["qk"] + f + WEIGHT_LEAD)
                src = bank(LT["qk"] + f)
                slot = tmp_slot()
                scale = HD ** -0.5 if f < 4 else 1.0
                dve.tensor_scalar(slot, src, v("b_in", f), scale, ALU.add, ALU.mult).then_inc(tmp_w, 1)
                lo_of_tmp(qk_lo[:, f, :], qk_hi[:, f, :], R["qk"])
                conv_taps(8)
            for j in range(4):
                split(CH["v"] + j + WEIGHT_LEAD)
                if j < 2:
                    conv_taps(6)
            for t in range(NT):
                lo(v_lo[:, t, :], bank(LT["v"] + t), v_hi[:, t, :], R["v"])

            def out1(h, rows, dst, src):
                return dve.tensor_scalar(dst, src, vecs[rows, VO["b_in"] + BI_V + h // 2:VO["b_in"] + BI_V + h // 2 + 1], None, ALU.add)

            attention(attn1, outs_of(attn1, out1, qk_hi, qk_lo, R["o1_half"], R["o1"]),
                      lambda h, t: conv_taps(2) if h < H1 - 1 else None)
            conv_taps(CONV_K * CT)
            dve.wait_ge(R["ln_sum"], 1)
            for k in range(CT):
                m = dve.scalar_tensor_tensor(c_acc[:, k, :], ps[:, STAT_BANK, :], -1.0 / D_CONV, c_acc[:, k, :], ALU.mult, ALU.add)
                m.then_inc(R["ln_mean"], 1)
            r = wait_rs()
            for k in range(CT):
                dve.tensor_tensor(c_acc[:, k, :], c_acc[:, k, :], r, ALU.mult).then_inc(R["cn"], 1)
                dve.wait_ge(R["cn"], 2 * k + 1)
                dve.wait_ge(R["cn_sig"], k + 1)
                dve.tensor_scalar(c_acc[:, k, :], c_acc[:, k, :], v("g_ln", k), v("b_ln", k), ALU.mult, ALU.add).then_inc(R["cn"], 1)
                dve.wait_ge(R["cn"], 2 * k + 2)
                slot = tmp_slot()
                dve.tensor_tensor(slot, c_acc[:, k, :], gsig[:, k % 2, :], ALU.mult).then_inc(tmp_w, 1)
                lo_of_tmp(cv_lo[:, k, :], cv_hi[:, k, :], R["cv"])
            for f in range(KT):
                t0, c0 = LT["gates"] + 4 * f, CH["gates"] + 3 * f
                for j in range(3):
                    split(c0 + j + WEIGHT_LEAD)
                    if j < 2:
                        mod_unit()
                        mod_unit()
                for j in range(2):
                    src = bank(t0 + 2 + j)
                    dve.wait_ge(R["gate_sig"], 2 * f + j + 1)
                    if j == 0:
                        m = dve.tensor_tensor(gprod[:, 0, :], src, gsig[:, 0, :], ALU.mult)
                    else:
                        m = dve.scalar_tensor_tensor(gprod[:, 1, :], src, v("b_conv_o", f), gsig[:, 1, :], ALU.add, ALU.mult)
                    m.then_inc(R["gate_a"], 1)
                slot = tmp_slot()
                dve.wait_ge(R["gate_a"], 2 * f + 2)
                dve.tensor_tensor(slot, gprod[:, 0, :], gprod[:, 1, :], ALU.add).then_inc(tmp_w, 1)
                lo_of_tmp(y_lo[:, f, :], y_hi[:, f, :], R["y"])
                if f % 2 == 1:
                    mod_group(2 + f // 2)
            dve.wait_ge(mod_ready, 6)
            gain(1, "g_post_mix", 2, 0.0)
            gain(2, "g_pre_ffn", 4, 1.0)
            gain(3, "g_post_ffn", 5, 0.0)
            for k in range(KT):
                split(CH["mix"] + k + WEIGHT_LEAD)
                dve.tensor_copy(y_f[:, k, :], bank(LT["mix"] + k)).then_inc(R["y_f"], 1)

            def residual(y, order, i, ready):
                r = wait_rs()
                dve.wait_ge(gains, 4)
                for n, k in enumerate(order):
                    step(dve.scalar_tensor_tensor(y[:, k, :], y[:, k, :], gvec[:, KT * i + k:KT * i + k + 1], r, ALU.mult, ALU.mult))
                    dve.tensor_tensor(x[:, k, :], x[:, k, :], y[:, k, :], ALU.add).then_inc(ready, 1)

            dve.wait_ge(R["y_f"], KT)
            residual(y_f, range(KT), 1, R["x_mix"])
            r = wait_rs()
            for k in range(KT):
                modulated(k, r, 2, 3, R["h2"])
            t0, h0 = tmps[0], his[0]
            with dve.Fori(0, FT // 2) as i:
                for pair in range(2):
                    for j in range(2):
                        n = CH["up"] + 2 * pair + j + WEIGHT_LEAD
                        dve.wait_ge(w_hi_done, i * 4 + (n + 1))
                        dve.tensor_tensor(w_lo[:, n % SLOTS, :], w_raw[:, n % RAW, :], w_hi[:, n % SLOTS, :].bitcast(F32),
                                          ALU.subtract).then_inc(w_lo_done, 1)
                    for tap in (1, 0):
                        for j, (c, s, u_s, w_at) in enumerate(((c_val, R["cf_val"], R["u_val"], 0), (c_gate[:, :], R["cf_gate"], R["u_gate"], FT))):
                            if tap == 1:
                                dve.wait_ge(u_s, i * 2 + (up_free + pair + 1))
                            else:
                                dve.wait_ge(s, i * 4 + (2 * pair + 1))
                            dve.scalar_tensor_tensor(c, u_ff[:, 2 * pair + j, tap:tap + TOK],
                                                     vecs[:, bass.ds(i * 2 + (VO["w_dwf"] + tap * 2 * FT + w_at + pair), 1)],
                                                     c, ALU.mult, ALU.add).then_inc(s, 1)
                    dve.wait_ge(R["gel"], i * 2 + (pair + 1))
                    dve.wait_ge(R["cf_val"], i * 4 + (2 * pair + 2))
                    slot = (t0 + pair) % 2
                    dve.tensor_tensor(tmp[:, slot, :], gel, c_val, ALU.mult).then_inc(tmp_w, 1)
                    dve.wait_ge(hi_done, i * 2 + (h0 + pair + 1))
                    at_k = bass.ds(i * (2 * TOK) + pair * TOK, TOK)
                    dve.tensor_tensor(g_lo.rearrange("p k n -> p (k n)")[:, at_k], tmp[:, slot, :],
                                      g_hi.rearrange("p k n -> p (k n)")[:, at_k].bitcast(F32), ALU.subtract).then_inc(R["g"], 1)
            tmps[0] += FT
            his[0] += FT
            for k in range(3):
                split(CH["down"] + k + WEIGHT_LEAD)
            with dve.Fori(0, (FT - 6) // 4) as i:
                for j in range(4):
                    n = CH["down"] + 3 + j + WEIGHT_LEAD
                    dve.wait_ge(w_hi_done, i * 4 + (n + 1))
                    dve.tensor_tensor(w_lo[:, n % SLOTS, :], w_raw[:, n % RAW, :], w_hi[:, n % SLOTS, :].bitcast(F32),
                                      ALU.subtract).then_inc(w_lo_done, 1)
            for k in range(3 + (FT - 6) // 4 * 4, FT):
                split(CH["down"] + k + WEIGHT_LEAD)
            dve.wait_ge(down_step, FT)
            for k in range(KT):
                dve.tensor_copy(y_d[:, KT - 1 - k, :], ps[:, KT - 1 - k, :]).then_inc(R["y_d"], 1)
            dve.wait_ge(R["y_d"], KT)

            def scaled_lo(lo_, hi, gain_, k, s, val, ready):
                his[0] += 1
                dve.wait_ge(s, val)
                dve.wait_ge(hi_done, his[0])
                dve.scalar_tensor_tensor(lo_[:, k, :], x[:, k, :], v(gain_, k), hi[:, k, :].bitcast(F32), ALU.mult,
                                         ALU.subtract).then_inc(ready, 1)

            residual(y_d, range(KT), 3, R["x_ffn"])
            for k in range(KT):
                scaled_lo(a_lo, a_hi, "norm_a", k, R["x_ffn"], k + 1, R["in_a"])
            r = wait_rs()
            for f in range(KT):
                split(CH["a_q"] + f + WEIGHT_LEAD)
                src = bank(LT["a_q"] + f)
                slot = tmp_slot()
                dve.scalar_tensor_tensor(slot, src, HD ** -0.5, r, ALU.mult, ALU.mult).then_inc(tmp_w, 1)
                lo_of_tmp(b_lo[:, f, :], b_hi[:, f, :], R["q_a"])
            for f in range(2):
                split(CH["a_k"] + f + WEIGHT_LEAD)
                src = bank(LT["a_k"] + f)
                slot = tmp_slot()
                dve.tensor_tensor(slot, src, r, ALU.mult).then_inc(tmp_w, 1)
                lo_of_tmp(ka_lo[:, f, :], ka_hi[:, f, :], R["k_a"])

            def silu_tiles(name, z, sg, t_sem, sig_sem, ready):
                for f in range(KT):
                    split(CH[name] + f + WEIGHT_LEAD)
                    dve.tensor_tensor(z[:, f, :], bank(LT[name] + f), r, ALU.mult).then_inc(t_sem, 1)
                    dve.wait_ge(t_sem, f + 1)
                    dve.wait_ge(sig_sem, f + 1)
                    dve.tensor_tensor(z[:, f, :], z[:, f, :], sg[:, :], ALU.mult).then_inc(ready, 1)

            silu_tiles("a_z", z2, zs, R["z_t"], R["z_sig"], R["z_a"])
            for f in range(2):
                split(CH["a_v"] + f + WEIGHT_LEAD)
            dve.wait_ge(R["rcol_t"], 1)
            dve.tensor_copy(rcol[:, :], ps[:, STAT_BANK, :].rearrange("p (t q) -> p t q", q=P)[:, :, 0]).then_inc(stat_free, 1)
            dve.wait_ge(stat_free, 7)
            for t in range(NT):
                src = bank(LT["a_v"] + t)
                slot = tmp_slot()
                dve.tensor_scalar(slot[:, 0:256], src[:, 0:256], rcol[:, t:t + 1], None, ALU.mult).then_inc(tmp_w, 1)
                lo_of_tmp(va_lo[:, t, :], va_hi[:, t, :], R["v_a"], 256)
            dve.wait_ge(sink_in, 16)
            dve.wait_ge(R["z_a"], KT)

            def gated(z, base=0):
                return lambda h, rows, dst, src: dve.tensor_tensor(dst, src, z[rows, base + h // 2, :], ALU.mult)

            attention(attn2, outs_of(attn2, gated(z2), b_hi, b_lo, R["o2_half"], R["o2"]))

            def rest(l, after, nxt):
                i = 0 if l == "a" else 1
                for k in range(KT):
                    split(CH[l + "_out"] + k + WEIGHT_LEAD)
                    dve.tensor_tensor(x[:, k, :], bank(LT[l + "_out"] + k), x[:, k, :], ALU.add).then_inc(R["x_attn"], 1)
                    scaled_lo(after[1], after[0], f"ple_g{i}", k, R["x_attn"], KT * i + k + 1, R["in_g"])
                for k in range(PT_K):
                    lo(p_lo[:, k, :], p_raw[:, k, :], p_hi[:, k, :], R["p"])
                for k in range(2):
                    split(CH[l + "_ple"] + k + WEIGHT_LEAD)
                for k in range(KT):
                    dve.tensor_copy(pl[:, k, :], bank(LT[l + "_ple"] + k)).then_inc(R["pl"], 1)
                r = wait_rs()
                for k in range(KT):
                    split(CH[l + "_gate"] + k + WEIGHT_LEAD)
                    g = gs2[:, k % 2, :]
                    dve.tensor_tensor(g, bank(LT[l + "_gate"] + k), r, ALU.mult).then_inc(R["gt"], 1)
                    dve.wait_ge(R["gsig"], KT * i + k + 1)
                    dve.wait_ge(R["pl"], KT * i + k + 1)
                    step(dve.tensor_tensor(pl[:, k, :], pl[:, k, :], g, ALU.mult))
                    dve.tensor_tensor(x[:, k, :], x[:, k, :], pl[:, k, :], ALU.add).then_inc(R["x_ple"], 1)
                    if nxt is not None:
                        scaled_lo(nxt[1], nxt[0], "norm_b", k, R["x_ple"], KT * i + k + 1, R["in_b"])

            rest("a", (a_hi, a_lo), (b_hi, b_lo))
            r = wait_rs()
            for f in range(QT + KVT):
                split(CH["b_c"] + f + WEIGHT_LEAD)
                dve.tensor_tensor(cq_f[:, f, :], bank(LT["b_c"] + f), r, ALU.mult).then_inc(R["cq"], 1)
            split(CH["b_c"] + 5 + WEIGHT_LEAD)
            src = bank(LT["b_c"] + 5)
            dve.tensor_tensor(kr_f[64:128, :], src[64:128, :], r[64:128, :], ALU.mult).then_inc(R["kr"], 1)
            dve.wait_ge(R["kr"], 1)
            dve.tensor_tensor(kr_r[64:96, :], kr_f[96:128, :], rope[96:128, :], ALU.mult)
            step(dve.tensor_tensor(kr_f[64:96, :], kr_f[64:96, :], rope[64:96, :], ALU.mult))
            dve.tensor_tensor(kr_f[64:96, :], kr_f[64:96, :], kr_r[64:96, :], ALU.add).then_inc(R["kr_sum"], 1)
            dve.wait_ge(R["kr_sum"], 1)
            for b in range(2):
                lo(k3_lo[64:96, b, :], kr_f[64:96, :], k3_hi[64:96, b, :], R["kr"])
            dve.wait_ge(R["cq"], QT + KVT)
            for part, (n0_, n_, name, hi, lo_) in enumerate(((0, QT, "q_norm", cq_hi, cq_lo), (QT, KVT, "kv_norm", ck_hi, ck_lo))):
                r2 = wait_rs()
                for k in range(n_):
                    slot = tmp_slot()
                    dve.scalar_tensor_tensor(slot, cq_f[:, n0_ + k, :], v(name, k), r2, ALU.mult, ALU.mult).then_inc(tmp_w, 1)
                    lo_of_tmp(lo_[:, k, :], hi[:, k, :], R["cqn"])
            silu_tiles("b_z", z3, zs3, R["z_tb"], R["z_sigb"], R["z_b"])
            for hf in range(2):
                a = attn3[hf]
                split(CH[f"b_v{hf}"] + WEIGHT_LEAD)
                for t in range(NT):
                    lo(vb_lo[:, t, :], bank(LT[f"b_v{hf}"] + t), vb_hi[:, t, :], R["v_b"])

                def key_lo(h):
                    src = bank(a.k_lin(h - h % 2))[64 * (h % 2):64 * (h % 2) + 64, :]
                    lo(k3_lo[0:64, h % 2, :], src, k3_hi[0:64, h % 2, :], R["k_b"])

                def query(h):
                    src = bank(a.q_lin(h))
                    if hf or h:
                        dve.wait_ge(R["q_b"], 8 * hf + h)
                    dve.tensor_tensor(q3_f[0:96, :], src[0:96, :], rope[0:96, :], ALU.mult)
                    dve.tensor_tensor(q3_r[64:96, :], src[96:128, :], rope[96:128, :], ALU.mult).then_inc(R["q_t"], 1)
                    lo(q3_lo[0:96, h % 2, :], q3_f[0:96, :], q3_hi[0:96, h % 2, :], R["q_b"])
                    if h % 2:
                        split(CH[f"b_h{hf}"] + h // 2 + WEIGHT_LEAD)

                def steps_of(h, t):
                    if h < 0 or h + 2 >= 8:
                        return
                    if t == 2:
                        if h % 2 == 0:
                            key_lo(h + 2)
                        query(h + 2)
                    if t == 3 and h % 2 == 0:
                        key_lo(h + 3)

                key_lo(0)
                key_lo(1)
                query(0)
                query(1)
                attention(a, outs_of(a, gated(z3, 4 * hf), a_hi, a_lo, R["o3_half"], R["o3"], 4 * hf), steps_of)
            rest("b", (b_hi, b_lo), None)
            r = wait_rs()
            for k in range(KT):
                dve.scalar_tensor_tensor(x[:, k, :], x[:, k, :], v("final_g", k), r, ALU.mult, ALU.mult).then_inc(R["fin"], 1)


def _feature_tiles(a):
    t = np.ascontiguousarray(a.T)
    return np.ascontiguousarray(t.reshape(-1, P, t.shape[1]).transpose(1, 0, 2))


def _columns(vec):
    return vec.reshape(-1, P).T


def _weight_stream(i):
    chunks = []

    def rows(w):
        return np.asarray(w).reshape(-1, P, w.shape[1])

    def out_tiles(w, group=1):
        r = rows(w)
        kt, n = r.shape[0], r.shape[2] // P
        t = r.reshape(kt, P, n // group, group, P).transpose(2, 1, 3, 0, 4)
        chunks.extend(t.reshape(n // group, P, group * kt * P))

    def row_chunks(w, per):
        r = rows(w)
        chunks.extend(r.reshape(-1, per, P, r.shape[2]).transpose(0, 2, 1, 3).reshape(r.shape[0] // per, P, -1))

    w_in = np.asarray(i["w_in"][0])
    q, k, v, ga, gb, gate_a, gate_b = np.split(w_in, np.cumsum([D_ATTN] * 3 + [D_CONV] * 2 + [D]), axis=1)
    for f in range(CT):
        out_tiles(ga[:, P * f:P * f + P])
        out_tiles(gb[:, P * f:P * f + P])
    out_tiles(q)
    out_tiles(k)
    row_chunks(v, 2)
    for f in range(KT):
        s = slice(P * f, P * f + P)
        out_tiles(gate_a[:, s])
        out_tiles(gate_b[:, s])
        out_tiles(np.concatenate([i["w_attn_o"][0][:, s], i["w_conv_o"][0][:, s]], axis=0))
    out_tiles(i["w_mix_o"][0])
    for f in range(FT):
        out_tiles(i["w_up"][0][:, P * f:P * f + P])
        out_tiles(i["w_up"][0][:, D_FF + P * f:D_FF + P * f + P])
    row_chunks(i["w_down"][0], 1)
    a = np.asarray(i["a_w_in_2"][0])
    q, k, v, z = np.split(a, np.cumsum([D, 256, 256]), axis=1)
    order = head_order()
    out_tiles(q.reshape(D, A_HEADS, HD)[:, order].reshape(D, D))
    out_tiles(k)
    out_tiles(z.reshape(D, A_HEADS, HD)[:, order].reshape(D, D))
    row_chunks(v, 4)
    out_tiles(np.asarray(i["a_w_out_2"][0]).reshape(A_HEADS, HD, D)[order].reshape(D, D))
    out_tiles(i["ple_w_2"][0], 4)
    out_tiles(i["ple_w_gate_2"][0])
    b = np.asarray(i["b_w_in_2"][0])
    cq, ckv, kr, z = np.split(b, np.cumsum([Q_LORA, KV_LORA, B_ROPE]), axis=1)
    swap = np.r_[B_ROPE // 2:B_ROPE, 0:B_ROPE // 2]
    out_tiles(cq)
    out_tiles(ckv)
    out_tiles(np.concatenate([kr, kr[:, swap], kr, kr[:, swap]], axis=1))
    out_tiles(z)
    qb = np.asarray(i["b_w_qb_2"][0]).reshape(Q_LORA, B_HEADS, B_NOPE + B_ROPE)
    qb = np.concatenate([qb, qb[:, :, B_NOPE:][:, :, swap]], axis=2)
    kvb = np.asarray(i["b_w_kvb_2"][0]).reshape(KV_LORA, B_HEADS, B_NOPE + B_V)
    for half in range(2):
        row_chunks(kvb[:, 8 * half:8 * half + 8, B_NOPE:].reshape(KV_LORA, 8 * B_V), 2)
        for h in range(8 * half, 8 * half + 8, 2):
            parts = [rows(qb[:, h]), rows(qb[:, h + 1]), rows(kvb[:, h:h + 2, :B_NOPE].reshape(KV_LORA, P))]
            chunks.append(np.concatenate([p.transpose(1, 0, 2).reshape(P, -1) for p in parts], axis=1))
    out_tiles(i["b_w_out_2"][0])
    out_tiles(i["ple_w_2"][1], 4)
    out_tiles(i["ple_w_gate_2"][1])
    return np.stack(chunks)


def _constants():
    half = B_ROPE // 2
    inv = (np.float32(10000.0) ** (-np.arange(half, dtype=np.float32) / np.float32(half))).astype(np.float32)
    ang = (np.arange(TOK, dtype=np.float32)[:, None] * inv[None, :]).astype(np.float32).T
    rope = np.ones((P, TOK), np.float32)
    rope[64:96] = np.concatenate([np.cos(ang), np.cos(ang)])
    rope[96:128] = np.concatenate([-np.sin(ang), np.sin(ang)])
    slopes = (2.0 ** (-8.0 * np.arange(1, A_HEADS + 1) / A_HEADS)).astype(np.float32)[head_order()]
    dist = np.abs(np.arange(3 * P)[None, :] - P - np.arange(P)[:, None])
    alibi = np.where(dist <= WINDOW, -slopes[:, None, None] * dist.astype(np.float32), np.float32(MASKED)).astype(np.float32)
    return np.eye(P, dtype=np.float32), rope, alibi


def kernel(**inputs):
    import concourse.bacc as _bacc
    from concourse.bass_utils import run_bass_kernel_spmd as _run

    i = {k: np.asarray(a) for k, a in inputs.items()}
    ident, rope, alibi = _constants()
    vec = {
        "c": i["c"][0], "b_ada": i["b_ada"][0], "g_pre_mix": i["g_pre_mix"][0], "g_post_mix": i["g_post_mix"][0],
        "b_in": i["b_in"][0], "w_dw": i["w_dw_conv"][0].reshape(-1), "b_dw": i["b_dw_conv"][0], "g_ln": i["g_conv_ln"][0],
        "b_ln": i["b_conv_ln"][0], "b_conv_o": i["b_conv_o"][0], "g_pre_ffn": i["g_pre_ffn"][0],
        "g_post_ffn": i["g_post_ffn"][0], "w_dwf": i["w_dw_ffn"][0].reshape(-1), "b_dwf": i["b_dw_ffn"][0],
        "norm_a": i["norm_g_2"][0], "norm_b": i["norm_g_2"][1], "q_norm": i["b_q_norm_2"][0], "kv_norm": i["b_kv_norm_2"][0],
        "ple_g0": i["ple_norm_g_2"][0], "ple_g1": i["ple_norm_g_2"][1], "final_g": i["final_norm_g_2"],
    }
    where = np.minimum(TOK - P + np.arange(P)[:, None] - np.arange(TOK)[None, :], MAX_REL) + MAX_REL
    arrays = {
        "in_x": _feature_tiles(i["x"][0]),
        "in_w": _weight_stream(i),
        "in_ada": np.ascontiguousarray(i["w_ada"][0].reshape(KT, P, 6, D).transpose(2, 0, 1, 3)),
        "in_vecs": np.ascontiguousarray(np.concatenate([_columns(vec[n]) for n, _ in VECS], axis=1)),
        "in_ident": ident, "in_rope": rope,
        "in_rel": np.ascontiguousarray(i["rel_bias"][0][:, where]),
        "in_alibi": alibi,
        "in_sink": np.ascontiguousarray(i["a_sink_2"]),
        "in_p": np.stack([_feature_tiles(i["p_2"][l, 0]) for l in range(2)]),
    }
    nc = _bacc.Bacc("TRN2", target_bir_lowering=False, num_devices=1)
    args = [nc.dram_tensor(n, a.shape, mybir.dt.from_np(a.dtype), kind="ExternalInput").ap() for n, a in arrays.items()]
    args.append(nc.dram_tensor("out_0", (P, KT, TOK), F32, kind="ExternalOutput").ap())
    build(nc, *args)
    r = _run(nc, [arrays], core_ids=[0])
    got = np.asarray(r.results[0]["out_0"])
    return np.ascontiguousarray(got.transpose(1, 0, 2).reshape(D, TOK).T).reshape(1, TOK, D)
```

```python
from contextlib import ExitStack

import numpy as np

import concourse.bass as bass
from concourse import mybir

F32 = mybir.dt.float32
F32R = mybir.dt.float32r
ALU = mybir.AluOpType
ACT = mybir.ActivationFunctionType
AX = mybir.AxisListType

P = 128
TOK = 512
D = 1024
KT = D // P
NT = TOK // P
EPS = 1e-6

H1 = 8
HD = 64
D_ATTN = H1 * HD
D_CONV = 512
CONV_K = 31
PAD = CONV_K - 1
CT = D_CONV // P
CHUNK = 64
MAX_REL = 128
D_FF = 2816
FT = D_FF // P
FFN_K = 3
A_HEADS, A_KV, A_GROUP = 16, 4, 4
WINDOW = 128
B_HEADS, B_NOPE, B_ROPE, B_V = 16, 64, 32, 64
Q_LORA, KV_LORA = 384, 256
QT, KVT = Q_LORA // P, KV_LORA // P
PLE = 256
PT_K = PLE // P
MASKED = -1e30
LOWEST = -3e38

CHW = KT * P
RAW = 2
SLOTS = 4
WEIGHT_LEAD = 3
LIN = 4
S_BANK, T_BANK = 4, 6
MOD_BANK, STAT_BANK = 6, 7

STAGES = [("glu", 8), ("qk", 8), ("v", 4), ("gates", 2 * KT), ("ac", KT), ("mix", KT), ("up", 2 * FT), ("down", FT),
          ("a_q", KT), ("a_k", 2), ("a_z", KT), ("a_v", 2), ("a_out", KT), ("a_ple", 2), ("a_gate", KT),
          ("b_c", 6), ("b_z", KT), ("b_v0", 1), ("b_h0", 4), ("b_v1", 1), ("b_h1", 4), ("b_out", KT),
          ("b_ple", 2), ("b_gate", KT)]
CH = {}
N_CHUNKS = 0
for _name, _n in STAGES:
    CH[_name] = N_CHUNKS
    N_CHUNKS += _n

VECS = [("c", KT), ("b_ada", 6 * KT), ("g_pre_mix", KT), ("g_post_mix", KT), ("b_in", 36), ("w_dw", CONV_K * CT),
        ("b_dw", CT), ("g_ln", CT), ("b_ln", CT), ("b_conv_o", KT), ("g_pre_ffn", KT), ("g_post_ffn", KT),
        ("w_dwf", FFN_K * 2 * FT), ("b_dwf", 2 * FT), ("norm_a", KT), ("norm_b", KT), ("q_norm", QT),
        ("kv_norm", KVT), ("ple_g0", KT), ("ple_g1", KT), ("final_g", KT)]
VO = {}
N_VECS = 0
for _name, _n in VECS:
    VO[_name] = N_VECS
    N_VECS += _n
BI_Q, BI_K, BI_V, BI_GA, BI_GB, BI_A, BI_B = 0, 4, 8, 12, 16, 20, 28

ADA_LATE = [2, 4, 3, 5]


def head_order():
    order = []
    for pair in range(A_KV // 2):
        for j in range(A_GROUP):
            order += [2 * pair * A_GROUP + j, (2 * pair + 1) * A_GROUP + j]
    return order


def mla_tiles():
    order = [("k", 0), ("q", 0), ("q", 1)]
    for i in range(NT * 8 + NT):
        h, t = divmod(i, NT)
        if t == 1 and h >= 1:
            order.append(("o", h - 1))
        if t == 2 and h + 2 < 8:
            order.append(("q", h + 2))
        if t == 3 and h % 2 == 0 and h + 2 < 8:
            order.append(("k", h + 2))
    return order


def build(nc, t_x, t_w, t_ada, t_vecs, t_ident, t_rope, t_rope_k, t_rel, t_alibi, t_sink, t_p, out):
    with ExitStack() as ctx:
        base0 = [None]

        def sb(name, shape, dt=F32):
            return ctx.enter_context(nc.sbuf_tensor(name, shape, dt))

        def sem(name):
            return ctx.enter_context(nc.semaphore(name))

        x = sb("x_resid", [P, KT, TOK])
        a_at = -(-nc.sbuf_base // 64) * 64
        sb("a_place", [P, 2 * KT * TOK + 16])
        a_hi = nc.alloc_sbuf_tensor_at("a_hi", [P, KT, TOK], F32R, offset=a_at)
        a_lo = nc.alloc_sbuf_tensor_at("a_lo", [P, KT, TOK], F32R, offset=a_at + 4 * KT * TOK)
        gate_b = nc.alloc_sbuf_tensor_at("gate_b", [P, KT, TOK], F32, offset=a_at)
        w_raw = sb("w_raw", [P, RAW, CHW])
        w_hi, w_lo = sb("w_hi", [P, SLOTS, CHW], F32R), sb("w_lo", [P, SLOTS, CHW], F32R)
        vecs = sb("vecs", [P, N_VECS])
        ident = sb("ident", [P, P])
        ones = sb("ones", [P, P])
        rope = sb("rope", [P, TOK])
        sink = sb("sink", [P, 2, A_HEADS])
        mod = sb("mod", [P, 6 * KT])
        gvec = sb("gvec", [P, 4 * KT])
        c_act = sb("c_act", [P, 2 * KT])
        rs = sb("rs", [P, 3, TOK])
        sq = sb("sq", [P, 2, TOK])
        tmp = sb("tmp", [P, 2, TOK])
        col = sb("col", [P, 5, 4])
        rcol = sb("rcol", [P, NT])
        arena_kib = 100
        slab_at = -(-nc.sbuf_base // 64) * 64
        sb("arena", [P, arena_kib * 256 + 16])

        def at(name, kib, shape, dt=F32):
            size = 4 * int(np.prod(shape[1:]))
            assert kib * 1024 + size <= arena_kib * 1024, name
            return nc.alloc_sbuf_tensor_at(name, shape, dt, offset=slab_at + int(kib * 1024))

        qk_hi, qk_lo = at("qk_hi", 0, [P, 8, TOK], F32R), at("qk_lo", 16, [P, 8, TOK], F32R)
        v_hi, v_lo = at("v_hi", 32, [P, NT, D_ATTN], F32R), at("v_lo", 40, [P, NT, D_ATTN], F32R)
        c_acc = at("c_acc", 48, [P, CT, TOK])
        u_pad = at("u_pad", 56, [P, CT, PAD + TOK])
        rel = at("rel", 65, [P, 2, TOK])
        p1 = at("p1", 69, [P, 4, TOK])
        pt1_hi, pt1_lo = at("pt1_hi", 77, [P, NT, TOK], F32R), at("pt1_lo", 85, [P, NT, TOK], F32R)
        ada_a = at("ada_a", 69, [P, 6, D])
        ada_b = at("ada_b", 92, [P, 2, D])
        acc_a = at("acc_a", 48, [P, 2, D])
        acc_b = at("acc_b", 56, [P, D])
        sig = at("sig", 93, [P, TOK])
        cv_hi, cv_lo = at("cv_hi", 32, [P, CT, TOK], F32R), at("cv_lo", 40, [P, CT, TOK], F32R)
        gate_t = at("gate_t", 77, [P, KT, TOK])
        gprod = at("gprod", 24, [P, 2, TOK])
        y_hi, y_lo = at("y_hi", 60, [P, KT, TOK], F32R), at("y_lo", 76, [P, KT, TOK], F32R)
        y_f = at("y_f", 0, [P, KT, TOK])
        g_hi, g_lo = at("g_hi", 0, [P, FT, TOK], F32R), at("g_lo", 44, [P, FT, TOK], F32R)
        U0 = FFN_K - 1
        u_ff = at("u_ff", 88, [P, 4, U0 + TOK])
        c_gate = at("c_gate", 97, [P, TOK])
        c_val, gel = sq[:, 1, :], sq[:, 0, :]
        y_d = at("y_d", 0, [P, KT, TOK])
        b_hi, b_lo = at("b_hi", 0, [P, KT, TOK], F32R), at("b_lo", 16, [P, KT, TOK], F32R)
        ka_hi, ka_lo = at("ka_hi", 32, [P, 2, TOK], F32R), at("ka_lo", 36, [P, 2, TOK], F32R)
        va_hi, va_lo = at("va_hi", 40, [P, NT, 256], F32R), at("va_lo", 44, [P, NT, 256], F32R)
        z2 = at("z2", 48, [P, KT, TOK])
        p2 = at("p2", 64, [P, 4, 384])
        pt2_hi, pt2_lo = at("pt2_hi", 72, [P, NT, TOK], F32R), at("pt2_lo", 80, [P, NT, TOK], F32R)
        alibi = at("alibi", 88, [P, 2, 384])
        zs = at("zs", 92, [P, TOK])
        pl = at("pl", 32, [P, KT, TOK])
        p_raw = at("p_raw", 88, [P, PT_K, TOK])
        p_hi, p_lo = at("p_hi", 92, [P, PT_K, TOK], F32R), at("p_lo", 96, [P, PT_K, TOK], F32R)
        gs2 = at("gs2", 72, [P, 2, TOK])
        vb_hi, vb_lo = at("vb_hi", 0, [P, NT, TOK], F32R), at("vb_lo", 8, [P, NT, TOK], F32R)
        z3 = at("z3", 32, [P, KT, TOK])
        cq_hi, cq_lo = at("cq_hi", 48, [P, QT, TOK], F32R), at("cq_lo", 54, [P, QT, TOK], F32R)
        ck_hi, ck_lo = at("ck_hi", 60, [P, KVT, TOK], F32R), at("ck_lo", 64, [P, KVT, TOK], F32R)
        cq_f = at("cq_f", 76, [P, QT + KVT, TOK])
        kr_f = at("kr_f", 86, [P, TOK])
        p3 = at("p3", 68, [P, 4, TOK])
        pt3_hi, pt3_lo = at("pt3_hi", 76, [P, NT, TOK], F32R), at("pt3_lo", 84, [P, NT, TOK], F32R)
        q3_hi, q3_lo = at("q3_hi", 16, [P, 2, TOK], F32R), at("q3_lo", 20, [P, 2, TOK], F32R)
        k3_hi, k3_lo = at("k3_hi", 92, [P, 2, TOK], F32R), at("k3_lo", 96, [P, 2, TOK], F32R)
        q3_f = at("q3_f", 24, [P, TOK])
        q3_r = at("q3_r", 26, [P, TOK])
        zs3 = at("zs3", 68, [P, TOK])
        rope_k = at("rope_k", 70, [P, TOK])
        kr_r = at("kr_r", 88, [P, TOK])

        ps = ctx.enter_context(nc.psum_tensor("ps", [P, 8, TOK], F32))

        consts_in, x_in, rel_in, sink_in = sem("consts_in"), sem("x_in"), [sem(f"rel_in{i}") for i in range(2)], sem("sink_in")
        alibi_in, p_in, out_done = [sem(f"alibi_in{i}") for i in range(2)], sem("p_in"), sem("out_done")
        w_land = [sem(f"w_land{i}") for i in range(RAW)]
        w_hi_done, w_lo_done, down_step = sem("w_hi_done"), sem("w_lo_done"), sem("down_step")
        ada_land = [sem(f"ada_land{i}") for i in range(8)]
        ada_used = sem("ada_used")
        sig_c, c_ready, mod_sum, mod_ready, gains = sem("sig_c"), sem("c_ready"), sem("mod_sum"), sem("mod_ready"), sem("gains")
        ones_set, margins = sem("ones_set"), sem("margins")
        sq_ready, sq_used, stat_free, rs_ready = sem("sq_ready"), sem("sq_used"), sem("stat_free"), sem("rs_ready")
        tmp_w, hi_done = sem("tmp_w"), sem("hi_done")
        lin_done = sem("lin_done")
        dve_step, act_step, conv_step = sem("dve_step"), sem("act_step"), sem("conv_step")
        s_done, s_free, m_ready, e_done = sem("s_done"), sem("s_free"), sem("m_ready"), sem("e_done")
        v_half, r_ready, p_ready, t_done, pt_hi_done, pt_ready = sem("v_half"), sem("r_ready"), sem("p_ready"), sem("t_done"), sem("pt_hi_done"), sem("pt_ready")
        rel_ready = sem("rel_ready")
        h_ready = {n: sem("ready_" + n) for n in (
            "h1", "glu_sig", "glu", "conv", "cs", "sinks", "xl", "rope_k", "qk", "v", "o1_half", "o1", "ln_mean", "cv", "gate_sig", "gate_a", "y", "y_f", "x_mix", "h2",
            "u_val", "u_gate", "cf_val", "cf_gate", "gel", "g", "down", "y_d", "x_ffn",
            "in_a", "q_a", "k_a", "z_t", "z_sig", "z_a", "rcol", "v_a", "o2_half", "o2", "x_attn", "in_g", "p", "pl", "gt", "gsig", "x_ple",
            "in_b", "cq", "kr", "kr_sum", "cqn", "ln_sum", "cn", "cn_sig", "rcol_t", "z_tb", "z_sigb", "z_b", "v_b", "q_t", "q_r", "q_b", "k_b", "o3_half", "o3", "fin")}
        R = h_ready
        v_step = sem("v_step")

        def v(name, i=0, n=1):
            return vecs[:, VO[name] + i:VO[name] + i + n]

        evicted = []

        def plan(n, s, start=0, per=1):
            first = len(evicted)
            evicted.extend((s, start + per * (j + 1)) for j in range(n))
            return first

        LT = {}
        first = len(evicted)
        for f in range(CT):
            evicted.append((R["glu"], f + 1))
            evicted.append((R["glu_sig"], f + 1))
        LT["glu"] = first
        LT["qk"] = plan(8, R["qk"])
        LT["v"] = plan(NT, R["v"])
        LT["gates"] = plan(2 * KT, R["gate_sig"])
        LT["o1"] = len(evicted)
        for i in range(H1 // 2):
            evicted += [(R["o1_half"], i + 1), (R["o1"], i + 1)]
        LT["ac"] = plan(2 * KT, R["gate_a"])
        LT["mix"] = plan(KT, R["y_f"])
        up_free = 2
        LT["up"] = len(evicted)
        for i in range(FT):
            evicted += [(R["u_val"], up_free + i + 1), (R["u_gate"], up_free + i + 1)]
        n_up = len(evicted)
        LT["a_q"] = plan(KT, R["q_a"])
        LT["a_k"] = plan(2, R["k_a"])
        LT["a_z"] = plan(KT, R["z_t"])
        LT["a_v"] = plan(NT, R["v_a"])
        LT["o2"] = len(evicted)
        for i in range(A_HEADS // 2):
            evicted += [(R["o2_half"], i + 1), (R["o2"], i + 1)]
        for l, s in (("a", 0), ("b", KT)):
            if l == "b":
                LT["b_c"] = len(evicted)
                evicted += [(R["cq"], j + 1) for j in range(QT + KVT)] + [(R["kr"], 1)]
                LT["b_z"] = plan(KT, R["z_tb"])
                for half in range(2):
                    LT[f"b_v{half}"] = plan(NT, R["v_b"], NT * half)
                    for kind, h in mla_tiles():
                        g = 8 * half + h
                        if h == 0 and kind == "k":
                            LT[f"b_h{half}"] = len(evicted)
                        evicted.append({"k": (R["k_b"], g + 2), "q": (R["q_t"], g + 1),
                                        "o": (R["o3_half"], g // 2 + 1) if h % 2 == 0 else (R["o3"], g // 2 + 1)}[kind])
            LT[l + "_out"] = plan(KT, R["x_attn"], s)
            LT[l + "_ple"] = plan(KT, R["pl"], s)
            LT[l + "_gate"] = plan(KT, R["gt"], s)

        class Attn:
            def __init__(self, heads, n0, rows, q, k, vv, pbuf, pt, spans, lin, over_keys):
                self.heads, self.n0, self.rows, self.q, self.k, self.v = heads, n0, rows, q, k, vv
                self.p, self.pt, self.spans, self.lin, self.over_keys = pbuf, pt, spans, lin, over_keys

        def half(h):
            return slice(64 * (h % 2), 64 * (h % 2) + 64)

        causal = [(0, t + 1) for t in range(NT)]
        band = [(max(t - 1, 0), min(t + 2, NT)) for t in range(NT)]
        full = [(0, NT)] * NT
        n1 = NT * H1
        n2 = n1 + NT * A_HEADS
        attn1 = Attn(H1, 0, half, lambda h: (qk_hi[half(h), h // 2, :], qk_lo[half(h), h // 2, :]),
                     lambda h: (qk_hi[half(h), 4 + h // 2, :], qk_lo[half(h), 4 + h // 2, :]),
                     lambda h, s: (v_hi[:, s, P * (h // 2):P * (h // 2) + P], v_lo[:, s, P * (h // 2):P * (h // 2) + P]),
                     p1, (pt1_hi, pt1_lo), causal, lambda h: LT["o1"] + h, [[(0, 0, 2), (1, 1, 2)], [(0, 2, 4), (1, 2, 4), (2, 2, 4), (3, 3, 4)]])
        attn2 = Attn(A_HEADS, n1, half, lambda h: (b_hi[half(h), h // 2, :], b_lo[half(h), h // 2, :]),
                     lambda h: (ka_hi[half(h), h // 8, :], ka_lo[half(h), h // 8, :]),
                     lambda h, s: (va_hi[:, s, P * (h // 8):P * (h // 8) + P], va_lo[:, s, P * (h // 8):P * (h // 8) + P]),
                     p2, (pt2_hi, pt2_lo), band, lambda h: LT["o2"] + h, [[(0, 0, 2), (1, 0, 2), (2, 1, 2)], [(2, 2, 4), (3, 2, 4), (1, 2, 3)]])

        def mla(hf):
            order = mla_tiles()
            place = {kh: i for i, kh in enumerate(order)}
            a = Attn(8, n2 + 8 * NT * hf, half, lambda h: (q3_hi[0:96, h % 2, :], q3_lo[0:96, h % 2, :]),
                     lambda h: (k3_hi[0:96, h % 2, :], k3_lo[0:96, h % 2, :]),
                     lambda h, s: (vb_hi[:, s, P * (h // 2):P * (h // 2) + P], vb_lo[:, s, P * (h // 2):P * (h // 2) + P]),
                     p3, (pt3_hi, pt3_lo), full, lambda h: LT[f"b_h{hf}"] + place[("o", h)], [[(s, 0, 2) for s in range(4)], [(s, 2, 4) for s in range(4)]])
            a.q_lin = lambda h: LT[f"b_h{hf}"] + place[("q", h)]
            a.k_lin = lambda h: LT[f"b_h{hf}"] + place[("k", h)]
            a.hf = hf
            return a

        attn3 = [mla(0), mla(1)]

        used_at = {}

        def chunks_of(name, tiles, per=1, first=None):
            t0 = LT[name] if first is None else first
            for j in range(dict(STAGES)[name]):
                used_at[CH[name] + j] = (lin_done, t0 + tiles * (j + 1) // per)

        for name in ("glu", "qk", "gates", "mix", "up", "a_q", "a_k", "a_z", "a_out", "a_gate", "b_c", "b_z", "b_out", "b_gate"):
            chunks_of(name, 1)
        for j in range(3):
            used_at[CH["v"] + j] = (v_step, j + 1)
        used_at[CH["v"] + 3] = (lin_done, LT["v"] + NT)
        chunks_of("ac", 2)
        for j in range(FT):
            used_at[CH["down"] + j] = (down_step, j + 1)
        used_at[CH["a_v"]] = (v_step, 4)
        used_at[CH["a_v"] + 1] = (lin_done, LT["a_v"] + NT)
        for l in "ab":
            chunks_of(l + "_ple", KT // 2)
        for hf in range(2):
            used_at[CH[f"b_v{hf}"]] = (lin_done, LT[f"b_v{hf}"] + NT)
            for pair in range(4):
                used_at[CH[f"b_h{hf}"] + pair] = (lin_done, attn3[hf].q_lin(2 * pair + 1) + 1)

        block = ctx.enter_context(nc.Block())

        @block.sync
        def _(sp):
            for n in range(RAW):
                sp.dma_start(w_raw[:, n, :], t_w[n]).then_inc(w_land[n], 16)
            turns = (N_CHUNKS - RAW) // RAW
            with sp.Fori(0, turns) as i:
                for j in range(RAW):
                    sp.wait_ge(w_lo_done, i * RAW + (j + 1))
                    sp.dma_start(w_raw[:, j, :], t_w[bass.ds(i * RAW + (RAW + j), 1)].rearrange("o p n -> (o p) n")
                                 ).then_inc(w_land[j], 16)
            for n in range(RAW + turns * RAW, N_CHUNKS):
                sp.wait_ge(w_lo_done, n - RAW + 1)
                sp.dma_start(w_raw[:, n % RAW, :], t_w[n]).then_inc(w_land[n % RAW], 16)
            for k in range(KT):
                sp.wait_ge(R["fin"], k + 1)
                sp.dma_start(out[:, k, :], x[:, k, :]).then_inc(out_done, 16)
            sp.wait_ge(out_done, 16 * KT)

        @block.gpsimd
        def _(pool):
            pool.dma_start(vecs[:, :], t_vecs).then_inc(consts_in, 16)
            pool.dma_start(x[:, :, :], t_x).then_inc(x_in, 16)
            pool.dma_start(ident[:, :], t_ident).then_inc(consts_in, 16)
            pool.dma_start(rope[:, :], t_rope).then_inc(consts_in, 16)
            pool.memset(ones[:, :], 1.0).then_inc(ones_set, 1)
            for u in range(16):
                if u >= 6:
                    pool.wait_ge(ada_used, u - 5)
                pool.dma_start(ada_a[:, u % 6, :], t_ada[(1, 0)[u // 8], u % 8]).then_inc(ada_land[u % 6], 16)
            pool.dma_start(sink[:, 0, :], t_sink.to_broadcast([P, A_HEADS])).then_inc(sink_in, 16)

            pool.wait_ge(mod_ready, 2)
            pool.memset(u_pad[:, :, 0:PAD], 0.0).then_inc(margins, 1)
            for h in range(H1):
                if h == 0:
                    pool.wait_ge(R["qk"], 8)
                if h >= 2:
                    pool.wait_ge(m_ready, NT * (h - 1))
                pool.dma_start(rel[:, h % 2, :], t_rel[h]).then_inc(rel_in[h % 2], 16)
                pool.wait_ge(rel_in[h % 2], 16 * (h // 2 + 1))
                pool.memset(rel[0:CHUNK, h % 2, TOK - CHUNK:TOK], MASKED).then_inc(rel_ready, 1)
            for u in range(32):
                if u < 2:
                    pool.wait_ge(lin_done, LT["o1"] + H1)
                else:
                    pool.wait_ge(ada_used, 16 + u - 1)
                pool.dma_start(ada_b[:, u % 2, :], t_ada[ADA_LATE[u // 8], u % 8]).then_inc(ada_land[6 + u % 2], 16)
            pool.wait_ge(R["y"], KT)
            pool.dma_start(x[:, :, :], t_x).then_inc(x_in, 16)
            pool.wait_ge(ada_used, 48)
            pool.wait_ge(R["y_f"], KT)
            pool.memset(u_ff[:, :, 0:U0], 0.0).then_inc(margins, 1)
            for layer in range(2):
                if layer == 0:
                    pool.wait_ge(R["x_ffn"], KT)
                    pool.dma_start(rope_k[:, :], t_rope_k).then_inc(R["rope_k"], 16)
                    for h in range(A_HEADS):
                        if h >= 2:
                            pool.wait_ge(m_ready, attn2.n0 + NT * (h - 1))
                        pool.dma_start(alibi[:, h % 2, :], t_alibi[h]).then_inc(alibi_in[h % 2], 16)
                else:
                    for g in range(16):
                        pool.wait_ge(R["q_t"], g + 1)
                        pool.tensor_tensor(q3_f[64:96, :], q3_f[64:96, :], q3_r[64:96, :], ALU.add).then_inc(R["q_r"], 1)
                pool.wait_ge((R["o2"], R["o3"])[layer], 8)
                pool.dma_start(p_raw[:, :, :], t_p[layer]).then_inc(p_in, 16)

        @block.tensor
        def _(pe):
            events, squares = [0], [0]

            def mm3(o, w, r, start, stop, skip=False):
                pe.matmul(o, w[0], r[0], start=start, stop=False, skip_group_check=skip)
                pe.matmul(o, w[0], r[1], start=False, stop=False, skip_group_check=skip)
                return pe.matmul(o, w[1], r[0], start=False, stop=stop, skip_group_check=skip)

            def weights(n):
                pe.wait_ge(w_lo_done, n + 1)
                return w_hi[:, n % SLOTS, :], w_lo[:, n % SLOTS, :]

            def free_bank(tile):
                if tile >= LIN:
                    s, val = (R["y_d"], KT) if n_up <= tile < n_up + LIN else evicted[tile - LIN]
                    pe.wait_ge(s, val)
                return ps[:, tile % LIN, :]

            def cols(w, at, width=P):
                return tuple(part[:, at:at + width] for part in w)

            def tiles(name, n, src, ready=None, base=0, kt=KT, per=1, between=None):
                for f in range(n):
                    o = free_bank(LT[name] + f)
                    w = weights(CH[name] + f // per)
                    for k in range(kt):
                        if ready is not None:
                            pe.wait_ge(ready, base + k + 1)
                        m = mm3(o, cols(w, P * (f % per * kt + k)), (src[0][:, k, :], src[1][:, k, :]), k == 0, k == kt - 1)
                    m.then_inc(lin_done, 1)
                    if between is not None:
                        between(f)

            def token_tiles(tile, chunk, n_chunks, src, width, kt, base_step, skip=False):
                banks = [free_bank(tile + t) for t in range(NT)]
                per = kt // n_chunks
                for j in range(n_chunks):
                    w = weights(chunk + j)
                    for kk in range(per):
                        k = j * per + kk
                        for t in range(NT):
                            m = mm3(banks[t][:, 0:width], (src[0][:, k, P * t:P * t + P], src[1][:, k, P * t:P * t + P]),
                                    cols(w, kk * width, width), k == 0, k == kt - 1)
                            if k == kt - 1:
                                m.then_inc(lin_done, 1)
                            elif kk == per - 1 and t == NT - 1:
                                m.then_inc(v_step, 1)

            def begin_event():
                if events[0]:
                    pe.wait_ge(stat_free, events[0])
                events[0] += 1

            def square_sum(k, n):
                if k == 0:
                    begin_event()
                q = squares[0]
                pe.wait_ge(sq_ready, q + 1)
                pe.matmul(ps[:, STAT_BANK, :], ones[:, :], sq[:, q % 2, :], start=(k == 0), stop=(k == n - 1)).then_inc(sq_used, 1)
                squares[0] += 1

            def behind(f):
                if f:
                    square_sum(f - 1, KT)

            def mod_group(g, acc):
                pe.wait_ge(ada_used, 8 * (g + 1))
                if g:
                    pe.wait_ge(mod_ready, g)
                for j in range(KT):
                    m = pe.matmul(ps[:, MOD_BANK, j:j + 1], acc[:, P * j:P * j + P], ones[:, 0:1], start=True, stop=True)
                m.then_inc(mod_sum, 1)

            def scores(a, h, t):
                n = a.n0 + NT * h + t
                if n >= n2 + 2:
                    pe.wait_ge(s_free, n - n2 - 1)
                elif n >= 2:
                    pe.wait_ge(m_ready, n - 1)
                b, e = a.spans[t]
                q, k = a.q(h), a.k(h)
                mm3(ps[:, S_BANK + n % 2, 0:P * (e - b)], cols(q, P * t), cols(k, P * b, P * (e - b)), True, True).then_inc(s_done, 1)

            def turn(a, h, t):
                n = a.n0 + NT * h + t
                pe.wait_ge(p_ready, n + 1)
                if n >= 2:
                    pe.wait_ge(pt_ready, n - 1)
                b, e = a.spans[t]
                for s in range(b, e):
                    m = pe.transpose(ps[:, T_BANK + n % 2, P * s:P * s + P], a.p[:, n % 4, P * (s - b):P * (s - b) + P], ident[:, :])
                m.then_inc(t_done, 1)

            def values(a, h, part):
                pe.wait_ge(pt_ready, a.n0 + NT * h + 2 * (part + 1))
                o = free_bank(a.lin(h)) if part == 0 else ps[:, a.lin(h) % LIN, :]
                keys = a.over_keys[part]
                for i, (s, t0, t1) in enumerate(keys):
                    r = tuple(pt[:, s, P * t0:P * t1] for pt in a.pt)
                    m = mm3(o[:, P * t0:P * t1], a.v(h, s), r, i == 0, i == len(keys) - 1, skip=True)
                m.then_inc((v_half, lin_done)[part], 1)

            def attention(a, before=None, after=None):
                pe.wait_ge(stat_free, events[0])
                for i in range(NT * a.heads + NT):
                    h, t = divmod(i, NT)
                    if h < a.heads:
                        if t == 0 and before is not None:
                            before(h)
                        scores(a, h, t)
                    if 0 <= i - 3 < NT * a.heads:
                        turn(a, *divmod(i - 3, NT))
                    if t == 1 and h >= 1:
                        values(a, h - 1, 0)
                    if t == 3 and h >= 1:
                        values(a, h - 1, 1)
                    if after is not None:
                        after(h, t)

            A, B = (a_hi, a_lo), (b_hi, b_lo)

            pe.wait_ge(ones_set, 1)
            for k in range(KT):
                square_sum(k, KT)
            mod_group(0, acc_a[:, 0, :])
            mod_group(1, acc_a[:, 1, :])
            tiles("glu", 8, A, R["h1"])
            tiles("qk", 8, A)
            token_tiles(LT["v"], CH["v"], 4, A, D_ATTN, KT, 0)
            pe.wait_ge(R["qk"], 8)
            pe.wait_ge(R["v"], NT)

            def conv_norm(f):
                if f == 9:
                    pe.wait_ge(conv_step, CONV_K * CT)
                    pe.wait_ge(stat_free, events[0])
                    for k in range(CT):
                        m = pe.matmul(ps[:, STAT_BANK, :], ones[:, :], c_acc[:, k, :], start=(k == 0), stop=(k == CT - 1))
                    m.then_inc(R["ln_sum"], 1)
                if f == 11:
                    pe.wait_ge(R["ln_mean"], CT)
                    for k in range(CT):
                        square_sum(k, CT)

            tiles("gates", 2 * KT, A, between=conv_norm)
            pe.wait_ge(R["qk"], 8)
            pe.wait_ge(R["v"], NT)
            attention(attn1)
            pe.wait_ge(pt_ready, n1)
            pe.wait_ge(R["o1"], H1 // 2)
            for f in range(KT):
                w = weights(CH["ac"] + f)
                for j, src in enumerate(((qk_hi, qk_lo), (cv_hi, cv_lo))):
                    o = free_bank(LT["ac"] + 2 * f + j)
                    for k in range(CT):
                        if j:
                            pe.wait_ge(R["cv"], k + 1)
                        m = mm3(o, cols(w, P * (CT * j + k)), (src[0][:, k, :], src[1][:, k, :]), k == 0, k == CT - 1)
                    m.then_inc(lin_done, 1)
                if f % 4 == 3:
                    mod_group(2 + f // 4, acc_b)

            def behind_mix(f):
                behind(f)
                if f % 4 == 3:
                    mod_group(4 + f // 4, acc_b)

            tiles("mix", KT, (y_hi, y_lo), R["y"], between=behind_mix)
            square_sum(KT - 1, KT)
            for k in range(KT):
                square_sum(k, KT)
            with pe.Fori(0, FT // 2) as i:
                for j in range(4):
                    tile, n = LT["up"] + j, CH["up"] + j
                    pe.wait_ge(w_lo_done, i * 4 + (n + 1))
                    pe.wait_ge((R["u_val"], R["u_gate"])[j % 2], i * 2 + (up_free + j // 2 - 1))
                    w = w_hi[:, n % SLOTS, :], w_lo[:, n % SLOTS, :]
                    for k in range(KT):
                        if j == 0:
                            pe.wait_ge(R["h2"], k + 1)
                        m = mm3(ps[:, tile % LIN, :], cols(w, P * k), (a_hi[:, k, :], a_lo[:, k, :]), k == 0, k == KT - 1)
                    m.then_inc(lin_done, 1)
            pe.wait_ge(R["u_val"], up_free + FT)
            pe.wait_ge(R["u_gate"], up_free + FT)

            def down(k, n, slot, start, stop, ready):
                pe.wait_ge(w_lo_done, n)
                pe.wait_ge(R["g"], ready)
                w = w_hi[:, slot, :], w_lo[:, slot, :]
                r = (g_hi[:, k, :], g_lo[:, k, :]) if isinstance(k, int) else tuple(
                    g.rearrange("p k n -> p (k n)")[:, bass.ds(k, TOK)] for g in (g_hi, g_lo))
                for f in range(KT):
                    m = mm3(ps[:, f, :], cols(w, P * f), r, start, stop)
                m.then_inc(down_step, 1)

            for k in range(2):
                down(k, CH["down"] + k + 1, (CH["down"] + k) % SLOTS, k == 0, False, k + 1)
            turns = (FT - 2) // 4
            with pe.Fori(0, turns - 1) as i:
                for j in range(4):
                    n = CH["down"] + 2 + j
                    down(i * (4 * TOK) + (2 + j) * TOK, i * 4 + (n + 1), n % SLOTS, False, False, i * 4 + (3 + j))
            for k in range(FT - 4, FT):
                down(k, CH["down"] + k + 1, (CH["down"] + k) % SLOTS, False, k == FT - 1, k + 1)
            for k in range(KT):
                if k == 0:
                    pe.wait_ge(R["y_d"], 1)
                square_sum(k, KT)
            pe.wait_ge(R["y_d"], KT)
            for k in range(KT):
                square_sum(k, KT)

            tiles("a_q", KT, A, R["in_a"])
            tiles("a_k", 2, A)
            tiles("a_z", KT, A)
            pe.wait_ge(rs_ready, 6)
            begin_event()
            for t in range(NT):
                m = pe.transpose(ps[:, STAT_BANK, P * t:P * t + P], rs[:, 5 % 3, P * t:P * t + P], ident[:, :])
            m.then_inc(R["rcol_t"], 1)
            token_tiles(LT["a_v"], CH["a_v"], 2, A, 256, KT, 3)
            pe.wait_ge(R["q_a"], KT)
            pe.wait_ge(R["k_a"], 2)
            pe.wait_ge(R["v_a"], NT)
            attention(attn2)

            def rest(l, src, after, o_ready):
                pe.wait_ge(pt_ready, n2 if l == "a" else n2 + 16 * NT)
                pe.wait_ge(o_ready, 8)
                tiles(l + "_out", KT, src, between=behind)
                square_sum(KT - 1, KT)
                base = 0 if l == "a" else PT_K
                tiles(l + "_ple", KT, (p_hi, p_lo), R["p"], base, kt=PT_K, per=4)
                tiles(l + "_gate", KT, after, R["in_g"], 0 if l == "a" else KT, between=behind)
                square_sum(KT - 1, KT)

            rest("a", B, A, R["o2"])

            tiles("b_c", 6, B, R["in_b"])
            for k in range(QT):
                square_sum(k, QT)
            for k in range(KVT):
                square_sum(k, KVT)
            tiles("b_z", KT, B)
            pe.wait_ge(R["cqn"], QT + KVT)
            pe.wait_ge(R["kr"], 3)
            for hf in range(2):
                a = attn3[hf]
                token_tiles(LT[f"b_v{hf}"], CH[f"b_v{hf}"], 1, (ck_hi, ck_lo), TOK, KVT, 0)

                def queries(h):
                    w = weights(CH[f"b_h{hf}"] + h // 2)
                    o = free_bank(a.q_lin(h))
                    for k in range(QT):
                        m = mm3(o, cols(w, P * (h % 2 * QT + k)), (cq_hi[:, k, :], cq_lo[:, k, :]), k == 0, k == QT - 1)
                    m.then_inc(lin_done, 1)

                def keys(h):
                    w = weights(CH[f"b_h{hf}"] + h // 2)
                    o = free_bank(a.k_lin(h))
                    for k in range(KVT):
                        m = mm3(o, cols(w, P * (2 * QT + k)), (ck_hi[:, k, :], ck_lo[:, k, :]), k == 0, k == KVT - 1)
                    m.then_inc(lin_done, 1)

                def before(h):
                    pe.wait_ge(R["q_b"], 8 * hf + h + 1)
                    pe.wait_ge(R["k_b"], 8 * hf + h + 1)
                    if h == 0:
                        pe.wait_ge(R["v_b"], NT * (hf + 1))

                def after(h, t):
                    if t == 2 and h + 2 < a.heads:
                        queries(h + 2)
                    if t == 3 and h % 2 == 0 and h + 2 < a.heads:
                        keys(h + 2)

                keys(0)
                queries(0)
                queries(1)
                attention(a, before, after)
            rest("b", A, B, R["o3"])

        @block.scalar
        def _(act):
            tmps, his, sqs, rss, steps, evs = [0], [0], [0], [0], [0], [0]

            def split(n):
                if n >= N_CHUNKS:
                    return
                act.wait_ge(w_land[n % RAW], 16 * (n // RAW + 1))
                if n >= SLOTS:
                    act.wait_ge(*used_at[n - SLOTS])
                act.activation(w_hi[:, n % SLOTS, :], w_raw[:, n % RAW, :], ACT.Copy).then_inc(w_hi_done, 1)

            def hi_of_tmp(dst, n=None):
                act.wait_ge(tmp_w, tmps[0] + 1)
                act.activation(dst, tmp[:, tmps[0] % 2, :] if n is None else tmp[:, tmps[0] % 2, 0:n], ACT.Copy).then_inc(hi_done, 1)
                tmps[0] += 1

            def square(src, s, val):
                if s is not None:
                    act.wait_ge(s, val)
                q = sqs[0]
                if q >= 2:
                    act.wait_ge(sq_used, q - 1)
                act.activation(sq[:, q % 2, :], src, ACT.Square).then_inc(sq_ready, 1)
                sqs[0] += 1

            def rsqrt(n):
                act.wait_ge(sq_used, sqs[0])
                act.activation(rs[:, rss[0] % 3, :], ps[:, STAT_BANK, :], ACT.Ln, bias=EPS, scale=1.0 / n).then_inc(stat_free, 1)
                evs[0] += 1
                act.wait_ge(stat_free, evs[0])
                act.activation(rs[:, rss[0] % 3, :], rs[:, rss[0] % 3, :], ACT.Exp, scale=-0.5).then_inc(rs_ready, 1)
                rss[0] += 1

            def exps(a, h, t):
                n = a.n0 + NT * h + t
                b, e = a.spans[t]
                w, c = P * (e - b), n % 4
                act.wait_ge(m_ready, n + 1)
                least, total = col[:, 0, c:c + 1], col[:, 1, c:c + 1]
                if a is attn2:
                    g = head_order()[h]
                    act.activation(col[:, 2, c:c + 1], sink[:, 0, g:g + 1], ACT.Exp, bias=least)
                if a in attn3:
                    act.wait_ge(t_done, n - 3)
                    act.activation(a.p[:, c, 0:w], ps[:, S_BANK + n % 2, 0:w], ACT.Exp, bias=least,
                                   accum_out=total).then_inc(s_free, 1)
                else:
                    act.activation(a.p[:, c, 0:w], a.p[:, c, 0:w], ACT.Exp, bias=least, scale=-1.0,
                                   accum_out=total).then_inc(e_done, 1)

            def scale_p(a, n):
                act.wait_ge(r_ready, n - n2 + 1)
                act.activation(a.p[:, n % 4, :], a.p[:, n % 4, :], ACT.Copy, scale=col[:, 4, n % 4:n % 4 + 1]).then_inc(p_ready, 1)

            def turn_hi(a, h, t):
                n = a.n0 + NT * h + t
                b, e = a.spans[t]
                act.wait_ge(t_done, n + 1)
                if t == 0 and h:
                    act.wait_ge(v_half, a.n0 // NT + h)
                if t == 2 and h:
                    act.wait_ge(lin_done, a.lin(h - 1) + 1)
                act.activation(a.pt[0][:, b:e, P * t:P * t + P],
                               ps[:, T_BANK + n % 2, P * b:P * e].rearrange("p (s q) -> p s q", q=P), ACT.Copy).then_inc(pt_hi_done, 1)

            def attention(a, outs, after=None):
                for i in range(NT * a.heads + NT + 2):
                    h, t = divmod(i, NT)
                    if 0 <= i - 3 < NT * a.heads:
                        turn_hi(a, *divmod(i - 3, NT))
                    if h < a.heads:
                        exps(a, h, t)
                    if a in attn3 and 0 <= i - 1 < NT * a.heads:
                        scale_p(a, a.n0 + i - 1)
                    if after is not None:
                        after(h, t)
                    if t == 1 and h >= 3 and h % 2 == 1:
                        outs(h // 2 - 1)

            def outs_of(bufs):
                return lambda i: hi_of_tmp(bufs[:, i, :])

            for n in range(WEIGHT_LEAD):
                split(n)
            act.wait_ge(consts_in, 48)
            act.activation(c_act[:, KT:2 * KT], v("c", 0, KT), ACT.Sigmoid).then_inc(sig_c, 1)
            for k in range(KT):
                square(x[:, k, :], x_in, 16)
            rsqrt(D)
            for k in range(KT):
                act.wait_ge(tmp_w, tmps[0] + 1)
                act.activation(a_hi[:, k, :], tmp[:, tmps[0] % 2, :], ACT.Identity, bias=mod[:, k:k + 1]).then_inc(hi_done, 1)
                tmps[0] += 1
            for f in range(CT):
                for j in range(2):
                    split(CH["glu"] + 2 * f + j + WEIGHT_LEAD)
                act.wait_ge(lin_done, LT["glu"] + 2 * f + 2)
                if f:
                    act.wait_ge(R["glu"], f)
                act.activation(sig[:, :], ps[:, (LT["glu"] + 2 * f + 1) % LIN, :], ACT.Sigmoid,
                               bias=v("b_in", BI_GB + f)).then_inc(R["glu_sig"], 1)
            for f in range(8):
                split(CH["qk"] + f + WEIGHT_LEAD)
                hi_of_tmp(qk_hi[:, f, :])
            for j in range(4):
                split(CH["v"] + j + WEIGHT_LEAD)
            for t in range(NT):
                act.wait_ge(lin_done, LT["v"] + t + 1)
                act.activation(v_hi[:, t, :], ps[:, (LT["v"] + t) % LIN, :], ACT.Copy).then_inc(hi_done, 1)
            for j in range(2 * KT):
                split(CH["gates"] + j + WEIGHT_LEAD)
                act.wait_ge(lin_done, LT["gates"] + j + 1)
                dst = x[:, j, :] if j < KT else gate_t[:, j - KT, :]
                act.activation(dst, ps[:, (LT["gates"] + j) % LIN, :], ACT.Sigmoid,
                               bias=v("b_in", BI_A + j)).then_inc(R["gate_sig"], 1)
                if j == 11:
                    for k in range(CT):
                        square(c_acc[:, k, :], R["ln_mean"], k + 1)
                    rsqrt(D_CONV)
                if j == 13:
                    for k in range(CT):
                        act.wait_ge(R["cn"], k + 1)
                        if k >= 2:
                            act.wait_ge(R["cs"], k - 1)
                        act.activation(sq[:, k % 2, :], c_acc[:, k, :], ACT.Sigmoid, bias=v("b_ln", k),
                                       scale=v("g_ln", k)).then_inc(R["cn_sig"], 1)
            act.wait_ge(R["gate_sig"], 2 * KT)
            for k in range(KT):
                act.activation(gate_b[:, k, :], gate_t[:, k, :], ACT.Copy).then_inc(R["gate_sig"], 1)
            act.wait_ge(R["gate_sig"], 3 * KT)
            attention(attn1, outs_of(qk_hi))
            for k in range(CT):
                act.activation(cv_hi[:, k, :], c_acc[:, k, :], ACT.Copy).then_inc(hi_done, 1)
            for f in range(KT):
                split(CH["ac"] + f + WEIGHT_LEAD)
                hi_of_tmp(y_hi[:, f, :])
            for k in range(KT):
                split(CH["mix"] + k + WEIGHT_LEAD)
                square(y_f[:, k, :], R["y_f"], k + 1)
            rsqrt(D)
            for k in range(KT):
                square(x[:, k, :], R["x_mix"], k + 1)
            rsqrt(D)
            act.wait_ge(gains, 4)
            for k in range(KT):
                act.wait_ge(tmp_w, tmps[0] + 1)
                act.activation(a_hi[:, k, :], tmp[:, tmps[0] % 2, :], ACT.Identity,
                               bias=mod[:, 3 * KT + k:3 * KT + k + 1]).then_inc(hi_done, 1)
                tmps[0] += 1
            act.wait_ge(margins, 2)
            act.sem_inc(R["u_val"], up_free)
            act.sem_inc(R["u_gate"], up_free)
            t0 = tmps[0]
            with act.Fori(0, FT // 2) as i:
                for pair in range(2):
                    for j in range(2):
                        k = 2 * pair + j
                        n = CH["up"] + k + WEIGHT_LEAD
                        act.wait_ge(w_land[n % RAW], i * 32 + 16 * (n // RAW + 1))
                        act.wait_ge(lin_done, i * 4 + (LT["up"] + k))
                        act.activation(w_hi[:, n % SLOTS, :], w_raw[:, n % RAW, :], ACT.Copy).then_inc(w_hi_done, 1)
                    act.wait_ge(tmp_w, i * 2 + (t0 + pair))
                    for j, (c, s, b_at, w_at) in enumerate(((c_val, R["u_val"], 0, 0), (c_gate[:, :], R["u_gate"], FT, FT))):
                        bank = (LT["up"] + 2 * pair + j) % LIN
                        act.wait_ge(lin_done, i * 4 + (LT["up"] + 2 * pair + j + 1))
                        act.activation(c, ps[:, bank, :], ACT.Identity,
                                       bias=vecs[:, bass.ds(i * 2 + (VO["b_dwf"] + b_at + pair), 1)],
                                       scale=vecs[:, bass.ds(i * 2 + (VO["w_dwf"] + 2 * 2 * FT + w_at + pair), 1)])
                        act.activation(u_ff[:, 2 * pair + j, U0:U0 + TOK], ps[:, bank, :], ACT.Copy).then_inc(s, 1)
                    act.wait_ge(R["cf_gate"], i * 4 + (2 * pair + 2))
                    act.activation(gel, c_gate[:, :], ACT.Gelu_apprx_tanh).then_inc(R["gel"], 1)
                    act.wait_ge(tmp_w, i * 2 + (t0 + pair + 1))
                    act.activation(g_hi.rearrange("p k n -> p (k n)")[:, bass.ds(i * (2 * TOK) + pair * TOK, TOK)],
                                   tmp[:, (t0 + pair) % 2, :], ACT.Copy).then_inc(hi_done, 1)
            tmps[0] += FT
            for k in range(3):
                split(CH["down"] + k + WEIGHT_LEAD)
            with act.Fori(0, (FT - 6) // 4) as i:
                for j in range(4):
                    n = CH["down"] + 3 + j + WEIGHT_LEAD
                    act.wait_ge(w_land[n % RAW], i * 32 + 16 * (n // RAW + 1))
                    act.wait_ge(down_step, i * 4 + (3 + j))
                    act.activation(w_hi[:, n % SLOTS, :], w_raw[:, n % RAW, :], ACT.Copy).then_inc(w_hi_done, 1)
            for k in range(3 + (FT - 6) // 4 * 4, FT):
                split(CH["down"] + k + WEIGHT_LEAD)
            for k in range(KT):
                square(y_d[:, KT - 1 - k, :], R["y_d"], k + 1)
            rsqrt(D)

            def scaled_input(hi, gain, k, s, val):
                square(x[:, k, :], s, val)
                act.activation(hi[:, k, :], x[:, k, :], ACT.Identity, scale=v(gain, k)).then_inc(hi_done, 1)

            for k in range(KT):
                scaled_input(a_hi, "norm_a", k, R["x_ffn"], k + 1)
            rsqrt(D)
            for f in range(KT):
                split(CH["a_q"] + f + WEIGHT_LEAD)
                hi_of_tmp(b_hi[:, f, :])
            for f in range(2):
                split(CH["a_k"] + f + WEIGHT_LEAD)
                hi_of_tmp(ka_hi[:, f, :])
            for f in range(KT):
                split(CH["a_z"] + f + WEIGHT_LEAD)
                act.wait_ge(R["z_t"], f + 1)
                if f:
                    act.wait_ge(R["z_a"], f)
                act.activation(zs[:, :], z2[:, f, :], ACT.Sigmoid).then_inc(R["z_sig"], 1)
            for f in range(2):
                split(CH["a_v"] + f + WEIGHT_LEAD)
            evs[0] += 1
            for t in range(NT):
                hi_of_tmp(va_hi[:, t, :], 256)
            act.wait_ge(sink_in, 16)
            attention(attn2, outs_of(b_hi))

            def rest(l, after, nxt):
                i = 0 if l == "a" else 1
                for k in range(KT):
                    split(CH[l + "_out"] + k + WEIGHT_LEAD)
                    scaled_input(after, f"ple_g{i}", k, R["x_attn"], KT * i + k + 1)
                rsqrt(D)
                act.wait_ge(p_in, 16 * (i + 1))
                for k in range(PT_K):
                    act.activation(p_hi[:, k, :], p_raw[:, k, :], ACT.Copy).then_inc(hi_done, 1)
                for k in range(2):
                    split(CH[l + "_ple"] + k + WEIGHT_LEAD)
                for k in range(KT):
                    split(CH[l + "_gate"] + k + WEIGHT_LEAD)
                    act.wait_ge(R["gt"], KT * i + k + 1)
                    act.activation(gs2[:, k % 2, :], gs2[:, k % 2, :], ACT.Sigmoid).then_inc(R["gsig"], 1)
                    if nxt is not None:
                        scaled_input(nxt, "norm_b", k, R["x_ple"], KT * i + k + 1)
                    else:
                        square(x[:, k, :], R["x_ple"], KT * i + k + 1)
                rsqrt(D)

            rest("a", a_hi, b_hi)
            for f in range(QT + KVT):
                split(CH["b_c"] + f + WEIGHT_LEAD)
                square(cq_f[:, f, :], R["cq"], f + 1)
                if f == QT - 1:
                    rsqrt(Q_LORA)
            rsqrt(KV_LORA)
            split(CH["b_c"] + 5 + WEIGHT_LEAD)
            act.wait_ge(R["kr_sum"], 1)
            for b in range(2):
                act.activation(k3_hi[64:96, b, :], kr_f[64:96, :], ACT.Copy).then_inc(hi_done, 1)
            for k in range(QT + KVT):
                hi_of_tmp(cq_hi[:, k, :] if k < QT else ck_hi[:, k - QT, :])
            for f in range(KT):
                split(CH["b_z"] + f + WEIGHT_LEAD)
                act.wait_ge(R["z_tb"], f + 1)
                if f:
                    act.wait_ge(R["z_b"], f)
                act.activation(zs3[:, :], z3[:, f, :], ACT.Sigmoid).then_inc(R["z_sigb"], 1)
            for hf in range(2):
                a = attn3[hf]
                split(CH[f"b_v{hf}"] + WEIGHT_LEAD)
                for t in range(NT):
                    act.wait_ge(lin_done, LT[f"b_v{hf}"] + t + 1)
                    act.activation(vb_hi[:, t, :], ps[:, (LT[f"b_v{hf}"] + t) % LIN, :], ACT.Copy).then_inc(hi_done, 1)

                def key_hi(h):
                    src = ps[64 * (h % 2):64 * (h % 2) + 64, a.k_lin(h - h % 2) % LIN, :]
                    act.wait_ge(lin_done, a.k_lin(h - h % 2) + 1)
                    if h >= 2:
                        act.wait_ge(s_done, a.n0 + NT * (h - 1))
                    if h % 2:
                        act.wait_ge(R["k_b"], 8 * hf + h)
                    act.activation(k3_hi[0:64, h % 2, :], src, ACT.Copy).then_inc(hi_done, 1)

                def query_hi(h):
                    act.wait_ge(R["q_r"], 8 * hf + h + 1)
                    if h >= 2:
                        act.wait_ge(s_done, a.n0 + NT * (h - 1))
                    act.activation(q3_hi[0:96, h % 2, :], q3_f[0:96, :], ACT.Copy).then_inc(hi_done, 1)
                    if h % 2:
                        split(CH[f"b_h{hf}"] + h // 2 + WEIGHT_LEAD)

                def after(h, t):
                    if t == 0 and h % 2 == 1 and h + 1 < 8:
                        key_hi(h + 1)
                    if t == 1 and 1 <= h <= 6:
                        query_hi(h + 1)
                    if t == 0 and h % 2 == 0 and 2 <= h <= 6:
                        key_hi(h + 1)

                key_hi(0)
                key_hi(1)
                query_hi(0)
                query_hi(1)
                attention(a, lambda i, hf=hf: hi_of_tmp(a_hi[:, 4 * hf + i, :]), after)
            rest("b", b_hi, None)

        @block.vector
        def _(dve):
            tmps, his, lin, steps, taps, units, rss, evs = [0], [0], [0], [0], [0], [0], [0], [0]

            def split(n):
                if n >= N_CHUNKS:
                    return
                dve.wait_ge(w_hi_done, n + 1)
                dve.tensor_tensor(w_lo[:, n % SLOTS, :], w_raw[:, n % RAW, :], w_hi[:, n % SLOTS, :].bitcast(F32),
                                  ALU.subtract).then_inc(w_lo_done, 1)

            def step(ins):
                steps[0] += 1
                ins.then_inc(dve_step, 1)
                dve.wait_ge(dve_step, steps[0])

            def lo(dst, src, hi, ready):
                his[0] += 1
                dve.wait_ge(hi_done, his[0])
                return dve.tensor_tensor(dst, src, hi.bitcast(F32), ALU.subtract).then_inc(ready, 1)

            def tmp_slot():
                tmps[0] += 1
                return tmp[:, (tmps[0] - 1) % 2, :]

            def lo_of_tmp(dst, hi, ready, n=TOK):
                lo(dst, tmp[:, (tmps[0] - 1) % 2, 0:n], hi, ready)

            def bank(tile):
                dve.wait_ge(lin_done, tile + 1)
                return ps[:, tile % LIN, :]

            def wait_rs():
                rss[0] += 1
                dve.wait_ge(rs_ready, rss[0])
                return rs[:, (rss[0] - 1) % 3, :]

            def mod_unit():
                u = units[0]
                units[0] += 1
                slot, turn = (u % 6, u // 6) if u < 16 else (6 + u % 2, (u - 16) // 2)
                src = ada_a[:, u % 6, :] if u < 16 else ada_b[:, u % 2, :]
                acc = acc_a[:, u // 8, :] if u < 16 else acc_b[:, :]
                dve.wait_ge(ada_land[slot], 16 * (turn + 1))
                k = u % 8
                if k == 0:
                    if u >= 24:
                        dve.wait_ge(mod_sum, u // 8)
                    dve.tensor_scalar(acc, src, c_act[:, 0:1], None, ALU.mult).then_inc(ada_used, 1)
                else:
                    dve.wait_ge(ada_used, u)
                    dve.scalar_tensor_tensor(acc, src, c_act[:, k:k + 1], acc, ALU.mult, ALU.add).then_inc(ada_used, 1)

            def mod_group(g):
                grp = (1, 0, *ADA_LATE)[g]
                dve.wait_ge(mod_sum, g + 1)
                dve.tensor_tensor(mod[:, KT * grp:KT * grp + KT], ps[:, MOD_BANK, 0:KT], v("b_ada", KT * grp, KT),
                                  ALU.add).then_inc(mod_ready, 1)

            def gain(i, name, grp, add):
                dve.scalar_tensor_tensor(gvec[:, KT * i:KT * i + KT], mod[:, KT * grp:KT * grp + KT], add, v(name, 0, KT),
                                         ALU.add, ALU.mult).then_inc(gains, 1)

            def conv_taps(n):
                for _ in range(n):
                    i = taps[0]
                    if i == CONV_K * CT:
                        return
                    taps[0] += 1
                    k, f = divmod(i, CT)
                    src, w = u_pad[:, f, k:k + TOK], v("w_dw", k * CT + f)
                    if k == 0:
                        dve.tensor_scalar(c_acc[:, f, :], src, w, v("b_dw", f), ALU.mult, ALU.add).then_inc(conv_step, 1)
                    else:
                        dve.wait_ge(conv_step, i - CT + 1)
                        dve.scalar_tensor_tensor(c_acc[:, f, :], src, w, c_acc[:, f, :], ALU.mult, ALU.add).then_inc(conv_step, 1)

            def maxima(a, h, t):
                n = a.n0 + NT * h + t
                b, e = a.spans[t]
                w, c = P * (e - b), n % 4
                s = ps[:, S_BANK + n % 2, 0:w]
                dve.wait_ge(s_done, n + 1)
                if a in attn3:
                    dve.tensor_reduce(col[:, 0, c:c + 1], s, AX.X, ALU.max, negate=True).then_inc(m_ready, 1)
                    return
                if n >= 4:
                    dve.wait_ge(t_done, n - 3)
                if a is attn1:
                    if t == 0:
                        dve.wait_ge(rel_ready, h + 1)
                    bias, least = rel[:, h % 2, TOK - w:TOK], -LOWEST
                else:
                    g = head_order()[h]
                    if t == 0:
                        dve.wait_ge(alibi_in[h % 2], 16 * (h // 2 + 1))
                    off = P * (b - t + 1)
                    bias, least = alibi[:, h % 2, off:off + w], sink[:, 1, g:g + 1]
                dve.tensor_tensor_reduce(a.p[:, c, 0:w], s, bias, -1.0, least, ALU.add, ALU.min, col[:, 0, c:c + 1]).then_inc(m_ready, 1)

            def with_sink(a, n):
                if a is attn2:
                    c = n % 4
                    dve.wait_ge(e_done, n + 1)
                    dve.tensor_tensor(col[:, 3, c:c + 1], col[:, 1, c:c + 1], col[:, 2, c:c + 1], ALU.add).then_inc(R["sinks"], 1)

            def inverse(a, n):
                c = n % 4
                if a in attn3:
                    dve.wait_ge(s_free, n - n2 + 1)
                elif a is attn2:
                    dve.wait_ge(R["sinks"], n - n1 + 1)
                else:
                    dve.wait_ge(e_done, n + 1)
                dve.reciprocal(col[:, 4, c:c + 1], col[:, 3 if a is attn2 else 1, c:c + 1]).then_inc(r_ready if a in attn3 else R["xl"], 1)

            def norms(a, n):
                if a in attn3:
                    return
                b, e = a.spans[n % NT]
                dve.wait_ge(R["xl"], n + 1)
                dve.tensor_scalar(a.p[:, n % 4, 0:P * (e - b)], a.p[:, n % 4, 0:P * (e - b)], col[:, 4, n % 4:n % 4 + 1],
                                  None, ALU.mult).then_inc(p_ready, 1)

            def turn_lo(a, h, t):
                n = a.n0 + NT * h + t
                b, e = a.spans[t]
                dve.wait_ge(pt_hi_done, n + 1)
                dve.tensor_tensor(a.pt[1][:, b:e, P * t:P * t + P],
                                  ps[:, T_BANK + n % 2, P * b:P * e].rearrange("p (s q) -> p s q", q=P),
                                  a.pt[0][:, b:e, P * t:P * t + P].bitcast(F32), ALU.subtract).then_inc(pt_ready, 1)

            def attention(a, outs, after=None):
                half_out, pair_lo = outs
                last = NT * a.heads
                for i in range(last + NT + 3):
                    h, t = divmod(i, NT)
                    if 0 <= i - 1 < last:
                        with_sink(a, a.n0 + i - 1)
                    if h < a.heads:
                        maxima(a, h, t)
                    if 0 <= i - 1 < last:
                        inverse(a, a.n0 + i - 1)
                    if t == 0 and h >= 2:
                        half_out(h - 2)
                    if 0 <= i - 1 < last:
                        norms(a, a.n0 + i - 1)
                    if 0 <= i - 3 < last:
                        turn_lo(a, *divmod(i - 3, NT))
                    if after is not None:
                        after(h, t)
                    if t == 2 and h >= 3 and h % 2 == 1:
                        pair_lo(h - 2)

            def outs_of(a, op, hi, lo_, half_sem, ready, base=0):
                def half_out(h):
                    rows = half(h)
                    m = op(h, rows, tmp[rows, tmps[0] % 2, :], bank(a.lin(h))[rows, :])
                    if h % 2 == 0:
                        m.then_inc(half_sem, 1)
                    else:
                        m.then_inc(tmp_w, 1)
                        tmps[0] += 1

                def pair_lo(h):
                    lo_of_tmp(lo_[:, base + h // 2, :], hi[:, base + h // 2, :], ready)

                return half_out, pair_lo

            for n in range(WEIGHT_LEAD):
                split(n)
            dve.wait_ge(consts_in, 48)
            dve.wait_ge(sig_c, 1)
            step(dve.tensor_tensor(c_act[:, 0:KT], v("c", 0, KT), c_act[:, KT:2 * KT], ALU.mult))
            for u in range(16):
                mod_unit()
            mod_group(0)
            dve.wait_ge(mod_ready, 1)
            gain(0, "g_pre_mix", 1, 1.0)
            mod_group(1)
            r = wait_rs()
            dve.wait_ge(gains, 1)
            dve.wait_ge(mod_ready, 2)

            def modulated(k, r, i, grp, ready):
                slot = tmp_slot()
                dve.scalar_tensor_tensor(slot, x[:, k, :], gvec[:, KT * i + k:KT * i + k + 1], r, ALU.mult, ALU.mult).then_inc(tmp_w, 1)
                his[0] += 1
                dve.wait_ge(hi_done, his[0])
                dve.scalar_tensor_tensor(a_lo[:, k, :], slot, mod[:, KT * grp + k:KT * grp + k + 1], a_hi[:, k, :].bitcast(F32),
                                         ALU.add, ALU.subtract).then_inc(ready, 1)

            for k in range(KT):
                modulated(k, r, 0, 0, R["h1"])
            dve.wait_ge(margins, 1)
            for f in range(CT):
                for j in range(2):
                    split(CH["glu"] + 2 * f + j + WEIGHT_LEAD)
                src = bank(LT["glu"] + 2 * f)
                dve.wait_ge(R["glu_sig"], f + 1)
                dve.scalar_tensor_tensor(u_pad[:, f, PAD:PAD + TOK], src, v("b_in", BI_GA + f), sig[:, :], ALU.add,
                                         ALU.mult).then_inc(R["glu"], 1)
            dve.wait_ge(R["glu"], CT)
            for f in range(8):
                split(CH["qk"] + f + WEIGHT_LEAD)
                src = bank(LT["qk"] + f)
                slot = tmp_slot()
                scale = HD ** -0.5 if f < 4 else 1.0
                dve.tensor_scalar(slot, src, v("b_in", f), scale, ALU.add, ALU.mult).then_inc(tmp_w, 1)
                conv_taps(5)
                lo_of_tmp(qk_lo[:, f, :], qk_hi[:, f, :], R["qk"])
            for j in range(4):
                split(CH["v"] + j + WEIGHT_LEAD)
                conv_taps(5)
            for t in range(NT):
                lo(v_lo[:, t, :], bank(LT["v"] + t), v_hi[:, t, :], R["v"])

            def out1(h, rows, dst, src):
                return dve.tensor_scalar(dst, src, vecs[rows, VO["b_in"] + BI_V + h // 2:VO["b_in"] + BI_V + h // 2 + 1], None, ALU.add)

            for j in range(2 * KT):
                split(CH["gates"] + j + WEIGHT_LEAD)
                if j < 10:
                    conv_taps(7)
                if j == 10:
                    dve.wait_ge(R["ln_sum"], 1)
                    for k in range(CT):
                        dve.scalar_tensor_tensor(c_acc[:, k, :], ps[:, STAT_BANK, :], -1.0 / D_CONV, c_acc[:, k, :], ALU.mult,
                                                 ALU.add).then_inc(R["ln_mean"], 1)
                if j == 13:
                    r = wait_rs()
                    for k in range(CT):
                        dve.tensor_tensor(c_acc[:, k, :], c_acc[:, k, :], r, ALU.mult).then_inc(R["cn"], 1)
                    for k in range(CT):
                        dve.wait_ge(R["cn_sig"], k + 1)
                        dve.tensor_scalar(c_acc[:, k, :], c_acc[:, k, :], v("g_ln", k), v("b_ln", k), ALU.mult, ALU.add).then_inc(R["cn"], 1)
                        dve.wait_ge(R["cn"], CT + k + 1)
                        dve.tensor_tensor(c_acc[:, k, :], c_acc[:, k, :], sq[:, k % 2, :], ALU.mult).then_inc(R["cs"], 1)
            attention(attn1, outs_of(attn1, out1, qk_hi, qk_lo, R["o1_half"], R["o1"]))
            for k in range(CT):
                lo(cv_lo[:, k, :], c_acc[:, k, :], cv_hi[:, k, :], R["cv"])
            for f in range(KT):
                split(CH["ac"] + f + WEIGHT_LEAD)
                t0 = LT["ac"] + 2 * f
                dve.tensor_tensor(gprod[:, 0, :], bank(t0), x[:, f, :], ALU.mult).then_inc(R["gate_a"], 1)
                mod_unit()
                dve.scalar_tensor_tensor(gprod[:, 1, :], bank(t0 + 1), v("b_conv_o", f), gate_b[:, f, :], ALU.add,
                                         ALU.mult).then_inc(R["gate_a"], 1)
                mod_unit()
                slot = tmp_slot()
                dve.wait_ge(R["gate_a"], 2 * f + 2)
                dve.tensor_tensor(slot, gprod[:, 0, :], gprod[:, 1, :], ALU.add).then_inc(tmp_w, 1)
                lo_of_tmp(y_lo[:, f, :], y_hi[:, f, :], R["y"])
                if f % 4 == 3:
                    mod_group(2 + f // 4)
            for k in range(KT):
                split(CH["mix"] + k + WEIGHT_LEAD)
                mod_unit()
                mod_unit()
                dve.tensor_copy(y_f[:, k, :], bank(LT["mix"] + k)).then_inc(R["y_f"], 1)
                if k % 4 == 3:
                    mod_group(4 + k // 4)
            dve.wait_ge(mod_ready, 6)
            gain(1, "g_post_mix", 2, 0.0)
            gain(2, "g_pre_ffn", 4, 1.0)
            gain(3, "g_post_ffn", 5, 0.0)

            def residual(y, order, i, ready):
                r = wait_rs()
                dve.wait_ge(gains, 4)
                before = steps[0]
                for k in range(KT + 1):
                    if k < KT:
                        dve.scalar_tensor_tensor(y[:, k, :], y[:, k, :], gvec[:, KT * i + k:KT * i + k + 1], r, ALU.mult,
                                                 ALU.mult).then_inc(dve_step, 1)
                    if k:
                        dve.wait_ge(dve_step, before + k)
                        dve.tensor_tensor(x[:, k - 1, :], x[:, k - 1, :], y[:, k - 1, :], ALU.add).then_inc(ready, 1)
                steps[0] += KT

            dve.wait_ge(R["y_f"], KT)
            dve.wait_ge(x_in, 32)
            residual(y_f, range(KT), 1, R["x_mix"])
            r = wait_rs()
            for k in range(KT):
                modulated(k, r, 2, 3, R["h2"])
            t0, h0 = tmps[0], his[0]
            with dve.Fori(0, FT // 2) as i:
                for pair in range(2):
                    for j in range(2):
                        n = CH["up"] + 2 * pair + j + WEIGHT_LEAD
                        dve.wait_ge(w_hi_done, i * 4 + (n + 1))
                        dve.tensor_tensor(w_lo[:, n % SLOTS, :], w_raw[:, n % RAW, :], w_hi[:, n % SLOTS, :].bitcast(F32),
                                          ALU.subtract).then_inc(w_lo_done, 1)
                    for tap in (1, 0):
                        for j, (c, s, u_s, w_at) in enumerate(((c_val, R["cf_val"], R["u_val"], 0), (c_gate[:, :], R["cf_gate"], R["u_gate"], FT))):
                            if tap == 1:
                                dve.wait_ge(u_s, i * 2 + (up_free + pair + 1))
                            else:
                                dve.wait_ge(s, i * 4 + (2 * pair + 1))
                            dve.scalar_tensor_tensor(c, u_ff[:, 2 * pair + j, tap:tap + TOK],
                                                     vecs[:, bass.ds(i * 2 + (VO["w_dwf"] + tap * 2 * FT + w_at + pair), 1)],
                                                     c, ALU.mult, ALU.add).then_inc(s, 1)
                    dve.wait_ge(R["gel"], i * 2 + (pair + 1))
                    dve.wait_ge(R["cf_val"], i * 4 + (2 * pair + 2))
                    slot = (t0 + pair) % 2
                    dve.tensor_tensor(tmp[:, slot, :], gel, c_val, ALU.mult).then_inc(tmp_w, 1)
                    dve.wait_ge(hi_done, i * 2 + (h0 + pair + 1))
                    at_k = bass.ds(i * (2 * TOK) + pair * TOK, TOK)
                    dve.tensor_tensor(g_lo.rearrange("p k n -> p (k n)")[:, at_k], tmp[:, slot, :],
                                      g_hi.rearrange("p k n -> p (k n)")[:, at_k].bitcast(F32), ALU.subtract).then_inc(R["g"], 1)
            tmps[0] += FT
            his[0] += FT
            for k in range(3):
                split(CH["down"] + k + WEIGHT_LEAD)
            with dve.Fori(0, (FT - 6) // 4) as i:
                for j in range(4):
                    n = CH["down"] + 3 + j + WEIGHT_LEAD
                    dve.wait_ge(w_hi_done, i * 4 + (n + 1))
                    dve.tensor_tensor(w_lo[:, n % SLOTS, :], w_raw[:, n % RAW, :], w_hi[:, n % SLOTS, :].bitcast(F32),
                                      ALU.subtract).then_inc(w_lo_done, 1)
            for k in range(3 + (FT - 6) // 4 * 4, FT):
                split(CH["down"] + k + WEIGHT_LEAD)
            dve.wait_ge(down_step, FT)
            for k in range(KT):
                dve.tensor_copy(y_d[:, KT - 1 - k, :], ps[:, KT - 1 - k, :]).then_inc(R["y_d"], 1)
            dve.wait_ge(R["y_d"], KT)

            def scaled_lo(lo_, hi, gain_, k, s, val, ready):
                his[0] += 1
                dve.wait_ge(s, val)
                dve.wait_ge(hi_done, his[0])
                dve.scalar_tensor_tensor(lo_[:, k, :], x[:, k, :], v(gain_, k), hi[:, k, :].bitcast(F32), ALU.mult,
                                         ALU.subtract).then_inc(ready, 1)

            residual(y_d, range(KT), 3, R["x_ffn"])
            for k in range(KT):
                scaled_lo(a_lo, a_hi, "norm_a", k, R["x_ffn"], k + 1, R["in_a"])
            r = wait_rs()
            for f in range(KT):
                split(CH["a_q"] + f + WEIGHT_LEAD)
                src = bank(LT["a_q"] + f)
                slot = tmp_slot()
                dve.scalar_tensor_tensor(slot, src, HD ** -0.5, r, ALU.mult, ALU.mult).then_inc(tmp_w, 1)
                lo_of_tmp(b_lo[:, f, :], b_hi[:, f, :], R["q_a"])
            for f in range(2):
                split(CH["a_k"] + f + WEIGHT_LEAD)
                src = bank(LT["a_k"] + f)
                slot = tmp_slot()
                dve.tensor_tensor(slot, src, r, ALU.mult).then_inc(tmp_w, 1)
                lo_of_tmp(ka_lo[:, f, :], ka_hi[:, f, :], R["k_a"])

            def silu_tiles(name, z, sg, t_sem, sig_sem, ready):
                for f in range(KT):
                    split(CH[name] + f + WEIGHT_LEAD)
                    dve.tensor_tensor(z[:, f, :], bank(LT[name] + f), r, ALU.mult).then_inc(t_sem, 1)
                    dve.wait_ge(t_sem, f + 1)
                    dve.wait_ge(sig_sem, f + 1)
                    dve.tensor_tensor(z[:, f, :], z[:, f, :], sg[:, :], ALU.mult).then_inc(ready, 1)

            silu_tiles("a_z", z2, zs, R["z_t"], R["z_sig"], R["z_a"])
            for f in range(2):
                split(CH["a_v"] + f + WEIGHT_LEAD)
            dve.wait_ge(R["rcol_t"], 1)
            dve.tensor_copy(rcol[:, :], ps[:, STAT_BANK, :].rearrange("p (t q) -> p t q", q=P)[:, :, 0]).then_inc(stat_free, 1)
            dve.wait_ge(stat_free, 7)
            for t in range(NT):
                src = bank(LT["a_v"] + t)
                slot = tmp_slot()
                dve.tensor_scalar(slot[:, 0:256], src[:, 0:256], rcol[:, t:t + 1], None, ALU.mult).then_inc(tmp_w, 1)
                lo_of_tmp(va_lo[:, t, :], va_hi[:, t, :], R["v_a"], 256)
            dve.wait_ge(sink_in, 16)
            dve.tensor_scalar(sink[:, 1, :], sink[:, 0, :], -1.0, None, ALU.mult).then_inc(R["z_a"], 1)
            dve.wait_ge(R["z_a"], KT + 1)

            def gated(z, base=0):
                return lambda h, rows, dst, src: dve.tensor_tensor(dst, src, z[rows, base + h // 2, :], ALU.mult)

            attention(attn2, outs_of(attn2, gated(z2), b_hi, b_lo, R["o2_half"], R["o2"]))

            def rest(l, after, nxt):
                i = 0 if l == "a" else 1
                for k in range(KT):
                    split(CH[l + "_out"] + k + WEIGHT_LEAD)
                    dve.tensor_tensor(x[:, k, :], bank(LT[l + "_out"] + k), x[:, k, :], ALU.add).then_inc(R["x_attn"], 1)
                    scaled_lo(after[1], after[0], f"ple_g{i}", k, R["x_attn"], KT * i + k + 1, R["in_g"])
                for k in range(PT_K):
                    lo(p_lo[:, k, :], p_raw[:, k, :], p_hi[:, k, :], R["p"])
                for k in range(2):
                    split(CH[l + "_ple"] + k + WEIGHT_LEAD)
                for k in range(KT):
                    dve.tensor_copy(pl[:, k, :], bank(LT[l + "_ple"] + k)).then_inc(R["pl"], 1)
                r = wait_rs()
                for k in range(KT):
                    split(CH[l + "_gate"] + k + WEIGHT_LEAD)
                    g = gs2[:, k % 2, :]
                    dve.tensor_tensor(g, bank(LT[l + "_gate"] + k), r, ALU.mult).then_inc(R["gt"], 1)
                    dve.wait_ge(R["gsig"], KT * i + k + 1)
                    dve.wait_ge(R["pl"], KT * i + k + 1)
                    step(dve.tensor_tensor(pl[:, k, :], pl[:, k, :], g, ALU.mult))
                    dve.tensor_tensor(x[:, k, :], x[:, k, :], pl[:, k, :], ALU.add).then_inc(R["x_ple"], 1)
                    if nxt is not None:
                        scaled_lo(nxt[1], nxt[0], "norm_b", k, R["x_ple"], KT * i + k + 1, R["in_b"])

            rest("a", (a_hi, a_lo), (b_hi, b_lo))
            r = wait_rs()
            for f in range(QT + KVT):
                split(CH["b_c"] + f + WEIGHT_LEAD)
                dve.tensor_tensor(cq_f[:, f, :], bank(LT["b_c"] + f), r, ALU.mult).then_inc(R["cq"], 1)
            split(CH["b_c"] + 5 + WEIGHT_LEAD)
            src = bank(LT["b_c"] + 5)
            dve.tensor_tensor(kr_f[64:128, :], src[64:128, :], r[64:128, :], ALU.mult).then_inc(R["kr"], 1)
            dve.wait_ge(R["kr"], 1)
            dve.wait_ge(R["rope_k"], 16)
            dve.tensor_tensor(kr_r[64:96, :], kr_f[96:128, :], rope_k[96:128, :], ALU.mult)
            step(dve.tensor_tensor(kr_f[64:96, :], kr_f[64:96, :], rope_k[64:96, :], ALU.mult))
            dve.tensor_tensor(kr_f[64:96, :], kr_f[64:96, :], kr_r[64:96, :], ALU.add).then_inc(R["kr_sum"], 1)
            dve.wait_ge(R["kr_sum"], 1)
            for b in range(2):
                lo(k3_lo[64:96, b, :], kr_f[64:96, :], k3_hi[64:96, b, :], R["kr"])
            dve.wait_ge(R["cq"], QT + KVT)
            for part, (n0_, n_, name, hi, lo_) in enumerate(((0, QT, "q_norm", cq_hi, cq_lo), (QT, KVT, "kv_norm", ck_hi, ck_lo))):
                r2 = wait_rs()
                for k in range(n_):
                    slot = tmp_slot()
                    dve.scalar_tensor_tensor(slot, cq_f[:, n0_ + k, :], v(name, k), r2, ALU.mult, ALU.mult).then_inc(tmp_w, 1)
                    lo_of_tmp(lo_[:, k, :], hi[:, k, :], R["cqn"])
            silu_tiles("b_z", z3, zs3, R["z_tb"], R["z_sigb"], R["z_b"])
            for hf in range(2):
                a = attn3[hf]
                split(CH[f"b_v{hf}"] + WEIGHT_LEAD)
                for t in range(NT):
                    lo(vb_lo[:, t, :], bank(LT[f"b_v{hf}"] + t), vb_hi[:, t, :], R["v_b"])

                def key_lo(h):
                    src = bank(a.k_lin(h - h % 2))[64 * (h % 2):64 * (h % 2) + 64, :]
                    lo(k3_lo[0:64, h % 2, :], src, k3_hi[0:64, h % 2, :], R["k_b"])

                def query(h):
                    src = bank(a.q_lin(h))
                    if hf or h:
                        dve.wait_ge(R["q_b"], 8 * hf + h)
                    dve.tensor_tensor(q3_f[0:96, :], src[0:96, :], rope[0:96, :], ALU.mult)
                    dve.tensor_tensor(q3_r[64:96, :], src[96:128, :], rope[96:128, :], ALU.mult).then_inc(R["q_t"], 1)

                def query_lo(h):
                    lo(q3_lo[0:96, h % 2, :], q3_f[0:96, :], q3_hi[0:96, h % 2, :], R["q_b"])
                    if h % 2:
                        split(CH[f"b_h{hf}"] + h // 2 + WEIGHT_LEAD)

                def after(h, t):
                    if t == 0 and 1 <= h <= 6:
                        query(h + 1)
                    if t == 1 and h % 2 == 1 and h + 1 < 8:
                        key_lo(h + 1)
                    if t == 2 and 1 <= h <= 6:
                        query_lo(h + 1)
                    if t == 1 and h % 2 == 0 and 2 <= h <= 6:
                        key_lo(h + 1)

                key_lo(0)
                key_lo(1)
                for h in range(2):
                    query(h)
                    query_lo(h)
                attention(a, outs_of(a, gated(z3, 4 * hf), a_hi, a_lo, R["o3_half"], R["o3"], 4 * hf), after)
            rest("b", (b_hi, b_lo), None)
            r = wait_rs()
            for k in range(KT):
                dve.scalar_tensor_tensor(x[:, k, :], x[:, k, :], v("final_g", k), r, ALU.mult, ALU.mult).then_inc(R["fin"], 1)


def _feature_tiles(a):
    t = np.ascontiguousarray(a.T)
    return np.ascontiguousarray(t.reshape(-1, P, t.shape[1]).transpose(1, 0, 2))


def _columns(vec):
    return vec.reshape(-1, P).T


def _weight_stream(i):
    chunks = []

    def rows(w):
        return np.asarray(w).reshape(-1, P, w.shape[1])

    def out_tiles(w, group=1):
        r = rows(w)
        kt, n = r.shape[0], r.shape[2] // P
        t = r.reshape(kt, P, n // group, group, P).transpose(2, 1, 3, 0, 4)
        chunks.extend(t.reshape(n // group, P, group * kt * P))

    def row_chunks(w, per):
        r = rows(w)
        chunks.extend(r.reshape(-1, per, P, r.shape[2]).transpose(0, 2, 1, 3).reshape(r.shape[0] // per, P, -1))

    w_in = np.asarray(i["w_in"][0])
    q, k, v, ga, gb, gate_a, gate_b = np.split(w_in, np.cumsum([D_ATTN] * 3 + [D_CONV] * 2 + [D]), axis=1)
    for f in range(CT):
        out_tiles(ga[:, P * f:P * f + P])
        out_tiles(gb[:, P * f:P * f + P])
    out_tiles(q)
    out_tiles(k)
    row_chunks(v, 2)
    out_tiles(gate_a)
    out_tiles(gate_b)
    for f in range(KT):
        s = slice(P * f, P * f + P)
        out_tiles(np.concatenate([i["w_attn_o"][0][:, s], i["w_conv_o"][0][:, s]], axis=0))
    out_tiles(i["w_mix_o"][0])
    for f in range(FT):
        out_tiles(i["w_up"][0][:, P * f:P * f + P])
        out_tiles(i["w_up"][0][:, D_FF + P * f:D_FF + P * f + P])
    row_chunks(i["w_down"][0], 1)
    a = np.asarray(i["a_w_in_2"][0])
    q, k, v, z = np.split(a, np.cumsum([D, 256, 256]), axis=1)
    order = head_order()
    out_tiles(q.reshape(D, A_HEADS, HD)[:, order].reshape(D, D))
    out_tiles(k)
    out_tiles(z.reshape(D, A_HEADS, HD)[:, order].reshape(D, D))
    row_chunks(v, 4)
    out_tiles(np.asarray(i["a_w_out_2"][0]).reshape(A_HEADS, HD, D)[order].reshape(D, D))
    out_tiles(i["ple_w_2"][0], 4)
    out_tiles(i["ple_w_gate_2"][0])
    b = np.asarray(i["b_w_in_2"][0])
    cq, ckv, kr, z = np.split(b, np.cumsum([Q_LORA, KV_LORA, B_ROPE]), axis=1)
    swap = np.r_[B_ROPE // 2:B_ROPE, 0:B_ROPE // 2]
    out_tiles(cq)
    out_tiles(ckv)
    out_tiles(np.concatenate([kr, kr[:, swap], kr, kr[:, swap]], axis=1))
    out_tiles(z)
    qb = np.asarray(i["b_w_qb_2"][0]).reshape(Q_LORA, B_HEADS, B_NOPE + B_ROPE)
    qb = np.concatenate([qb, qb[:, :, B_NOPE:][:, :, swap]], axis=2)
    kvb = np.asarray(i["b_w_kvb_2"][0]).reshape(KV_LORA, B_HEADS, B_NOPE + B_V)
    for half in range(2):
        row_chunks(kvb[:, 8 * half:8 * half + 8, B_NOPE:].reshape(KV_LORA, 8 * B_V), 2)
        for h in range(8 * half, 8 * half + 8, 2):
            parts = [rows(qb[:, h]), rows(qb[:, h + 1]), rows(kvb[:, h:h + 2, :B_NOPE].reshape(KV_LORA, P))]
            chunks.append(np.concatenate([p.transpose(1, 0, 2).reshape(P, -1) for p in parts], axis=1))
    out_tiles(i["b_w_out_2"][0])
    out_tiles(i["ple_w_2"][1], 4)
    out_tiles(i["ple_w_gate_2"][1])
    return np.stack(chunks)


def _constants():
    half = B_ROPE // 2
    inv = (np.float32(10000.0) ** (-np.arange(half, dtype=np.float32) / np.float32(half))).astype(np.float32)
    ang = (np.arange(TOK, dtype=np.float32)[:, None] * inv[None, :]).astype(np.float32).T
    rope = np.ones((P, TOK), np.float32)
    rope[64:96] = np.concatenate([np.cos(ang), np.cos(ang)])
    rope[96:128] = np.concatenate([-np.sin(ang), np.sin(ang)])
    slopes = (2.0 ** (-8.0 * np.arange(1, A_HEADS + 1) / A_HEADS)).astype(np.float32)[head_order()]
    dist = np.abs(np.arange(3 * P)[None, :] - P - np.arange(P)[:, None])
    alibi = np.where(dist <= WINDOW, -slopes[:, None, None] * dist.astype(np.float32), np.float32(MASKED)).astype(np.float32)
    return np.eye(P, dtype=np.float32), rope * np.float32((B_NOPE + B_ROPE) ** -0.5), rope, alibi


def kernel(**inputs):
    import concourse.bacc as _bacc
    from concourse.bass_utils import run_bass_kernel_spmd as _run

    i = {k: np.asarray(a) for k, a in inputs.items()}
    ident, rope, rope_k, alibi = _constants()
    vec = {
        "c": i["c"][0], "b_ada": i["b_ada"][0], "g_pre_mix": i["g_pre_mix"][0], "g_post_mix": i["g_post_mix"][0],
        "b_in": i["b_in"][0], "w_dw": i["w_dw_conv"][0].reshape(-1), "b_dw": i["b_dw_conv"][0], "g_ln": i["g_conv_ln"][0],
        "b_ln": i["b_conv_ln"][0], "b_conv_o": i["b_conv_o"][0], "g_pre_ffn": i["g_pre_ffn"][0],
        "g_post_ffn": i["g_post_ffn"][0], "w_dwf": i["w_dw_ffn"][0].reshape(-1), "b_dwf": i["b_dw_ffn"][0],
        "norm_a": i["norm_g_2"][0], "norm_b": i["norm_g_2"][1], "q_norm": i["b_q_norm_2"][0], "kv_norm": i["b_kv_norm_2"][0],
        "ple_g0": i["ple_norm_g_2"][0], "ple_g1": i["ple_norm_g_2"][1], "final_g": i["final_norm_g_2"],
    }
    where = np.minimum(TOK - P + np.arange(P)[:, None] - np.arange(TOK)[None, :], MAX_REL) + MAX_REL
    arrays = {
        "in_x": _feature_tiles(i["x"][0]),
        "in_w": _weight_stream(i),
        "in_ada": np.ascontiguousarray(i["w_ada"][0].reshape(KT, P, 6, D).transpose(2, 0, 1, 3)),
        "in_vecs": np.ascontiguousarray(np.concatenate([_columns(vec[n]) for n, _ in VECS], axis=1)),
        "in_ident": ident, "in_rope": rope, "in_rope_k": rope_k,
        "in_rel": np.ascontiguousarray(i["rel_bias"][0][:, where]),
        "in_alibi": alibi,
        "in_sink": np.ascontiguousarray(i["a_sink_2"]),
        "in_p": np.stack([_feature_tiles(i["p_2"][l, 0]) for l in range(2)]),
    }
    nc = _bacc.Bacc("TRN2", target_bir_lowering=False, num_devices=1)
    args = [nc.dram_tensor(n, a.shape, mybir.dt.from_np(a.dtype), kind="ExternalInput").ap() for n, a in arrays.items()]
    args.append(nc.dram_tensor("out_0", (P, KT, TOK), F32, kind="ExternalOutput").ap())
    build(nc, *args)
    r = _run(nc, [arrays], core_ids=[0])
    got = np.asarray(r.results[0]["out_0"])
    return np.ascontiguousarray(got.transpose(1, 0, 2).reshape(D, TOK).T).reshape(1, TOK, D)
```

```python
from contextlib import ExitStack

import numpy as np

import concourse.bass as bass
from concourse import mybir

F32 = mybir.dt.float32
F32R = mybir.dt.float32r
ALU = mybir.AluOpType
ACT = mybir.ActivationFunctionType
AX = mybir.AxisListType

P = 128
TOK = 512
D = 1024
KT = D // P
NT = TOK // P
EPS = 1e-6

H1 = 8
HD = 64
D_ATTN = H1 * HD
D_CONV = 512
CONV_K = 31
PAD = CONV_K - 1
CT = D_CONV // P
CHUNK = 64
MAX_REL = 128
D_FF = 2816
FT = D_FF // P
FFN_K = 3
A_HEADS, A_KV, A_GROUP = 16, 4, 4
WINDOW = 128
B_HEADS, B_NOPE, B_ROPE, B_V = 16, 64, 32, 64
Q_LORA, KV_LORA = 384, 256
QT, KVT = Q_LORA // P, KV_LORA // P
PLE = 256
PT_K = PLE // P
MASKED = -1e30
LOWEST = -3e38

CHW = KT * P
RAW = 2
SLOTS = 4
WEIGHT_LEAD = 3
LIN = 4
S_BANK, T_BANK = 4, 6
MOD_BANK, STAT_BANK = 6, 7

STAGES = [("glu", 8), ("qk", 8), ("v", 4), ("gates", 2 * KT), ("ac", KT), ("mix", KT), ("up", 2 * FT), ("down", FT),
          ("a_q", KT), ("a_k", 2), ("a_z", KT), ("a_v", 2), ("a_out", KT), ("a_ple", 2), ("a_gate", KT),
          ("b_c", 6), ("b_z", KT), ("b_v0", 1), ("b_h0", 4), ("b_v1", 1), ("b_h1", 4), ("b_out", KT),
          ("b_ple", 2), ("b_gate", KT)]
CH = {}
N_CHUNKS = 0
for _name, _n in STAGES:
    CH[_name] = N_CHUNKS
    N_CHUNKS += _n

VECS = [("c", KT), ("b_ada", 6 * KT), ("g_pre_mix", KT), ("g_post_mix", KT), ("b_in", 36), ("w_dw", CONV_K * CT),
        ("b_dw", CT), ("g_ln", CT), ("b_ln", CT), ("b_conv_o", KT), ("g_pre_ffn", KT), ("g_post_ffn", KT),
        ("w_dwf", FFN_K * 2 * FT), ("b_dwf", 2 * FT), ("norm_a", KT), ("norm_b", KT), ("q_norm", QT),
        ("kv_norm", KVT), ("ple_g0", KT), ("ple_g1", KT), ("final_g", KT)]
VO = {}
N_VECS = 0
for _name, _n in VECS:
    VO[_name] = N_VECS
    N_VECS += _n
BI_Q, BI_K, BI_V, BI_GA, BI_GB, BI_A, BI_B = 0, 4, 8, 12, 16, 20, 28

SQ = {}
_n = 0
for _name, _count in (("pre_mix", KT), ("conv", CT), ("mix", KT), ("pre_ffn", KT), ("down", KT), ("norm_a", KT), ("a_out", KT),
                      ("a_gate", KT), ("lora", QT + KVT), ("b_out", KT), ("b_gate", KT)):
    SQ[_name] = _n
    _n += _count

ADA_LATE = [2, 4, 3, 5]


def head_order():
    order = []
    for pair in range(A_KV // 2):
        for j in range(A_GROUP):
            order += [2 * pair * A_GROUP + j, (2 * pair + 1) * A_GROUP + j]
    return order


def mla_pieces(h, t):
    pieces = []
    if h % 2 == 0 and t >= 1:
        pieces.append(("q", h + 2, t - 1, t))
    if h % 2 == 1 and t <= 1:
        pieces.append(("k", h + 1, t, t + 1))
    if h % 2 == 1 and t >= 2:
        pieces.append(("q", h + 2, t - 2, t - 1))
    if h % 2 == 0 and t == 0:
        pieces.append(("q", h + 1, QT - 1, QT))
    pieces = [p for p in pieces if p[1] < 8 and not (h == 0 and t == 0)]
    if t >= 1 and 1 <= h <= 8:
        pieces.append(("o", h - 1, t - 1, t))
    if t == 0 and h >= 2:
        pieces.append(("o", h - 2, 3, 4))
    return pieces


def mla_tiles():
    order = [("k", 0), ("q", 0)] + [("v", t) for t in range(NT)] + [("q", 1)]
    for i in range(NT * 8 + NT + 1):
        for kind, h, _, end in mla_pieces(*divmod(i, NT)):
            if end == {"k": KVT, "q": QT, "o": 4}[kind]:
                order.append((kind, h))
    return order


def build(nc, t_x, t_w, t_ada, t_vecs, t_ident, t_rope, t_rope_k, t_rel, t_alibi, t_sink, t_p, out):
    with ExitStack() as ctx:
        def sb(name, shape, dt=F32):
            return ctx.enter_context(nc.sbuf_tensor(name, shape, dt))

        def sem(name):
            return ctx.enter_context(nc.semaphore(name))

        x = sb("x_resid", [P, KT, TOK])
        a_at = -(-nc.sbuf_base // 64) * 64
        sb("a_place", [P, 2 * KT * TOK + 16])
        a_hi = nc.alloc_sbuf_tensor_at("a_hi", [P, KT, TOK], F32R, offset=a_at)
        a_lo = nc.alloc_sbuf_tensor_at("a_lo", [P, KT, TOK], F32R, offset=a_at + 4 * KT * TOK)
        gate_b = nc.alloc_sbuf_tensor_at("gate_b", [P, KT, TOK], F32, offset=a_at)
        w_raw = sb("w_raw", [P, RAW, CHW])
        w_hi, w_lo = sb("w_hi", [P, SLOTS, CHW], F32R), sb("w_lo", [P, SLOTS, CHW], F32R)
        vecs = sb("vecs", [P, N_VECS])
        ident = sb("ident", [P, P])
        ones = sb("ones", [P, P])
        rope = sb("rope", [P, TOK])
        sink = sb("sink", [P, 2, A_HEADS])
        mod = sb("mod", [P, 6 * KT])
        gvec = sb("gvec", [P, 4 * KT])
        c_act = sb("c_act", [P, 2 * KT])
        rs = sb("rs", [P, 3, TOK])
        sq = sb("sq", [P, 2, TOK])
        tmp = sb("tmp", [P, 2, TOK])
        col = sb("col", [P, 3, 4])
        rcol = sb("rcol", [P, NT])
        arena_kib = 100
        slab_at = -(-nc.sbuf_base // 64) * 64
        sb("arena", [P, arena_kib * 256 + 16])

        def at(name, kib, shape, dt=F32):
            size = 4 * int(np.prod(shape[1:]))
            assert kib * 1024 + size <= arena_kib * 1024, name
            return nc.alloc_sbuf_tensor_at(name, shape, dt, offset=slab_at + int(kib * 1024))

        qk_hi, qk_lo = at("qk_hi", 0, [P, 8, TOK], F32R), at("qk_lo", 16, [P, 8, TOK], F32R)
        v_hi, v_lo = at("v_hi", 32, [P, NT, D_ATTN], F32R), at("v_lo", 40, [P, NT, D_ATTN], F32R)
        c_acc = at("c_acc", 48, [P, CT, TOK])
        u_pad = at("u_pad", 56, [P, CT, PAD + TOK])
        rel = at("rel", 65, [P, 2, TOK])
        p1 = at("p1", 69, [P, 4, TOK])
        pt1_hi, pt1_lo = at("pt1_hi", 77, [P, NT, TOK], F32R), at("pt1_lo", 85, [P, NT, TOK], F32R)
        ada_a = at("ada_a", 69, [P, 6, D])
        ada_b = [at(f"ada_b{i}", kib, [P, D]) for i, kib in enumerate((92, 8, 12, 28, 96, 48))]
        ada_g = at("ada_g0", 96, [P, D]), at("ada_g1", 73, [P, D])
        acc_g = at("acc_g", 69, [P, D])
        ada_p = at("ada_p", 96, [P, D])
        acc_a = at("acc_a", 48, [P, 2, D])
        acc_b = at("acc_b", 56, [P, D])
        acc_p = at("acc_p", 60, [P, D])
        ada_q = sq.rearrange("p a n -> p (a n)")
        sig = at("sig", 93, [P, TOK])
        cv_hi, cv_lo = at("cv_hi", 32, [P, CT, TOK], F32R), at("cv_lo", 40, [P, CT, TOK], F32R)
        gate_t = at("gate_t", 77, [P, KT, TOK])
        gprod = at("gprod", 24, [P, 2, TOK])
        y_hi, y_lo = at("y_hi", 60, [P, KT, TOK], F32R), at("y_lo", 76, [P, KT, TOK], F32R)
        y_f = at("y_f", 32, [P, KT, TOK])
        g_hi, g_lo = at("g_hi", 0, [P, FT, TOK], F32R), at("g_lo", 44, [P, FT, TOK], F32R)
        U0 = FFN_K - 1
        u_ff = at("u_ff", 88, [P, 4, U0 + TOK])
        c_gate = at("c_gate", 97, [P, TOK])
        c_val, gel = sq[:, 1, :], sq[:, 0, :]
        y_d = at("y_d", 0, [P, KT, TOK])
        b_hi, b_lo = at("b_hi", 0, [P, KT, TOK], F32R), at("b_lo", 16, [P, KT, TOK], F32R)
        ka_hi, ka_lo = at("ka_hi", 32, [P, 2, TOK], F32R), at("ka_lo", 36, [P, 2, TOK], F32R)
        va_hi, va_lo = at("va_hi", 40, [P, NT, 256], F32R), at("va_lo", 44, [P, NT, 256], F32R)
        z2 = at("z2", 48, [P, KT, TOK])
        p2 = at("p2", 64, [P, 4, 1 + 384])
        minus_s = at("minus_s", 92, [P, 2, 1 + 384])
        pt2_hi, pt2_lo = at("pt2_hi", 72, [P, NT, TOK], F32R), at("pt2_lo", 80, [P, NT, TOK], F32R)
        alibi = at("alibi", 88, [P, 2, 384])
        zs = at("zs", 92, [P, TOK])
        o_pair2 = at("o_pair2", 96, [P, 2, TOK])
        pl = at("pl", 32, [P, KT, TOK])
        p_raw = at("p_raw", 88, [P, PT_K, TOK])
        p_hi, p_lo = at("p_hi", 92, [P, PT_K, TOK], F32R), at("p_lo", 96, [P, PT_K, TOK], F32R)
        gs2 = at("gs2", 72, [P, 2, TOK])
        vb_hi, vb_lo = at("vb_hi", 0, [P, NT, TOK], F32R), at("vb_lo", 8, [P, NT, TOK], F32R)
        z3 = at("z3", 32, [P, KT, TOK])
        cq_hi, cq_lo = at("cq_hi", 48, [P, QT, TOK], F32R), at("cq_lo", 54, [P, QT, TOK], F32R)
        ck_hi, ck_lo = at("ck_hi", 60, [P, KVT, TOK], F32R), at("ck_lo", 64, [P, KVT, TOK], F32R)
        cq_f = at("cq_f", 76, [P, QT + KVT, TOK])
        kr_f = at("kr_f", 86, [P, TOK])
        p3 = at("p3", 68, [P, 4, TOK])
        pt3_hi, pt3_lo = at("pt3_hi", 76, [P, NT, TOK], F32R), at("pt3_lo", 84, [P, NT, TOK], F32R)
        q3_hi, q3_lo = at("q3_hi", 16, [P, 2, TOK], F32R), at("q3_lo", 20, [P, 2, TOK], F32R)
        k3_hi, k3_lo = at("k3_hi", 92, [P, 2, TOK], F32R), at("k3_lo", 96, [P, 2, TOK], F32R)
        q3_f = at("q3_f", 24, [P, TOK])
        q3_r = at("q3_r", 26, [P, TOK])
        zs3 = at("zs3", 68, [P, TOK])
        o_pair3 = at("o_pair3", 28, [P, 2, TOK])
        rope_k = at("rope_k", 70, [P, TOK])
        kr_r = at("kr_r", 88, [P, TOK])

        ps = ctx.enter_context(nc.psum_tensor("ps", [P, 8, TOK], F32))

        consts_in, x_in, rel_in, sink_in = sem("consts_in"), sem("x_in"), [sem(f"rel_in{i}") for i in range(2)], sem("sink_in")
        alibi_in, p_in, out_done = [sem(f"alibi_in{i}") for i in range(2)], sem("p_in"), sem("out_done")
        w_land = [sem(f"w_land{i}") for i in range(RAW)]
        w_hi_done, w_lo_done, down_step = sem("w_hi_done"), sem("w_lo_done"), sem("down_step")
        ada_land = [sem(f"ada_land{i}") for i in range(12)]
        ada_p_land, ada_p_used, vecs_in, conv_step_p = sem("ada_p_land"), sem("ada_p_used"), sem("vecs_in"), sem("conv_step_p")
        ada_g_land, ada_g_prod, ada_g_used = [sem(f"ada_g_land{i}") for i in range(2)], sem("ada_g_prod"), sem("ada_g_used")
        ada_p_prod, conv_prod = sem("ada_p_prod"), sem("conv_prod")
        o_full, o_hi = sem("o_full"), sem("o_hi")
        ada_used = sem("ada_used")
        sig_c, mod_sum, mod_ready, gains = sem("sig_c"), sem("mod_sum"), sem("mod_ready"), sem("gains")
        ones_set, margins = sem("ones_set"), sem("margins")
        sq_ready, sq_used, stat_free, rs_ready = sem("sq_ready"), sem("sq_used"), sem("stat_free"), sem("rs_ready")
        tmp_w, hi_done = sem("tmp_w"), sem("hi_done")
        lin_done = sem("lin_done")
        dve_step, conv_step = sem("dve_step"), sem("conv_step")
        s_done, s_free, m_ready, e_done = sem("s_done"), sem("s_free"), sem("m_ready"), sem("e_done")
        v_half, r_ready, p_ready, p_ready_act, t_done, pt_hi_done, pt_ready = sem("v_half"), sem("r_ready"), sem("p_ready"), sem("p_ready_act"), sem("t_done"), sem("pt_hi_done"), sem("pt_ready")
        rel_ready = sem("rel_ready")
        h_ready = {n: sem("ready_" + n) for n in (
            "h1", "glu_sig", "glu", "cs", "rope_k", "qk", "v", "o1_half", "o1", "ln_mean", "cv", "gate_sig", "gate_a", "y", "y_f", "x_mix", "h2",
            "u_val", "u_gate", "cf_val", "cf_gate", "gel", "g", "down", "y_d", "x_ffn",
            "in_a", "q_a", "k_a", "z_t", "z_sig", "z_a", "v_a", "o2_half", "o2", "x_attn", "in_g", "p", "pl", "gt", "gsig", "x_ple",
            "in_b", "cq", "kr", "kr_sum", "cqn", "ln_sum", "cn", "cn_sig", "rcol_t", "z_tb", "z_sigb", "z_b", "v_b", "q_t", "q_r", "q_b", "k_b", "o3_half", "o3", "fin")}
        R = h_ready
        v_step = sem("v_step")

        def v(name, i=0, n=1):
            return vecs[:, VO[name] + i:VO[name] + i + n]

        evicted = []

        def plan(n, s, start=0, per=1):
            first = len(evicted)
            evicted.extend((s, start + per * (j + 1)) for j in range(n))
            return first

        LT = {}
        first = len(evicted)
        for f in range(CT):
            evicted.append((R["glu"], f + 1))
            evicted.append((R["glu_sig"], f + 1))
        LT["glu"] = first
        LT["qk"] = plan(8, R["qk"])
        LT["v"] = plan(NT, R["v"])
        LT["gates"] = plan(2 * KT, R["gate_sig"])
        LT["o1"] = len(evicted)
        for i in range(H1 // 2):
            evicted += [(R["o1_half"], i + 1), (R["o1"], i + 1)]
        LT["ac"] = plan(2 * KT, R["gate_a"])
        LT["mix"] = plan(KT, R["y_f"])
        up_free = 2
        LT["up"] = len(evicted)
        for i in range(FT):
            evicted += [(R["u_val"], up_free + i + 1), (R["u_gate"], up_free + i + 1)]
        n_up = len(evicted)
        LT["a_q"] = plan(KT, R["q_a"])
        LT["a_k"] = plan(2, R["k_a"])
        LT["a_z"] = plan(KT, R["z_t"])
        LT["a_v"] = plan(NT, R["v_a"])
        LT["o2"] = len(evicted)
        for i in range(A_HEADS // 2):
            evicted += [(R["o2_half"], i + 1), (o_full, i + 1)]
        for l, s in (("a", 0), ("b", KT)):
            if l == "b":
                LT["b_c"] = len(evicted)
                evicted += [(R["cq"], j + 1) for j in range(QT + KVT)] + [(R["kr"], 1)]
                LT["b_z"] = plan(KT, R["z_tb"])
                for half in range(2):
                    for kind, h in mla_tiles():
                        g = 8 * half + h
                        if h == 0 and kind == "k":
                            LT[f"b_h{half}"] = len(evicted)
                        if h == 0 and kind == "v":
                            LT[f"b_v{half}"] = len(evicted)
                        evicted.append({"v": (R["v_b"], NT * half + h + 1), "k": (R["k_b"], g + 2), "q": (R["q_t"], g + 1),
                                        "o": (R["o3_half"], g // 2 + 1) if h % 2 == 0 else (o_full, A_HEADS // 2 + g // 2 + 1)}[kind])
            LT[l + "_out"] = plan(KT, R["x_attn"], s)
            LT[l + "_ple"] = plan(KT, R["pl"], s)
            LT[l + "_gate"] = plan(KT, R["gt"], s)

        class Attn:
            def __init__(self, heads, n0, rows, q, k, vv, pbuf, pt, spans, lin, over_keys):
                self.heads, self.n0, self.rows, self.q, self.k, self.v = heads, n0, rows, q, k, vv
                self.p, self.pt, self.spans, self.lin, self.over_keys = pbuf, pt, spans, lin, over_keys
                self.p_at = 1 if pbuf is p2 else 0

        def half(h):
            return slice(64 * (h % 2), 64 * (h % 2) + 64)

        causal = [(0, t + 1) for t in range(NT)]
        band = [(max(t - 1, 0), min(t + 2, NT)) for t in range(NT)]
        full = [(0, NT)] * NT
        n1 = NT * H1
        n2 = n1 + NT * A_HEADS
        attn1 = Attn(H1, 0, half, lambda h: (qk_hi[half(h), h // 2, :], qk_lo[half(h), h // 2, :]),
                     lambda h: (qk_hi[half(h), 4 + h // 2, :], qk_lo[half(h), 4 + h // 2, :]),
                     lambda h, s: (v_hi[:, s, P * (h // 2):P * (h // 2) + P], v_lo[:, s, P * (h // 2):P * (h // 2) + P]),
                     p1, (pt1_hi, pt1_lo), causal, lambda h: LT["o1"] + h, [[(0, 0, 2), (1, 1, 2)], [(0, 2, 4), (1, 2, 4), (2, 2, 4), (3, 3, 4)]])
        attn2 = Attn(A_HEADS, n1, half, lambda h: (b_hi[half(h), h // 2, :], b_lo[half(h), h // 2, :]),
                     lambda h: (ka_hi[half(h), h // 8, :], ka_lo[half(h), h // 8, :]),
                     lambda h, s: (va_hi[:, s, P * (h // 8):P * (h // 8) + P], va_lo[:, s, P * (h // 8):P * (h // 8) + P]),
                     p2, (pt2_hi, pt2_lo), band, lambda h: LT["o2"] + h, [[(0, 0, 2), (1, 0, 2), (2, 1, 2)], [(2, 2, 4), (3, 2, 4), (1, 2, 3)]])

        def mla(hf):
            order = mla_tiles()
            place = {kh: i for i, kh in enumerate(order)}
            a = Attn(8, n2 + 8 * NT * hf, half, lambda h: (q3_hi[0:96, h % 2, :], q3_lo[0:96, h % 2, :]),
                     lambda h: (k3_hi[0:96, h % 2, :], k3_lo[0:96, h % 2, :]),
                     lambda h, s: (vb_hi[:, s, P * (h // 2):P * (h // 2) + P], vb_lo[:, s, P * (h // 2):P * (h // 2) + P]),
                     p3, (pt3_hi, pt3_lo), full, lambda h: LT[f"b_h{hf}"] + place[("o", h)], [[(s, 0, 2) for s in range(4)], [(s, 2, 4) for s in range(4)]])
            a.q_lin = lambda h: LT[f"b_h{hf}"] + place[("q", h)]
            a.k_lin = lambda h: LT[f"b_h{hf}"] + place[("k", h)]
            a.hf = hf
            return a

        attn3 = [mla(0), mla(1)]

        used_at = {}

        def chunks_of(name, tiles):
            t0 = LT[name]
            for j in range(dict(STAGES)[name]):
                used_at[CH[name] + j] = (lin_done, t0 + tiles * (j + 1))

        for name in ("glu", "qk", "gates", "mix", "up", "a_q", "a_k", "a_z", "a_out", "a_gate", "b_c", "b_z", "b_out", "b_gate"):
            chunks_of(name, 1)
        for j in range(3):
            used_at[CH["v"] + j] = (v_step, j + 1)
        used_at[CH["v"] + 3] = (lin_done, LT["v"] + NT)
        chunks_of("ac", 2)
        for j in range(FT):
            used_at[CH["down"] + j] = (down_step, j + 1)
        used_at[CH["a_v"]] = (v_step, 4)
        used_at[CH["a_v"] + 1] = (lin_done, LT["a_v"] + NT)
        for l in "ab":
            chunks_of(l + "_ple", KT // 2)
        for hf in range(2):
            used_at[CH[f"b_v{hf}"]] = (lin_done, LT[f"b_v{hf}"] + NT)
            for pair in range(4):
                used_at[CH[f"b_h{hf}"] + pair] = (lin_done, attn3[hf].q_lin(2 * pair + 1) + 1)

        block = ctx.enter_context(nc.Block())

        @block.sync
        def _(sp):
            for n in range(RAW):
                sp.dma_start(w_raw[:, n, :], t_w[n]).then_inc(w_land[n], 16)
            turns = (N_CHUNKS - RAW) // RAW
            with sp.Fori(0, turns) as i:
                for j in range(RAW):
                    sp.wait_ge(w_lo_done, i * RAW + (j + 1))
                    sp.dma_start(w_raw[:, j, :], t_w[bass.ds(i * RAW + (RAW + j), 1)].rearrange("o p n -> (o p) n")
                                 ).then_inc(w_land[j], 16)
            for n in range(RAW + turns * RAW, N_CHUNKS):
                sp.wait_ge(w_lo_done, n - RAW + 1)
                sp.dma_start(w_raw[:, n % RAW, :], t_w[n]).then_inc(w_land[n % RAW], 16)
            for k in range(KT):
                sp.wait_ge(R["fin"], k + 1)
                sp.dma_start(out[:, k, :], x[:, k, :]).then_inc(out_done, 16)
            sp.wait_ge(out_done, 16 * KT)

        @block.gpsimd
        def _(pool):
            pool.dma_start(vecs[:, :], t_vecs).then_inc(vecs_in, 16)
            for u in range(16):
                if u == 4:
                    pool.dma_start(x[:, :, :], t_x).then_inc(x_in, 16)
                    pool.memset(ones[:, :], 1.0).then_inc(ones_set, 1)
                if u >= 6:
                    pool.wait_ge(ada_used, u - 5)
                pool.dma_start(ada_a[:, u % 6, :], t_ada[(1, 0)[u // 8], u % 8]).then_inc(ada_land[u % 6], 16)
            pool.dma_start(ident[:, :], t_ident).then_inc(consts_in, 16)
            pool.dma_start(rope[:, :], t_rope).then_inc(consts_in, 16)
            pool.dma_start(sink[:, 0, :], t_sink.to_broadcast([P, A_HEADS])).then_inc(sink_in, 16)

            pool.wait_ge(mod_ready, 2)
            pool.memset(u_pad[:, :, 0:PAD], 0.0).then_inc(margins, 1)
            for k in range(2):
                pool.dma_start(ada_g[k][:, :], t_ada[ADA_LATE[0], k]).then_inc(ada_g_land[k], 16)
            for k in range(1, CONV_K):
                pool.wait_ge(conv_prod, k + 1)
                if k > 1:
                    pool.wait_ge(conv_step_p, k - 1)
                pool.tensor_tensor(c_acc[:, CT - 1, :], c_acc[:, CT - 1, :], sq[:, k % 2, :], ALU.add).then_inc(conv_step_p, 1)
            def load_rel(h):
                pool.dma_start(rel[:, h % 2, 0:TOK - CHUNK], t_rel[h][:, 0:TOK - CHUNK]).then_inc(rel_in[h % 2], 16)
                pool.dma_start(rel[CHUNK:P, h % 2, TOK - CHUNK:TOK], t_rel[h][CHUNK:P, TOK - CHUNK:TOK]).then_inc(rel_in[h % 2], 16)

            pool.memset(rel[0:CHUNK, :, TOK - CHUNK:TOK], MASKED).then_inc(rel_ready, 1)
            load_rel(0)
            load_rel(1)
            for k in range(KT):
                pool.wait_ge(ada_g_prod, k + 1)
                if k:
                    if k > 1:
                        pool.wait_ge(ada_g_used, k - 1)
                    pool.tensor_tensor(acc_g[:, :], acc_g[:, :], ada_g[k % 2][:, :], ALU.add).then_inc(ada_g_used, 1)
                    pool.wait_ge(ada_g_used, k)
                if k + 2 < KT:
                    pool.dma_start(ada_g[k % 2][:, :], t_ada[ADA_LATE[0], k + 2]).then_inc(ada_g_land[k % 2], 16)
            pool.dma_start(ada_p[:, :], t_ada[ADA_LATE[1], 0]).then_inc(ada_p_land, 16)
            for h in range(H1):
                pool.wait_ge(ada_p_prod, h + 1)
                if h + 1 < KT:
                    pool.dma_start(ada_p[:, :], t_ada[ADA_LATE[1], h + 1]).then_inc(ada_p_land, 16)
                if h:
                    if h > 1:
                        pool.wait_ge(ada_p_used, h - 1)
                    pool.tensor_tensor(acc_p[:, :], acc_p[:, :], ada_q, ALU.add).then_inc(ada_p_used, 1)
                if h + 2 < H1:
                    pool.wait_ge(m_ready, NT * (h + 1))
                    load_rel(h + 2)
            n_late = len(ada_b)

            def add_square(name, k):
                if 1 <= k <= KT - 2:
                    q = SQ[name] + k
                    pool.wait_ge(sq_ready, q + 1)
                    pool.wait_ge(sq_used, q - 1)
                    pool.tensor_tensor(sq[:, 0, :], sq[:, 0, :], sq[:, 1, :], ALU.add).then_inc(sq_used, 1)

            for u in range(16):
                if u == 0:
                    pool.wait_ge(lin_done, LT["o1"] + H1)
                if u == 5:
                    pool.wait_ge(R["cv"], CT)
                if u >= n_late:
                    pool.wait_ge(ada_used, 16 + u - n_late + 1)
                pool.dma_start(ada_b[u % n_late][:, :], t_ada[ADA_LATE[2 + u // 8], u % 8]).then_inc(ada_land[6 + u % n_late], 16)
                if u == KT + n_late - 1:
                    pool.wait_ge(R["y"], KT)
                    pool.dma_start(x[:, :, :], t_x).then_inc(x_in, 16)
            for k in range(KT):
                add_square("mix", k)
            pool.wait_ge(ada_used, 32)
            pool.wait_ge(R["y_f"], KT)
            pool.memset(u_ff[:, :, 0:U0], 0.0).then_inc(margins, 1)

            def pair_lo(pair, hi, lo, i, first, ready):
                pool.wait_ge(o_hi, first + i + 1)
                pool.tensor_tensor(lo[:, i, :], pair[:, i % 2, :], hi[:, i, :].bitcast(F32), ALU.subtract).then_inc(ready, 1)
                pool.wait_ge(ready, i + 1)

            for layer in range(2):
                if layer == 0:
                    pool.wait_ge(R["x_ffn"], KT)
                    pool.dma_start(rope_k[:, :], t_rope_k).then_inc(R["rope_k"], 16)
                    for h in range(A_HEADS):
                        if h >= 5 and h % 2:
                            pair_lo(o_pair2, b_hi, b_lo, (h - 5) // 2, 0, R["o2"])
                        if h >= 2:
                            pool.wait_ge(m_ready, attn2.n0 + NT * (h - 1))
                        pool.dma_start(alibi[:, h % 2, :], t_alibi[h]).then_inc(alibi_in[h % 2], 16)
                    for i in range(A_HEADS // 2 - 2, A_HEADS // 2):
                        pair_lo(o_pair2, b_hi, b_lo, i, 0, R["o2"])
                else:
                    for g in range(16):
                        pool.wait_ge(R["q_t"], g + 1)
                        pool.tensor_tensor(q3_f[64:96, :], q3_f[64:96, :], q3_r[64:96, :], ALU.add).then_inc(R["q_r"], 1)
                        if g % 2:
                            n = CH[f"b_h{g // 8}"] + g % 8 // 2 + WEIGHT_LEAD
                            pool.wait_ge(w_hi_done, n + 1)
                            pool.wait_ge(w_lo_done, n)
                            pool.wait_ge(R["q_r"], g + 1)
                            pool.tensor_tensor(w_lo[:, n % SLOTS, :], w_raw[:, n % RAW, :], w_hi[:, n % SLOTS, :].bitcast(F32),
                                               ALU.subtract).then_inc(w_lo_done, 1)
                            pool.wait_ge(w_lo_done, n + 1)
                        else:
                            pool.wait_ge(R["q_r"], g + 1)
                        i0 = g // 8 * 4
                        for i in {4: (0,), 6: (1,), 7: (2, 3)}.get(g % 8, ()):
                            pair_lo(o_pair3, a_hi, a_lo, i0 + i, A_HEADS // 2, R["o3"])
                pool.wait_ge((R["o2"], R["o3"])[layer], 8)
                pool.dma_start(p_raw[:, :, :], t_p[layer]).then_inc(p_in, 16)
                for stage in ("out", "gate"):
                    for k in range(KT):
                        add_square(f"{'ab'[layer]}_{stage}", k)

        @block.tensor
        def _(pe):
            events, squares = [0], [0]

            def mm3(o, w, r, start, stop, skip=False):
                pe.matmul(o, w[0], r[0], start=start, stop=False, skip_group_check=skip)
                pe.matmul(o, w[0], r[1], start=False, stop=False, skip_group_check=skip)
                return pe.matmul(o, w[1], r[0], start=False, stop=stop, skip_group_check=skip)

            def weights(n):
                pe.wait_ge(w_lo_done, n + 1)
                return w_hi[:, n % SLOTS, :], w_lo[:, n % SLOTS, :]

            def free_bank(tile):
                if tile >= LIN:
                    s, val = (R["y_d"], KT) if n_up <= tile < n_up + LIN else evicted[tile - LIN]
                    pe.wait_ge(s, val)
                return ps[:, tile % LIN, :]

            def cols(w, at, width=P):
                return tuple(part[:, at:at + width] for part in w)

            def tiles(name, n, src, ready=None, base=0, kt=KT, per=1, between=None):
                for f in range(n):
                    o = free_bank(LT[name] + f)
                    w = weights(CH[name] + f // per)
                    for k in range(kt):
                        if ready is not None:
                            pe.wait_ge(ready, base + k + 1)
                        m = mm3(o, cols(w, P * (f % per * kt + k)), (src[0][:, k, :], src[1][:, k, :]), k == 0, k == kt - 1)
                    m.then_inc(lin_done, 1)
                    if between is not None:
                        between(f)

            def token_tiles(tile, chunk, n_chunks, src, width, kt):
                banks = [free_bank(tile + t) for t in range(NT)]
                per = kt // n_chunks
                for j in range(n_chunks):
                    w = weights(chunk + j)
                    for kk in range(per):
                        k = j * per + kk
                        for t in range(NT):
                            m = mm3(banks[t][:, 0:width], (src[0][:, k, P * t:P * t + P], src[1][:, k, P * t:P * t + P]),
                                    cols(w, kk * width, width), k == 0, k == kt - 1)
                            if k == kt - 1:
                                m.then_inc(lin_done, 1)
                            elif kk == per - 1 and t == NT - 1:
                                m.then_inc(v_step, 1)

            def begin_event():
                if events[0]:
                    pe.wait_ge(stat_free, events[0])
                events[0] += 1

            def square_sum(k, n):
                if k == 0:
                    begin_event()
                q = squares[0]
                pe.wait_ge(sq_ready, q + 1)
                pe.matmul(ps[:, STAT_BANK, :], ones[:, :], sq[:, q % 2, :], start=(k == 0), stop=(k == n - 1)).then_inc(sq_used, 1)
                squares[0] += 1

            def added_squares(name):
                q = squares[0]
                assert q == SQ[name]
                begin_event()
                pe.wait_ge(sq_used, q + KT - 2)
                pe.matmul(ps[:, STAT_BANK, :], ones[:, :], sq[:, 0, :], start=True, stop=False).then_inc(sq_used, 1)
                pe.wait_ge(sq_ready, q + KT)
                pe.matmul(ps[:, STAT_BANK, :], ones[:, :], sq[:, 1, :], start=False, stop=True).then_inc(sq_used, 1)
                squares[0] += KT

            def mod_group(g, acc):
                pe.wait_ge(*((ada_g_used, KT - 1) if g == 2 else (ada_p_used, KT - 1) if g == 3 else
                             (ada_used, KT * (g + 1 if g < 2 else g - 1))))
                if g:
                    pe.wait_ge(mod_ready, g)
                for j in range(KT):
                    m = pe.matmul(ps[:, MOD_BANK, j:j + 1], acc[:, P * j:P * j + P], ones[:, 0:1], start=True, stop=True)
                m.then_inc(mod_sum, 1)

            def scores(a, h, t):
                n = a.n0 + NT * h + t
                if n >= n2 + 2:
                    pe.wait_ge(s_free, n - n2 - 1)
                elif n >= 2:
                    pe.wait_ge(m_ready, n - 1)
                b, e = a.spans[t]
                q, k = a.q(h), a.k(h)
                mm3(ps[:, S_BANK + n % 2, 0:P * (e - b)], cols(q, P * t), cols(k, P * b, P * (e - b)), True, True).then_inc(s_done, 1)

            def turn(a, h, t):
                n = a.n0 + NT * h + t
                if n >= n2:
                    pe.wait_ge(p_ready_act, n2 // 2 + n - n2 + 1)
                elif n % 2 == 1:
                    pe.wait_ge(p_ready_act, n // 2 + 1)
                else:
                    pe.wait_ge(p_ready, n // 2 + 1)
                if n >= 2:
                    pe.wait_ge(pt_ready, n - 1)
                b, e = a.spans[t]
                for s in range(b, e):
                    m = pe.transpose(ps[:, T_BANK + n % 2, P * s:P * s + P], a.p[:, n % 4, a.p_at + P * (s - b):a.p_at + P * (s - b) + P], ident[:, :])
                m.then_inc(t_done, 1)

            def values(a, h, part, keys_half=None):
                if keys_half != 1:
                    pe.wait_ge(pt_ready, a.n0 + NT * h + 2 * (part + 1))
                    if part == 0:
                        free_bank(a.lin(h))
                o = ps[:, a.lin(h) % LIN, :]
                keys = a.over_keys[part]
                for i, (s, t0, t1) in enumerate(keys):
                    if keys_half is None or i // 2 == keys_half:
                        r = tuple(pt[:, s, P * t0:P * t1] for pt in a.pt)
                        m = mm3(o[:, P * t0:P * t1], a.v(h, s), r, i == 0, i == len(keys) - 1, skip=True)
                if keys_half != 0:
                    m.then_inc((v_half, lin_done)[part], 1)

            def attention(a, before=None, after=None):
                pe.wait_ge(stat_free, events[0])
                for i in range(NT * a.heads + NT + 1):
                    h, t = divmod(i, NT)
                    if h < a.heads:
                        if t == 0 and before is not None:
                            before(h)
                        scores(a, h, t)
                    if 0 <= i - 3 < NT * a.heads:
                        turn(a, *divmod(i - 3, NT))
                    if a not in attn3:
                        if t == 2 and 1 <= h <= a.heads:
                            values(a, h - 1, 0)
                        if t == 0 and 2 <= h <= a.heads + 1:
                            values(a, h - 2, 1)
                    if after is not None:
                        after(h, t)

            A, B = (a_hi, a_lo), (b_hi, b_lo)

            pe.wait_ge(ones_set, 1)
            for k in range(KT):
                square_sum(k, KT)
            mod_group(0, acc_a[:, 0, :])
            mod_group(1, acc_a[:, 1, :])
            tiles("glu", 8, A, R["h1"])
            tiles("qk", 8, A)
            token_tiles(LT["v"], CH["v"], 4, A, D_ATTN, KT)

            def conv_norm(f):
                if f == 9:
                    pe.wait_ge(conv_step, CONV_K * (CT - 1))
                    pe.wait_ge(conv_step_p, CONV_K - 1)
                    pe.wait_ge(stat_free, events[0])
                    for k in range(CT):
                        m = pe.matmul(ps[:, STAT_BANK, :], ones[:, :], c_acc[:, k, :], start=(k == 0), stop=(k == CT - 1))
                    m.then_inc(R["ln_sum"], 1)
                if f == 12:
                    pe.wait_ge(R["ln_mean"], CT)
                    for k in range(CT):
                        square_sum(k, CT)

            tiles("gates", 2 * KT, A, between=conv_norm)
            mod_group(2, acc_g)
            pe.wait_ge(mod_ready, 3)
            pe.wait_ge(R["qk"], 8)
            pe.wait_ge(R["v"], NT)
            attention(attn1)
            pe.wait_ge(pt_ready, n1)
            pe.wait_ge(R["o1"], H1 // 2)
            mod_group(3, acc_p)
            for f in range(KT):
                w = weights(CH["ac"] + f)
                for j, src in enumerate(((qk_hi, qk_lo), (cv_hi, cv_lo))):
                    o = free_bank(LT["ac"] + 2 * f + j)
                    for k in range(CT):
                        if j:
                            pe.wait_ge(R["cv"], k + 1)
                        m = mm3(o, cols(w, P * (CT * j + k)), (src[0][:, k, :], src[1][:, k, :]), k == 0, k == CT - 1)
                    m.then_inc(lin_done, 1)
            mod_group(4, acc_b)
            tiles("mix", KT, (y_hi, y_lo), R["y"])
            mod_group(5, acc_b)
            added_squares("mix")
            for k in range(KT):
                square_sum(k, KT)
            with pe.Fori(0, FT // 2) as i:
                for j in range(4):
                    tile, n = LT["up"] + j, CH["up"] + j
                    pe.wait_ge(w_lo_done, i * 4 + (n + 1))
                    pe.wait_ge((R["u_val"], R["u_gate"])[j % 2], i * 2 + (up_free + j // 2 - 1))
                    w = w_hi[:, n % SLOTS, :], w_lo[:, n % SLOTS, :]
                    for k in range(KT):
                        if j == 0:
                            pe.wait_ge(R["h2"], k + 1)
                        m = mm3(ps[:, tile % LIN, :], cols(w, P * k), (a_hi[:, k, :], a_lo[:, k, :]), k == 0, k == KT - 1)
                    m.then_inc(lin_done, 1)
            pe.wait_ge(R["u_val"], up_free + FT)
            pe.wait_ge(R["u_gate"], up_free + FT)

            def down(k, n, slot, start, stop, ready):
                pe.wait_ge(w_lo_done, n)
                pe.wait_ge(R["g"], ready)
                w = w_hi[:, slot, :], w_lo[:, slot, :]
                r = (g_hi[:, k, :], g_lo[:, k, :]) if isinstance(k, int) else tuple(
                    g.rearrange("p k n -> p (k n)")[:, bass.ds(k, TOK)] for g in (g_hi, g_lo))
                for f in range(KT):
                    m = mm3(ps[:, f, :], cols(w, P * f), r, start, stop)
                m.then_inc(down_step, 1)

            for k in range(2):
                down(k, CH["down"] + k + 1, (CH["down"] + k) % SLOTS, k == 0, False, k + 1)
            turns = (FT - 2) // 4
            with pe.Fori(0, turns - 1) as i:
                for j in range(4):
                    n = CH["down"] + 2 + j
                    down(i * (4 * TOK) + (2 + j) * TOK, i * 4 + (n + 1), n % SLOTS, False, False, i * 4 + (3 + j))
            for k in range(FT - 4, FT):
                down(k, CH["down"] + k + 1, (CH["down"] + k) % SLOTS, False, k == FT - 1, k + 1)
            for k in range(KT):
                if k == 0:
                    pe.wait_ge(R["y_d"], 1)
                square_sum(k, KT)
            pe.wait_ge(R["y_d"], KT)
            for k in range(KT):
                square_sum(k, KT)

            tiles("a_q", KT, A, R["in_a"])
            tiles("a_k", 2, A)
            tiles("a_z", KT, A)
            pe.wait_ge(rs_ready, 6)
            begin_event()
            for t in range(NT):
                m = pe.transpose(ps[:, STAT_BANK, P * t:P * t + P], rs[:, 5 % 3, P * t:P * t + P], ident[:, :])
            m.then_inc(R["rcol_t"], 1)
            token_tiles(LT["a_v"], CH["a_v"], 2, A, 256, KT)
            pe.wait_ge(R["q_a"], KT)
            pe.wait_ge(R["k_a"], 2)
            pe.wait_ge(R["v_a"], NT)
            attention(attn2)

            def rest(l, src, after, o_ready):
                pe.wait_ge(pt_ready, n2 if l == "a" else n2 + 16 * NT)
                pe.wait_ge(o_ready, 8)
                tiles(l + "_out", KT, src)
                added_squares(l + "_out")
                base = 0 if l == "a" else PT_K
                tiles(l + "_ple", KT, (p_hi, p_lo), R["p"], base, kt=PT_K, per=4)
                tiles(l + "_gate", KT, after, R["in_g"], 0 if l == "a" else KT)

            rest("a", B, A, R["o2"])

            tiles("b_c", 6, B, R["in_b"], between=lambda f: added_squares("a_gate") if f == 0 else None)

            def lora_norms(f):
                if f < 2:
                    n = (QT, KVT)[f]
                    for k in range(n):
                        square_sum(k, n)

            tiles("b_z", KT, B, between=lora_norms)
            pe.wait_ge(R["cqn"], QT + KVT)
            pe.wait_ge(R["kr"], 3)
            for hf in range(2):
                a = attn3[hf]

                def project(tile, h, at, src, begin, end, n):
                    w = weights(CH[f"b_h{hf}"] + h // 2)
                    o = ps[:, tile % LIN, :]
                    if begin == 0:
                        free_bank(tile)
                    for k in range(begin, end):
                        m = mm3(o, cols(w, P * (at + k)), (src[0][:, k, :], src[1][:, k, :]), k == 0, k == n - 1, skip=True)
                    if end == n:
                        m.then_inc(lin_done, 1)

                def queries(h, begin=0, end=QT):
                    project(a.q_lin(h), h, h % 2 * QT, (cq_hi, cq_lo), begin, end, QT)

                def keys(h, begin=0, end=KVT):
                    project(a.k_lin(h), h, 2 * QT, (ck_hi, ck_lo), begin, end, KVT)

                def before(h):
                    pe.wait_ge(R["q_b"], 8 * hf + h + 1)
                    pe.wait_ge(R["k_b"], 8 * hf + h + 1)
                    if h == 0:
                        pe.wait_ge(R["v_b"], NT * (hf + 1))

                def after(h, t):
                    for kind, head, begin, end in mla_pieces(h, t):
                        if kind == "o":
                            values(a, head, begin // 2, begin % 2)
                        else:
                            (queries if kind == "q" else keys)(head, begin, end)

                keys(0)
                queries(0)
                token_tiles(LT[f"b_v{hf}"], CH[f"b_v{hf}"], 1, (ck_hi, ck_lo), TOK, KVT)
                queries(1)
                attention(a, before, after)
            rest("b", A, B, R["o3"])
            added_squares("b_gate")

        @block.scalar
        def _(act):
            tmps, sqs, rss, evs, prods = [0], [0], [0], [0], [0]

            def split(n):
                if n >= N_CHUNKS:
                    return
                act.wait_ge(w_land[n % RAW], 16 * (n // RAW + 1))
                if n >= SLOTS:
                    act.wait_ge(*used_at[n - SLOTS])
                act.activation(w_hi[:, n % SLOTS, :], w_raw[:, n % RAW, :], ACT.Copy).then_inc(w_hi_done, 1)

            def hi_of_tmp(dst, n=None):
                act.wait_ge(tmp_w, tmps[0] + 1)
                act.activation(dst, tmp[:, tmps[0] % 2, :] if n is None else tmp[:, tmps[0] % 2, 0:n], ACT.Copy).then_inc(hi_done, 1)
                tmps[0] += 1

            def square(src, s, val, added=None):
                act.wait_ge(s, val)
                q = sqs[0]
                if q >= 2:
                    act.wait_ge(sq_used, q - 1)
                slot = q % 2 if added is None else min(added, 1)
                act.activation(sq[:, slot, :], src, ACT.Square).then_inc(sq_ready, 1)
                sqs[0] += 1

            def rsqrt(n):
                act.wait_ge(sq_used, sqs[0])
                act.activation(rs[:, rss[0] % 3, :], ps[:, STAT_BANK, :], ACT.Ln, bias=EPS, scale=1.0 / n).then_inc(stat_free, 1)
                evs[0] += 1
                act.wait_ge(stat_free, evs[0])
                act.activation(rs[:, rss[0] % 3, :], rs[:, rss[0] % 3, :], ACT.Exp, scale=-0.5).then_inc(rs_ready, 1)
                rss[0] += 1

            def exps(a, h, t):
                n = a.n0 + NT * h + t
                b, e = a.spans[t]
                w, c = P * (e - b), n % 4
                act.wait_ge(m_ready, n + 1)
                least, total = col[:, 0, c:c + 1], col[:, 1, c:c + 1]
                if a in attn3:
                    act.wait_ge(t_done, n - 3)
                    act.activation(a.p[:, c, 0:w], ps[:, S_BANK + n % 2, 0:w], ACT.Exp, bias=least,
                                   accum_out=total).then_inc(s_free, 1)
                elif a is attn2:
                    act.activation(p2[:, c, 0:1 + w], minus_s[:, n % 2, 0:1 + w], ACT.Exp, bias=least, scale=-1.0,
                                   accum_out=total).then_inc(e_done, 1)
                else:
                    act.activation(p1[:, c, 0:w], p1[:, c, 0:w], ACT.Exp, bias=least, scale=-1.0,
                                   accum_out=total).then_inc(e_done, 1)

            def norms(a, n):
                if a not in attn3 and n % 2 == 0:
                    return
                b, e = a.spans[n % NT]
                p = a.p[:, n % 4, a.p_at:a.p_at + P * (e - b)]
                act.wait_ge(r_ready, n + 1)
                act.activation(p, p, ACT.Copy, scale=col[:, 2, n % 4:n % 4 + 1]).then_inc(p_ready_act, 1)

            def turn_hi(a, h, t):
                n = a.n0 + NT * h + t
                b, e = a.spans[t]
                act.wait_ge(t_done, n + 1)
                if t == 0 and h:
                    act.wait_ge(v_half, a.n0 // NT + h)
                if t == 2 and h:
                    act.wait_ge(lin_done, a.lin(h - 1) + 1)
                act.activation(a.pt[0][:, b:e, P * t:P * t + P],
                               ps[:, T_BANK + n % 2, P * b:P * e].rearrange("p (s q) -> p s q", q=P), ACT.Copy).then_inc(pt_hi_done, 1)

            def attention(a, outs, after=None, first=None):
                for i in range(NT * a.heads + NT + 3):
                    h, t = divmod(i, NT)
                    if first is not None:
                        first(h, t)
                    if 0 <= i - 3 < NT * a.heads:
                        turn_hi(a, *divmod(i - 3, NT))
                    if h < a.heads:
                        exps(a, h, t)
                    if 0 <= i - 1 < NT * a.heads:
                        norms(a, a.n0 + i - 1)
                    if after is not None:
                        after(h, t)
                    if t == 2 and h >= 3 and h % 2 == 1:
                        outs(h // 2 - 1)

            def outs_of(bufs):
                return lambda i: hi_of_tmp(bufs[:, i, :])

            def pairs_of(pair, hi, first, base):
                def hi_part(i):
                    act.wait_ge(o_full, first + base + i + 1)
                    act.activation(hi[:, base + i, :], pair[:, (base + i) % 2, :], ACT.Copy).then_inc(o_hi, 1)
                return hi_part

            act.wait_ge(vecs_in, 16)
            act.activation(c_act[:, KT:2 * KT], v("c", 0, KT), ACT.Sigmoid).then_inc(sig_c, 1)
            for n in range(WEIGHT_LEAD - 1):
                split(n)
            for k in range(KT):
                square(x[:, k, :], x_in, 16)
            rsqrt(D)
            split(WEIGHT_LEAD - 1)
            for k in range(KT):
                act.wait_ge(tmp_w, tmps[0] + 1)
                act.activation(a_hi[:, k, :], tmp[:, tmps[0] % 2, :], ACT.Identity, bias=mod[:, k:k + 1]).then_inc(hi_done, 1)
                tmps[0] += 1
            for f in range(CT):
                for j in range(2):
                    split(CH["glu"] + 2 * f + j + WEIGHT_LEAD)
                act.wait_ge(lin_done, LT["glu"] + 2 * f + 2)
                if f:
                    act.wait_ge(R["glu"], f)
                act.activation(sig[:, :], ps[:, (LT["glu"] + 2 * f + 1) % LIN, :], ACT.Sigmoid,
                               bias=v("b_in", BI_GB + f)).then_inc(R["glu_sig"], 1)
            def conv_products(n):
                for k in range(prods[0], min(prods[0] + n, CONV_K)):
                    src, w = u_pad[:, CT - 1, k:k + TOK], v("w_dw", k * CT + CT - 1)
                    if k == 0:
                        act.wait_ge(R["glu"], CT)
                        act.activation(c_acc[:, CT - 1, :], src, ACT.Identity, bias=v("b_dw", CT - 1), scale=w).then_inc(conv_prod, 1)
                    else:
                        if k > 2:
                            act.wait_ge(conv_step_p, k - 2)
                        act.activation(sq[:, k % 2, :], src, ACT.Copy, scale=w).then_inc(conv_prod, 1)
                    prods[0] = k + 1

            for f in range(8):
                split(CH["qk"] + f + WEIGHT_LEAD)
                hi_of_tmp(qk_hi[:, f, :])
                conv_products(2)
            for j in range(4):
                split(CH["v"] + j + WEIGHT_LEAD)
                conv_products(2)
            for t in range(NT):
                act.wait_ge(lin_done, LT["v"] + t + 1)
                act.activation(v_hi[:, t, :], ps[:, (LT["v"] + t) % LIN, :], ACT.Copy).then_inc(hi_done, 1)
            for j in range(2 * KT):
                split(CH["gates"] + j + WEIGHT_LEAD)
                act.wait_ge(lin_done, LT["gates"] + j + 1)
                dst = x[:, j, :] if j < KT else gate_t[:, j - KT, :]
                act.activation(dst, ps[:, (LT["gates"] + j) % LIN, :], ACT.Sigmoid,
                               bias=v("b_in", BI_A + j)).then_inc(R["gate_sig"], 1)
                conv_products(2)
                if 5 <= j < 5 + KT:
                    k = j - 5
                    act.wait_ge(ada_g_land[k % 2], 16 * (k // 2 + 1))
                    act.activation(ada_g[k % 2][:, :] if k else acc_g[:, :], ada_g[k % 2][:, :], ACT.Copy,
                                   scale=c_act[:, k:k + 1]).then_inc(ada_g_prod, 1)
                if j == 11:
                    for k in range(CT):
                        square(c_acc[:, k, :], R["ln_mean"], k + 1)
                    rsqrt(D_CONV)
                if j == 13:
                    for k in range(CT):
                        act.wait_ge(R["cn"], k + 1)
                        if k >= 2:
                            act.wait_ge(R["cs"], k - 1)
                        act.activation(sq[:, k % 2, :], c_acc[:, k, :], ACT.Sigmoid, bias=v("b_ln", k),
                                       scale=v("g_ln", k)).then_inc(R["cn_sig"], 1)
            act.wait_ge(R["gate_sig"], 2 * KT)
            for k in range(KT):
                act.activation(gate_b[:, k, :], gate_t[:, k, :], ACT.Copy).then_inc(R["gate_sig"], 1)
            act.wait_ge(R["gate_sig"], 3 * KT)

            def ada_product(h, t):
                if t == 3 and h < KT:
                    act.wait_ge(ada_p_land, 16 * (h + 1))
                    if h == 1:
                        act.wait_ge(R["cs"], CT)
                    if h > 1:
                        act.wait_ge(ada_p_used, h - 1)
                    act.activation(ada_q if h else acc_p[:, :], ada_p[:, :], ACT.Copy,
                                   scale=c_act[:, h:h + 1]).then_inc(ada_p_prod, 1)

            attention(attn1, outs_of(qk_hi), ada_product)
            for k in range(CT):
                act.activation(cv_hi[:, k, :], c_acc[:, k, :], ACT.Copy).then_inc(hi_done, 1)
            for f in range(KT):
                split(CH["ac"] + f + WEIGHT_LEAD)
                hi_of_tmp(y_hi[:, f, :])
            for k in range(KT):
                split(CH["mix"] + k + WEIGHT_LEAD)
                square(y_f[:, k, :], R["y_f"], k + 1, k)
            rsqrt(D)
            for k in range(KT):
                square(x[:, k, :], R["x_mix"], k + 1)
            rsqrt(D)
            act.wait_ge(gains, 4)
            for k in range(KT):
                act.wait_ge(tmp_w, tmps[0] + 1)
                act.activation(a_hi[:, k, :], tmp[:, tmps[0] % 2, :], ACT.Identity,
                               bias=mod[:, 3 * KT + k:3 * KT + k + 1]).then_inc(hi_done, 1)
                tmps[0] += 1
            act.wait_ge(margins, 2)
            act.sem_inc(R["u_val"], up_free)
            act.sem_inc(R["u_gate"], up_free)
            t0 = tmps[0]
            with act.Fori(0, FT // 2) as i:
                for pair in range(2):
                    for j in range(2):
                        k = 2 * pair + j
                        n = CH["up"] + k + WEIGHT_LEAD
                        act.wait_ge(w_land[n % RAW], i * 32 + 16 * (n // RAW + 1))
                        act.wait_ge(lin_done, i * 4 + (LT["up"] + k))
                        act.activation(w_hi[:, n % SLOTS, :], w_raw[:, n % RAW, :], ACT.Copy).then_inc(w_hi_done, 1)
                    act.wait_ge(tmp_w, i * 2 + (t0 + pair))
                    for j, (c, s, b_at, w_at) in enumerate(((c_val, R["u_val"], 0, 0), (c_gate[:, :], R["u_gate"], FT, FT))):
                        bank = (LT["up"] + 2 * pair + j) % LIN
                        act.wait_ge(lin_done, i * 4 + (LT["up"] + 2 * pair + j + 1))
                        act.activation(c, ps[:, bank, :], ACT.Identity,
                                       bias=vecs[:, bass.ds(i * 2 + (VO["b_dwf"] + b_at + pair), 1)],
                                       scale=vecs[:, bass.ds(i * 2 + (VO["w_dwf"] + 2 * 2 * FT + w_at + pair), 1)])
                        act.activation(u_ff[:, 2 * pair + j, U0:U0 + TOK], ps[:, bank, :], ACT.Copy).then_inc(s, 1)
                    act.wait_ge(R["cf_gate"], i * 4 + (2 * pair + 2))
                    act.activation(gel, c_gate[:, :], ACT.Gelu_apprx_tanh).then_inc(R["gel"], 1)
                    act.wait_ge(tmp_w, i * 2 + (t0 + pair + 1))
                    act.activation(g_hi.rearrange("p k n -> p (k n)")[:, bass.ds(i * (2 * TOK) + pair * TOK, TOK)],
                                   tmp[:, (t0 + pair) % 2, :], ACT.Copy).then_inc(hi_done, 1)
            tmps[0] += FT
            for k in range(3):
                split(CH["down"] + k + WEIGHT_LEAD)
            with act.Fori(0, (FT - 6) // 4) as i:
                for j in range(4):
                    n = CH["down"] + 3 + j + WEIGHT_LEAD
                    act.wait_ge(w_land[n % RAW], i * 32 + 16 * (n // RAW + 1))
                    act.wait_ge(down_step, i * 4 + (3 + j))
                    act.activation(w_hi[:, n % SLOTS, :], w_raw[:, n % RAW, :], ACT.Copy).then_inc(w_hi_done, 1)
            for k in range(3 + (FT - 6) // 4 * 4, FT):
                split(CH["down"] + k + WEIGHT_LEAD)
            for k in range(KT):
                square(y_d[:, KT - 1 - k, :], R["y_d"], k + 1)
            rsqrt(D)

            def scaled_input(hi, gain, k, s, val, added=None):
                square(x[:, k, :], s, val, added)
                act.activation(hi[:, k, :], x[:, k, :], ACT.Identity, scale=v(gain, k)).then_inc(hi_done, 1)

            for k in range(KT):
                scaled_input(a_hi, "norm_a", k, R["x_ffn"], k + 1)
            rsqrt(D)
            for f in range(KT):
                split(CH["a_q"] + f + WEIGHT_LEAD)
                hi_of_tmp(b_hi[:, f, :])
            for f in range(2):
                split(CH["a_k"] + f + WEIGHT_LEAD)
                hi_of_tmp(ka_hi[:, f, :])
            for f in range(KT):
                split(CH["a_z"] + f + WEIGHT_LEAD)
                act.wait_ge(R["z_t"], f + 1)
                if f:
                    act.wait_ge(R["z_a"], f)
                act.activation(zs[:, :], z2[:, f, :], ACT.Sigmoid).then_inc(R["z_sig"], 1)
            for f in range(2):
                split(CH["a_v"] + f + WEIGHT_LEAD)
            evs[0] += 1
            for t in range(NT):
                hi_of_tmp(va_hi[:, t, :], 256)
            act.wait_ge(sink_in, 16)
            attention(attn2, pairs_of(o_pair2, b_hi, 0, 0))

            def rest(l, after, nxt):
                i = 0 if l == "a" else 1
                for k in range(KT):
                    split(CH[l + "_out"] + k + WEIGHT_LEAD)
                    scaled_input(after, f"ple_g{i}", k, R["x_attn"], KT * i + k + 1, k)
                    if k == KT // 2:
                        act.wait_ge(p_in, 16 * (i + 1))
                        for kk in range(PT_K):
                            act.activation(p_hi[:, kk, :], p_raw[:, kk, :], ACT.Copy).then_inc(hi_done, 1)
                rsqrt(D)
                for k in range(2):
                    split(CH[l + "_ple"] + k + WEIGHT_LEAD)
                for k in range(KT):
                    split(CH[l + "_gate"] + k + WEIGHT_LEAD)
                    act.wait_ge(R["gt"], KT * i + k + 1)
                    act.activation(gs2[:, k % 2, :], gs2[:, k % 2, :], ACT.Sigmoid).then_inc(R["gsig"], 1)
                    if nxt is not None:
                        scaled_input(nxt, "norm_b", k, R["x_ple"], KT * i + k + 1, k)
                    else:
                        square(x[:, k, :], R["x_ple"], KT * i + k + 1, k)
                rsqrt(D)

            rest("a", a_hi, b_hi)
            for f in range(QT + KVT + 1):
                split(CH["b_c"] + f + WEIGHT_LEAD)
            for f in range(QT + KVT):
                square(cq_f[:, f, :], R["cq"], f + 1)
                if f == QT - 1:
                    rsqrt(Q_LORA)
            rsqrt(KV_LORA)
            for f in range(2):
                split(CH["b_z"] + f + WEIGHT_LEAD)
            act.wait_ge(R["kr_sum"], 1)
            for b in range(2):
                act.activation(k3_hi[64:96, b, :], kr_f[64:96, :], ACT.Copy).then_inc(hi_done, 1)
            for k in range(QT + KVT):
                hi_of_tmp(cq_hi[:, k, :] if k < QT else ck_hi[:, k - QT, :])
                if k == QT - 1:
                    split(CH["b_z"] + 2 + WEIGHT_LEAD)
            for f in range(KT):
                if f >= 3:
                    split(CH["b_z"] + f + WEIGHT_LEAD)
                act.wait_ge(R["z_tb"], f + 1)
                if f:
                    act.wait_ge(R["z_b"], f)
                act.activation(zs3[:, :], z3[:, f, :], ACT.Sigmoid).then_inc(R["z_sigb"], 1)
            for hf in range(2):
                a = attn3[hf]
                split(CH[f"b_v{hf}"] + WEIGHT_LEAD)

                def key_hi(h):
                    src = ps[64 * (h % 2):64 * (h % 2) + 64, a.k_lin(h - h % 2) % LIN, :]
                    act.wait_ge(lin_done, a.k_lin(h - h % 2) + 1)
                    if h >= 2:
                        act.wait_ge(s_done, a.n0 + NT * (h - 1))
                    if h % 2:
                        act.wait_ge(R["k_b"], 8 * hf + h)
                    act.activation(k3_hi[0:64, h % 2, :], src, ACT.Copy).then_inc(hi_done, 1)

                def query_hi(h):
                    act.wait_ge(R["q_r"], 8 * hf + h + 1)
                    if h >= 2:
                        act.wait_ge(s_done, a.n0 + NT * (h - 1))
                    act.activation(q3_hi[0:96, h % 2, :], q3_f[0:96, :], ACT.Copy).then_inc(hi_done, 1)
                    if h % 2:
                        split(CH[f"b_h{hf}"] + h // 2 + WEIGHT_LEAD)

                def first(h, t):
                    if t == 0 and h % 2 == 0 and 2 <= h <= 6:
                        key_hi(h + 1)

                def after(h, t):
                    if t == 2 - h % 2 and 1 <= h <= 6:
                        query_hi(h + 1)
                    if t == 2 and h % 2 == 1 and h + 1 < 8:
                        key_hi(h + 1)

                key_hi(0)
                key_hi(1)
                query_hi(0)
                for t in range(NT):
                    act.wait_ge(lin_done, LT[f"b_v{hf}"] + t + 1)
                    act.activation(vb_hi[:, t, :], ps[:, (LT[f"b_v{hf}"] + t) % LIN, :], ACT.Copy).then_inc(hi_done, 1)
                query_hi(1)
                attention(a, pairs_of(o_pair3, a_hi, A_HEADS // 2, 4 * hf), after, first)
            rest("b", b_hi, None)

        @block.vector
        def _(dve):
            tmps, his, lin, steps, taps, units, rss, evs = [0], [0], [0], [0], [0], [0], [0], [0]

            def split(n):
                if n >= N_CHUNKS:
                    return
                dve.wait_ge(w_hi_done, n + 1)
                dve.tensor_tensor(w_lo[:, n % SLOTS, :], w_raw[:, n % RAW, :], w_hi[:, n % SLOTS, :].bitcast(F32),
                                  ALU.subtract).then_inc(w_lo_done, 1)

            def step(ins):
                steps[0] += 1
                ins.then_inc(dve_step, 1)
                dve.wait_ge(dve_step, steps[0])

            def lo(dst, src, hi, ready):
                his[0] += 1
                dve.wait_ge(hi_done, his[0])
                return dve.tensor_tensor(dst, src, hi.bitcast(F32), ALU.subtract).then_inc(ready, 1)

            def tmp_slot():
                tmps[0] += 1
                return tmp[:, (tmps[0] - 1) % 2, :]

            def lo_of_tmp(dst, hi, ready, n=TOK):
                lo(dst, tmp[:, (tmps[0] - 1) % 2, 0:n], hi, ready)

            def bank(tile):
                dve.wait_ge(lin_done, tile + 1)
                return ps[:, tile % LIN, :]

            def wait_rs():
                rss[0] += 1
                dve.wait_ge(rs_ready, rss[0])
                return rs[:, (rss[0] - 1) % 3, :]

            def mod_unit():
                u = units[0]
                units[0] += 1
                late = u - 16
                slot, turn = (u % 6, u // 6) if late < 0 else (6 + late % len(ada_b), late // len(ada_b))
                src = ada_a[:, u % 6, :] if late < 0 else ada_b[late % len(ada_b)][:, :]
                acc = acc_a[:, u // 8, :] if u < 16 else acc_b[:, :]
                dve.wait_ge(ada_land[slot], 16 * (turn + 1))
                k = u % 8
                if k == 0:
                    if u >= 24:
                        dve.wait_ge(mod_sum, u // 8 + 2)
                    dve.tensor_scalar(acc, src, c_act[:, 0:1], None, ALU.mult).then_inc(ada_used, 1)
                else:
                    dve.wait_ge(ada_used, u)
                    dve.scalar_tensor_tensor(acc, src, c_act[:, k:k + 1], acc, ALU.mult, ALU.add).then_inc(ada_used, 1)

            def mod_group(g):
                grp = (1, 0, *ADA_LATE)[g]
                dve.wait_ge(mod_sum, g + 1)
                dve.tensor_tensor(mod[:, KT * grp:KT * grp + KT], ps[:, MOD_BANK, 0:KT], v("b_ada", KT * grp, KT),
                                  ALU.add).then_inc(mod_ready, 1)

            def gain(i, name, grp, add):
                dve.scalar_tensor_tensor(gvec[:, KT * i:KT * i + KT], mod[:, KT * grp:KT * grp + KT], add, v(name, 0, KT),
                                         ALU.add, ALU.mult).then_inc(gains, 1)

            def conv_taps(n):
                for _ in range(n):
                    i = taps[0]
                    if i == CONV_K * (CT - 1):
                        return
                    taps[0] += 1
                    k, f = divmod(i, CT - 1)
                    src, w = u_pad[:, f, k:k + TOK], v("w_dw", k * CT + f)
                    if k == 0:
                        dve.tensor_scalar(c_acc[:, f, :], src, w, v("b_dw", f), ALU.mult, ALU.add).then_inc(conv_step, 1)
                    else:
                        dve.wait_ge(conv_step, i - CT + 2)
                        dve.scalar_tensor_tensor(c_acc[:, f, :], src, w, c_acc[:, f, :], ALU.mult, ALU.add).then_inc(conv_step, 1)

            def maxima(a, h, t):
                n = a.n0 + NT * h + t
                b, e = a.spans[t]
                w, c = P * (e - b), n % 4
                s = ps[:, S_BANK + n % 2, 0:w]
                dve.wait_ge(s_done, n + 1)
                if a in attn3:
                    dve.tensor_reduce(col[:, 0, c:c + 1], s, AX.X, ALU.max, negate=True).then_inc(m_ready, 1)
                    return
                if a is attn1:
                    if n >= 4:
                        dve.wait_ge(t_done, n - 3)
                    if t == 0:
                        if h == 0:
                            dve.wait_ge(rel_ready, 1)
                        dve.wait_ge(rel_in[h % 2], 32 * (h // 2 + 1))
                    bias, least, dst = rel[:, h % 2, TOK - w:TOK], -LOWEST, p1[:, c, 0:w]
                else:
                    g = head_order()[h]
                    if t == 0:
                        dve.wait_ge(alibi_in[h % 2], 16 * (h // 2 + 1))
                    off = P * (b - t + 1)
                    bias, least, dst = alibi[:, h % 2, off:off + w], sink[:, 1, g:g + 1], minus_s[:, n % 2, 1:1 + w]
                    if t < 2:
                        if t == 1 or h:
                            dve.wait_ge(e_done, n - 1)
                        dve.tensor_copy(minus_s[:, n % 2, 0:1], least)
                dve.tensor_tensor_reduce(dst, s, bias, -1.0, least, ALU.add, ALU.min, col[:, 0, c:c + 1]).then_inc(m_ready, 1)

            def inverse(a, n):
                c = n % 4
                dve.wait_ge(*((s_free, n - n2 + 1) if a in attn3 else (e_done, n + 1)))
                dve.reciprocal(col[:, 2, c:c + 1], col[:, 1, c:c + 1]).then_inc(r_ready, 1)

            def norms(a, n):
                if a in attn3 or n % 2 == 1:
                    return
                b, e = a.spans[n % NT]
                p = a.p[:, n % 4, a.p_at:a.p_at + P * (e - b)]
                dve.wait_ge(r_ready, n + 1)
                dve.tensor_scalar(p, p, col[:, 2, n % 4:n % 4 + 1], None, ALU.mult).then_inc(p_ready, 1)

            def turn_lo(a, h, t):
                n = a.n0 + NT * h + t
                b, e = a.spans[t]
                dve.wait_ge(pt_hi_done, n + 1)
                dve.tensor_tensor(a.pt[1][:, b:e, P * t:P * t + P],
                                  ps[:, T_BANK + n % 2, P * b:P * e].rearrange("p (s q) -> p s q", q=P),
                                  a.pt[0][:, b:e, P * t:P * t + P].bitcast(F32), ALU.subtract).then_inc(pt_ready, 1)

            def attention(a, outs, after=None, first=None):
                half_out, pair_lo = outs
                last = NT * a.heads
                for i in range(last + NT + NT):
                    h, t = divmod(i, NT)
                    if first is not None:
                        first(h, t)
                    if h < a.heads:
                        maxima(a, h, t)
                    if 0 <= i - 1 < last:
                        inverse(a, a.n0 + i - 1)
                    if 0 <= i - 3 < last:
                        turn_lo(a, *divmod(i - 3, NT))
                    if 0 <= i - 1 < last:
                        norms(a, a.n0 + i - 1)
                    if t == 1 and 2 <= h < a.heads + 2:
                        half_out(h - 2)
                    if after is not None:
                        after(h, t)
                    if pair_lo is not None and t == 3 and h >= 3 and h % 2 == 1:
                        pair_lo(h - 2)

            def outs_of(a, op, hi, lo_, half_sem, ready, base=0):
                def half_out(h):
                    rows = half(h)
                    m = op(h, rows, tmp[rows, tmps[0] % 2, :], bank(a.lin(h))[rows, :])
                    if h % 2 == 0:
                        m.then_inc(half_sem, 1)
                    else:
                        m.then_inc(tmp_w, 1)
                        tmps[0] += 1

                def pair_lo(h):
                    lo_of_tmp(lo_[:, base + h // 2, :], hi[:, base + h // 2, :], ready)

                return half_out, pair_lo

            dve.wait_ge(vecs_in, 16)
            dve.wait_ge(sig_c, 1)
            step(dve.tensor_tensor(c_act[:, 0:KT], v("c", 0, KT), c_act[:, KT:2 * KT], ALU.mult))
            for u in range(16):
                mod_unit()
                if u in (0, 2, 15):
                    split((0, 2, 15).index(u))
            mod_group(0)
            dve.wait_ge(mod_ready, 1)
            gain(0, "g_pre_mix", 1, 1.0)
            mod_group(1)
            r = wait_rs()
            dve.wait_ge(gains, 1)
            dve.wait_ge(mod_ready, 2)

            def modulated(r, i, grp, ready):
                for k in range(KT + 1):
                    if 2 <= k < KT:
                        dve.wait_ge(ready, k - 1)
                    if k < KT:
                        dve.scalar_tensor_tensor(tmp_slot(), x[:, k, :], gvec[:, KT * i + k:KT * i + k + 1], r, ALU.mult,
                                                 ALU.mult).then_inc(tmp_w, 1)
                    if k:
                        his[0] += 1
                        dve.wait_ge(hi_done, his[0])
                        dve.scalar_tensor_tensor(a_lo[:, k - 1, :], tmp[:, (tmps[0] - (2 if k < KT else 1)) % 2, :],
                                                 mod[:, KT * grp + k - 1:KT * grp + k], a_hi[:, k - 1, :].bitcast(F32),
                                                 ALU.add, ALU.subtract).then_inc(ready, 1)

            modulated(r, 0, 0, R["h1"])
            dve.wait_ge(consts_in, 32)
            dve.wait_ge(margins, 1)
            for f in range(CT):
                for j in range(2):
                    split(CH["glu"] + 2 * f + j + WEIGHT_LEAD)
                src = bank(LT["glu"] + 2 * f)
                dve.wait_ge(R["glu_sig"], f + 1)
                dve.scalar_tensor_tensor(u_pad[:, f, PAD:PAD + TOK], src, v("b_in", BI_GA + f), sig[:, :], ALU.add,
                                         ALU.mult).then_inc(R["glu"], 1)
            dve.wait_ge(R["glu"], CT)
            for f in range(8):
                split(CH["qk"] + f + WEIGHT_LEAD)
                src = bank(LT["qk"] + f)
                slot = tmp_slot()
                scale = HD ** -0.5 if f < 4 else 1.0
                dve.tensor_scalar(slot, src, v("b_in", f), scale, ALU.add, ALU.mult).then_inc(tmp_w, 1)
                conv_taps(3 if f < 6 else 1)
                lo_of_tmp(qk_lo[:, f, :], qk_hi[:, f, :], R["qk"])
            for j in range(4):
                split(CH["v"] + j + WEIGHT_LEAD)
                conv_taps(5)
            for t in range(NT):
                lo(v_lo[:, t, :], bank(LT["v"] + t), v_hi[:, t, :], R["v"])

            def out1(h, rows, dst, src):
                return dve.tensor_scalar(dst, src, vecs[rows, VO["b_in"] + BI_V + h // 2:VO["b_in"] + BI_V + h // 2 + 1], None, ALU.add)

            for j in range(2 * KT):
                split(CH["gates"] + j + WEIGHT_LEAD)
                if j < 10:
                    conv_taps(6 if j < 5 else 5)
                if j == 10:
                    dve.wait_ge(R["ln_sum"], 1)
                    for k in range(CT):
                        dve.scalar_tensor_tensor(c_acc[:, k, :], ps[:, STAT_BANK, :], -1.0 / D_CONV, c_acc[:, k, :], ALU.mult,
                                                 ALU.add).then_inc(R["ln_mean"], 1)
                if j == 13:
                    r = wait_rs()
                    for k in range(CT):
                        dve.tensor_tensor(c_acc[:, k, :], c_acc[:, k, :], r, ALU.mult).then_inc(R["cn"], 1)
                    for k in range(CT):
                        dve.wait_ge(R["cn_sig"], k + 1)
                        dve.tensor_scalar(c_acc[:, k, :], c_acc[:, k, :], v("g_ln", k), v("b_ln", k), ALU.mult, ALU.add).then_inc(R["cn"], 1)
                        dve.wait_ge(R["cn"], CT + k + 1)
                        dve.tensor_tensor(c_acc[:, k, :], c_acc[:, k, :], sq[:, k % 2, :], ALU.mult).then_inc(R["cs"], 1)
            mod_group(2)
            attention(attn1, outs_of(attn1, out1, qk_hi, qk_lo, R["o1_half"], R["o1"]))
            for k in range(CT):
                lo(cv_lo[:, k, :], c_acc[:, k, :], cv_hi[:, k, :], R["cv"])
            mod_group(3)
            for f in range(KT):
                split(CH["ac"] + f + WEIGHT_LEAD)
                t0 = LT["ac"] + 2 * f
                dve.tensor_tensor(gprod[:, 0, :], bank(t0), x[:, f, :], ALU.mult).then_inc(R["gate_a"], 1)
                dve.scalar_tensor_tensor(gprod[:, 1, :], bank(t0 + 1), v("b_conv_o", f), gate_b[:, f, :], ALU.add,
                                         ALU.mult).then_inc(R["gate_a"], 1)
                for _ in range((2, *[1] * (KT - 2), 0)[f]):
                    mod_unit()
                slot = tmp_slot()
                dve.wait_ge(R["gate_a"], 2 * f + 2)
                dve.tensor_tensor(slot, gprod[:, 0, :], gprod[:, 1, :], ALU.add).then_inc(tmp_w, 1)
                lo_of_tmp(y_lo[:, f, :], y_hi[:, f, :], R["y"])
            mod_group(4)
            for k in range(KT):
                split(CH["mix"] + k + WEIGHT_LEAD)
                for _ in range((2, *[1] * (KT - 2), 0)[k]):
                    mod_unit()
                dve.tensor_copy(y_f[:, k, :], bank(LT["mix"] + k)).then_inc(R["y_f"], 1)
            mod_group(5)
            dve.wait_ge(mod_ready, 6)
            gain(1, "g_post_mix", 2, 0.0)
            gain(2, "g_pre_ffn", 4, 1.0)
            gain(3, "g_post_ffn", 5, 0.0)

            def residual(y, order, i, ready):
                r = wait_rs()
                dve.wait_ge(gains, 4)
                before = steps[0]
                for k in range(KT + 1):
                    if k < KT:
                        dve.scalar_tensor_tensor(y[:, k, :], y[:, k, :], gvec[:, KT * i + k:KT * i + k + 1], r, ALU.mult,
                                                 ALU.mult).then_inc(dve_step, 1)
                    if k:
                        dve.wait_ge(dve_step, before + k)
                        dve.tensor_tensor(x[:, k - 1, :], x[:, k - 1, :], y[:, k - 1, :], ALU.add).then_inc(ready, 1)
                steps[0] += KT

            dve.wait_ge(R["y_f"], KT)
            dve.wait_ge(x_in, 32)
            residual(y_f, range(KT), 1, R["x_mix"])
            r = wait_rs()
            modulated(r, 2, 3, R["h2"])
            t0, h0 = tmps[0], his[0]
            with dve.Fori(0, FT // 2) as i:
                for pair in range(2):
                    for j in range(2):
                        n = CH["up"] + 2 * pair + j + WEIGHT_LEAD
                        dve.wait_ge(w_hi_done, i * 4 + (n + 1))
                        dve.tensor_tensor(w_lo[:, n % SLOTS, :], w_raw[:, n % RAW, :], w_hi[:, n % SLOTS, :].bitcast(F32),
                                          ALU.subtract).then_inc(w_lo_done, 1)
                    for tap in (1, 0):
                        for j, (c, s, u_s, w_at) in enumerate(((c_val, R["cf_val"], R["u_val"], 0), (c_gate[:, :], R["cf_gate"], R["u_gate"], FT))):
                            if tap == 1:
                                dve.wait_ge(u_s, i * 2 + (up_free + pair + 1))
                            else:
                                dve.wait_ge(s, i * 4 + (2 * pair + 1))
                            dve.scalar_tensor_tensor(c, u_ff[:, 2 * pair + j, tap:tap + TOK],
                                                     vecs[:, bass.ds(i * 2 + (VO["w_dwf"] + tap * 2 * FT + w_at + pair), 1)],
                                                     c, ALU.mult, ALU.add).then_inc(s, 1)
                    dve.wait_ge(R["gel"], i * 2 + (pair + 1))
                    dve.wait_ge(R["cf_val"], i * 4 + (2 * pair + 2))
                    slot = (t0 + pair) % 2
                    dve.tensor_tensor(tmp[:, slot, :], gel, c_val, ALU.mult).then_inc(tmp_w, 1)
                    dve.wait_ge(hi_done, i * 2 + (h0 + pair + 1))
                    at_k = bass.ds(i * (2 * TOK) + pair * TOK, TOK)
                    dve.tensor_tensor(g_lo.rearrange("p k n -> p (k n)")[:, at_k], tmp[:, slot, :],
                                      g_hi.rearrange("p k n -> p (k n)")[:, at_k].bitcast(F32), ALU.subtract).then_inc(R["g"], 1)
            tmps[0] += FT
            his[0] += FT
            for k in range(3):
                split(CH["down"] + k + WEIGHT_LEAD)
            with dve.Fori(0, (FT - 6) // 4) as i:
                for j in range(4):
                    n = CH["down"] + 3 + j + WEIGHT_LEAD
                    dve.wait_ge(w_hi_done, i * 4 + (n + 1))
                    dve.tensor_tensor(w_lo[:, n % SLOTS, :], w_raw[:, n % RAW, :], w_hi[:, n % SLOTS, :].bitcast(F32),
                                      ALU.subtract).then_inc(w_lo_done, 1)
            for k in range(3 + (FT - 6) // 4 * 4, FT):
                split(CH["down"] + k + WEIGHT_LEAD)
            dve.wait_ge(down_step, FT)
            for k in range(KT):
                dve.tensor_copy(y_d[:, KT - 1 - k, :], ps[:, KT - 1 - k, :]).then_inc(R["y_d"], 1)
            dve.wait_ge(R["y_d"], KT)

            def scaled_lo(lo_, hi, gain_, k, s, val, ready):
                his[0] += 1
                dve.wait_ge(s, val)
                dve.wait_ge(hi_done, his[0])
                dve.scalar_tensor_tensor(lo_[:, k, :], x[:, k, :], v(gain_, k), hi[:, k, :].bitcast(F32), ALU.mult,
                                         ALU.subtract).then_inc(ready, 1)

            residual(y_d, range(KT), 3, R["x_ffn"])
            for k in range(KT):
                scaled_lo(a_lo, a_hi, "norm_a", k, R["x_ffn"], k + 1, R["in_a"])
            r = wait_rs()
            for f in range(KT):
                split(CH["a_q"] + f + WEIGHT_LEAD)
                src = bank(LT["a_q"] + f)
                slot = tmp_slot()
                dve.scalar_tensor_tensor(slot, src, HD ** -0.5, r, ALU.mult, ALU.mult).then_inc(tmp_w, 1)
                lo_of_tmp(b_lo[:, f, :], b_hi[:, f, :], R["q_a"])
            for f in range(2):
                split(CH["a_k"] + f + WEIGHT_LEAD)
                src = bank(LT["a_k"] + f)
                slot = tmp_slot()
                dve.tensor_tensor(slot, src, r, ALU.mult).then_inc(tmp_w, 1)
                lo_of_tmp(ka_lo[:, f, :], ka_hi[:, f, :], R["k_a"])

            def gate_out(name, z, f, t_sem):
                dve.tensor_tensor(z[:, f, :], bank(LT[name] + f), r, ALU.mult).then_inc(t_sem, 1)

            def silu_tiles(name, z, sg, t_sem, sig_sem, ready, split_from=0, out_from=0):
                for f in range(KT):
                    if f >= split_from:
                        split(CH[name] + f + WEIGHT_LEAD)
                    if f >= out_from:
                        gate_out(name, z, f, t_sem)
                    dve.wait_ge(t_sem, f + 1)
                    dve.wait_ge(sig_sem, f + 1)
                    dve.tensor_tensor(z[:, f, :], z[:, f, :], sg[:, :], ALU.mult).then_inc(ready, 1)

            silu_tiles("a_z", z2, zs, R["z_t"], R["z_sig"], R["z_a"])
            for f in range(2):
                split(CH["a_v"] + f + WEIGHT_LEAD)
            dve.wait_ge(R["rcol_t"], 1)
            dve.tensor_copy(rcol[:, :], ps[:, STAT_BANK, :].rearrange("p (t q) -> p t q", q=P)[:, :, 0]).then_inc(stat_free, 1)
            dve.wait_ge(stat_free, 7)
            for t in range(NT + 1):
                if t >= 2 and t < NT:
                    dve.wait_ge(R["v_a"], t - 1)
                if t < NT:
                    src = bank(LT["a_v"] + t)
                    dve.tensor_scalar(tmp_slot()[:, 0:256], src[:, 0:256], rcol[:, t:t + 1], None, ALU.mult).then_inc(tmp_w, 1)
                if t:
                    slot = (tmps[0] - (2 if t < NT else 1)) % 2
                    lo(va_lo[:, t - 1, :], tmp[:, slot, 0:256], va_hi[:, t - 1, :], R["v_a"])
            dve.wait_ge(sink_in, 16)
            dve.tensor_scalar(sink[:, 1, :], sink[:, 0, :], -1.0, None, ALU.mult).then_inc(R["z_a"], 1)
            dve.wait_ge(R["z_a"], KT + 1)

            def gated(a, z, pair, half_sem, ready, base=0):
                def half_out(h):
                    rows, i = half(h), base + h // 2
                    if i >= 2 and h % 2 == 0:
                        dve.wait_ge(ready, i - 1)
                    dve.tensor_tensor(pair[rows, i % 2, :], bank(a.lin(h))[rows, :], z[rows, i, :], ALU.mult
                                      ).then_inc(half_sem if h % 2 == 0 else o_full, 1)
                return half_out, None

            attention(attn2, gated(attn2, z2, o_pair2, R["o2_half"], R["o2"]))

            def rest(l, after, nxt):
                i = 0 if l == "a" else 1
                if l == "b":
                    dve.wait_ge(w_lo_done, CH["b_out"] + WEIGHT_LEAD)
                for k in range(KT):
                    split(CH[l + "_out"] + k + WEIGHT_LEAD)
                    dve.tensor_tensor(x[:, k, :], bank(LT[l + "_out"] + k), x[:, k, :], ALU.add).then_inc(R["x_attn"], 1)
                    scaled_lo(after[1], after[0], f"ple_g{i}", k, R["x_attn"], KT * i + k + 1, R["in_g"])
                    if k == KT // 2:
                        for kk in range(PT_K):
                            lo(p_lo[:, kk, :], p_raw[:, kk, :], p_hi[:, kk, :], R["p"])
                for k in range(KT):
                    if k % 4 == 0:
                        split(CH[l + "_ple"] + k // 4 + WEIGHT_LEAD)
                    dve.tensor_copy(pl[:, k, :], bank(LT[l + "_ple"] + k)).then_inc(R["pl"], 1)
                r = wait_rs()
                for k in range(KT):
                    split(CH[l + "_gate"] + k + WEIGHT_LEAD)
                    g = gs2[:, k % 2, :]
                    dve.tensor_tensor(g, bank(LT[l + "_gate"] + k), r, ALU.mult).then_inc(R["gt"], 1)
                    dve.wait_ge(R["gsig"], KT * i + k + 1)
                    dve.wait_ge(R["pl"], KT * i + k + 1)
                    step(dve.tensor_tensor(pl[:, k, :], pl[:, k, :], g, ALU.mult))
                    dve.tensor_tensor(x[:, k, :], x[:, k, :], pl[:, k, :], ALU.add).then_inc(R["x_ple"], 1)
                    if nxt is not None:
                        scaled_lo(nxt[1], nxt[0], "norm_b", k, R["x_ple"], KT * i + k + 1, R["in_b"])

            rest("a", (a_hi, a_lo), (b_hi, b_lo))
            r = wait_rs()
            for f in range(QT + KVT):
                split(CH["b_c"] + f + WEIGHT_LEAD)
                dve.tensor_tensor(cq_f[:, f, :], bank(LT["b_c"] + f), r, ALU.mult).then_inc(R["cq"], 1)
            split(CH["b_c"] + 5 + WEIGHT_LEAD)
            src = bank(LT["b_c"] + 5)
            dve.tensor_tensor(kr_f[64:128, :], src[64:128, :], r[64:128, :], ALU.mult).then_inc(R["kr"], 1)
            dve.wait_ge(R["kr"], 1)
            dve.wait_ge(R["rope_k"], 16)
            for f in range(2):
                split(CH["b_z"] + f + WEIGHT_LEAD)
            dve.tensor_tensor(kr_r[64:96, :], kr_f[96:128, :], rope_k[96:128, :], ALU.mult)
            step(dve.tensor_tensor(kr_f[64:96, :], kr_f[64:96, :], rope_k[64:96, :], ALU.mult))
            dve.tensor_tensor(kr_f[64:96, :], kr_f[64:96, :], kr_r[64:96, :], ALU.add).then_inc(R["kr_sum"], 1)
            dve.wait_ge(R["kr_sum"], 1)
            for b in range(2):
                lo(k3_lo[64:96, b, :], kr_f[64:96, :], k3_hi[64:96, b, :], R["kr"])
            dve.wait_ge(R["cq"], QT + KVT)
            gate_out("b_z", z3, 0, R["z_tb"])
            for part, (n0_, n_, name, hi, lo_) in enumerate(((0, QT, "q_norm", cq_hi, cq_lo), (QT, KVT, "kv_norm", ck_hi, ck_lo))):
                r2 = wait_rs()
                for k in range(n_ + 1):
                    if part and k == 0:
                        dve.wait_ge(R["cqn"], QT)
                    if 2 <= k < n_:
                        dve.wait_ge(R["cqn"], n0_ + k - 1)
                    if k < n_:
                        dve.scalar_tensor_tensor(tmp_slot(), cq_f[:, n0_ + k, :], v(name, k), r2, ALU.mult, ALU.mult
                                                 ).then_inc(tmp_w, 1)
                    if k:
                        slot = (tmps[0] - (2 if k < n_ else 1)) % 2
                        lo(lo_[:, k - 1, :], tmp[:, slot, :], hi[:, k - 1, :], R["cqn"])
                if part == 0:
                    split(CH["b_z"] + 2 + WEIGHT_LEAD)
                    for f in range(1, 3):
                        gate_out("b_z", z3, f, R["z_tb"])
            silu_tiles("b_z", z3, zs3, R["z_tb"], R["z_sigb"], R["z_b"], 3, 3)
            for hf in range(2):
                a = attn3[hf]
                dve.wait_ge(w_lo_done, CH[f"b_v{hf}"] + WEIGHT_LEAD)
                split(CH[f"b_v{hf}"] + WEIGHT_LEAD)

                def key_lo(h):
                    src = bank(a.k_lin(h - h % 2))[64 * (h % 2):64 * (h % 2) + 64, :]
                    lo(k3_lo[0:64, h % 2, :], src, k3_hi[0:64, h % 2, :], R["k_b"])

                def query(h):
                    src = bank(a.q_lin(h))
                    if hf or h:
                        dve.wait_ge(R["q_b"], 8 * hf + h)
                    dve.tensor_tensor(q3_f[0:96, :], src[0:96, :], rope[0:96, :], ALU.mult)
                    dve.tensor_tensor(q3_r[64:96, :], src[96:128, :], rope[96:128, :], ALU.mult).then_inc(R["q_t"], 1)

                def query_lo(h):
                    lo(q3_lo[0:96, h % 2, :], q3_f[0:96, :], q3_hi[0:96, h % 2, :], R["q_b"])

                def first(h, t):
                    if t == 0 and h % 2 == 0 and 2 <= h <= 6:
                        key_lo(h + 1)
                    if t == 3 - h % 2 and 1 <= h <= 6:
                        query_lo(h + 1)
                    if t == 3 and h % 2 == 1 and h + 1 < 8:
                        key_lo(h + 1)

                def after(h, t):
                    if t == 1 - h % 2 and 1 <= h <= 6:
                        query(h + 1)

                key_lo(0)
                key_lo(1)
                query(0)
                query_lo(0)
                for t in range(NT):
                    lo(vb_lo[:, t, :], bank(LT[f"b_v{hf}"] + t), vb_hi[:, t, :], R["v_b"])
                query(1)
                query_lo(1)
                attention(a, gated(a, z3, o_pair3, R["o3_half"], R["o3"], 4 * hf), after, first)
            rest("b", (b_hi, b_lo), None)
            r = wait_rs()
            for k in range(KT):
                dve.scalar_tensor_tensor(x[:, k, :], x[:, k, :], v("final_g", k), r, ALU.mult, ALU.mult).then_inc(R["fin"], 1)


def _feature_tiles(a):
    t = np.ascontiguousarray(a.T)
    return np.ascontiguousarray(t.reshape(-1, P, t.shape[1]).transpose(1, 0, 2))


def _columns(vec):
    return vec.reshape(-1, P).T


def _weight_stream(i):
    chunks = []

    def rows(w):
        return np.asarray(w).reshape(-1, P, w.shape[1])

    def out_tiles(w, group=1):
        r = rows(w)
        kt, n = r.shape[0], r.shape[2] // P
        t = r.reshape(kt, P, n // group, group, P).transpose(2, 1, 3, 0, 4)
        chunks.extend(t.reshape(n // group, P, group * kt * P))

    def row_chunks(w, per):
        r = rows(w)
        chunks.extend(r.reshape(-1, per, P, r.shape[2]).transpose(0, 2, 1, 3).reshape(r.shape[0] // per, P, -1))

    w_in = np.asarray(i["w_in"][0])
    q, k, v, ga, gb, gate_a, gate_b = np.split(w_in, np.cumsum([D_ATTN] * 3 + [D_CONV] * 2 + [D]), axis=1)
    for f in range(CT):
        out_tiles(ga[:, P * f:P * f + P])
        out_tiles(gb[:, P * f:P * f + P])
    out_tiles(q)
    out_tiles(k)
    row_chunks(v, 2)
    out_tiles(gate_a)
    out_tiles(gate_b)
    for f in range(KT):
        s = slice(P * f, P * f + P)
        out_tiles(np.concatenate([i["w_attn_o"][0][:, s], i["w_conv_o"][0][:, s]], axis=0))
    out_tiles(i["w_mix_o"][0])
    for f in range(FT):
        out_tiles(i["w_up"][0][:, P * f:P * f + P])
        out_tiles(i["w_up"][0][:, D_FF + P * f:D_FF + P * f + P])
    row_chunks(i["w_down"][0], 1)
    a = np.asarray(i["a_w_in_2"][0])
    q, k, v, z = np.split(a, np.cumsum([D, 256, 256]), axis=1)
    order = head_order()
    out_tiles(q.reshape(D, A_HEADS, HD)[:, order].reshape(D, D))
    out_tiles(k)
    out_tiles(z.reshape(D, A_HEADS, HD)[:, order].reshape(D, D))
    row_chunks(v, 4)
    out_tiles(np.asarray(i["a_w_out_2"][0]).reshape(A_HEADS, HD, D)[order].reshape(D, D))
    out_tiles(i["ple_w_2"][0], 4)
    out_tiles(i["ple_w_gate_2"][0])
    b = np.asarray(i["b_w_in_2"][0])
    cq, ckv, kr, z = np.split(b, np.cumsum([Q_LORA, KV_LORA, B_ROPE]), axis=1)
    swap = np.r_[B_ROPE // 2:B_ROPE, 0:B_ROPE // 2]
    out_tiles(cq)
    out_tiles(ckv)
    out_tiles(np.concatenate([kr, kr[:, swap], kr, kr[:, swap]], axis=1))
    out_tiles(z)
    qb = np.asarray(i["b_w_qb_2"][0]).reshape(Q_LORA, B_HEADS, B_NOPE + B_ROPE)
    qb = np.concatenate([qb, qb[:, :, B_NOPE:][:, :, swap]], axis=2)
    kvb = np.asarray(i["b_w_kvb_2"][0]).reshape(KV_LORA, B_HEADS, B_NOPE + B_V)
    for half in range(2):
        row_chunks(kvb[:, 8 * half:8 * half + 8, B_NOPE:].reshape(KV_LORA, 8 * B_V), 2)
        for h in range(8 * half, 8 * half + 8, 2):
            parts = [rows(qb[:, h]), rows(qb[:, h + 1]), rows(kvb[:, h:h + 2, :B_NOPE].reshape(KV_LORA, P))]
            chunks.append(np.concatenate([p.transpose(1, 0, 2).reshape(P, -1) for p in parts], axis=1))
    out_tiles(i["b_w_out_2"][0])
    out_tiles(i["ple_w_2"][1], 4)
    out_tiles(i["ple_w_gate_2"][1])
    return np.stack(chunks)


def _constants():
    half = B_ROPE // 2
    inv = (np.float32(10000.0) ** (-np.arange(half, dtype=np.float32) / np.float32(half))).astype(np.float32)
    ang = (np.arange(TOK, dtype=np.float32)[:, None] * inv[None, :]).astype(np.float32).T
    rope = np.ones((P, TOK), np.float32)
    rope[64:96] = np.concatenate([np.cos(ang), np.cos(ang)])
    rope[96:128] = np.concatenate([-np.sin(ang), np.sin(ang)])
    slopes = (2.0 ** (-8.0 * np.arange(1, A_HEADS + 1) / A_HEADS)).astype(np.float32)[head_order()]
    dist = np.abs(np.arange(3 * P)[None, :] - P - np.arange(P)[:, None])
    alibi = np.where(dist <= WINDOW, -slopes[:, None, None] * dist.astype(np.float32), np.float32(MASKED)).astype(np.float32)
    return np.eye(P, dtype=np.float32), rope * np.float32((B_NOPE + B_ROPE) ** -0.5), rope, alibi


def kernel(**inputs):
    import concourse.bacc as _bacc
    from concourse.bass_utils import run_bass_kernel_spmd as _run

    i = {k: np.asarray(a) for k, a in inputs.items()}
    ident, rope, rope_k, alibi = _constants()
    vec = {
        "c": i["c"][0], "b_ada": i["b_ada"][0], "g_pre_mix": i["g_pre_mix"][0], "g_post_mix": i["g_post_mix"][0],
        "b_in": i["b_in"][0], "w_dw": i["w_dw_conv"][0].reshape(-1), "b_dw": i["b_dw_conv"][0], "g_ln": i["g_conv_ln"][0],
        "b_ln": i["b_conv_ln"][0], "b_conv_o": i["b_conv_o"][0], "g_pre_ffn": i["g_pre_ffn"][0],
        "g_post_ffn": i["g_post_ffn"][0], "w_dwf": i["w_dw_ffn"][0].reshape(-1), "b_dwf": i["b_dw_ffn"][0],
        "norm_a": i["norm_g_2"][0], "norm_b": i["norm_g_2"][1], "q_norm": i["b_q_norm_2"][0], "kv_norm": i["b_kv_norm_2"][0],
        "ple_g0": i["ple_norm_g_2"][0], "ple_g1": i["ple_norm_g_2"][1], "final_g": i["final_norm_g_2"],
    }
    where = np.minimum(TOK - P + np.arange(P)[:, None] - np.arange(TOK)[None, :], MAX_REL) + MAX_REL
    arrays = {
        "in_x": _feature_tiles(i["x"][0]),
        "in_w": _weight_stream(i),
        "in_ada": np.ascontiguousarray(i["w_ada"][0].reshape(KT, P, 6, D).transpose(2, 0, 1, 3)),
        "in_vecs": np.ascontiguousarray(np.concatenate([_columns(vec[n]) for n, _ in VECS], axis=1)),
        "in_ident": ident, "in_rope": rope, "in_rope_k": rope_k,
        "in_rel": np.ascontiguousarray(i["rel_bias"][0][:, where]),
        "in_alibi": alibi,
        "in_sink": np.ascontiguousarray(i["a_sink_2"]),
        "in_p": np.stack([_feature_tiles(i["p_2"][l, 0]) for l in range(2)]),
    }
    nc = _bacc.Bacc("TRN2", target_bir_lowering=False, num_devices=1)
    args = [nc.dram_tensor(n, a.shape, mybir.dt.from_np(a.dtype), kind="ExternalInput").ap() for n, a in arrays.items()]
    args.append(nc.dram_tensor("out_0", (P, KT, TOK), F32, kind="ExternalOutput").ap())
    build(nc, *args)
    r = _run(nc, [arrays], core_ids=[0])
    got = np.asarray(r.results[0]["out_0"])
    return np.ascontiguousarray(got.transpose(1, 0, 2).reshape(D, TOK).T).reshape(1, TOK, D)
```
